# Optimizing a Trainium2 kernel written in Bass

```python
import math
import jax, jax.numpy as jnp
from jax import lax
import numpy as np

D_MODEL = 1024
BATCH = 1
SEQ = 2048
DEPTH = 1

CHUNK = 64
D_MIX = D_MODEL
DN_HEADS = 4
DN_HEAD_DIM = 128
DN_WIDTH = DN_HEADS * DN_HEAD_DIM
SHORT_CONV = 4
CONF_WIDTH = D_MIX - DN_WIDTH
CONF_KERNEL = 31
C_IN = 4 * DN_WIDTH + 2 * DN_HEADS + 2 * CONF_WIDTH
N_GROUPS = 4
EXPERTS_PER_GROUP = 8
N_EXPERTS = N_GROUPS * EXPERTS_PER_GROUP
TOP_K = 2
D_EXPERT = 512
MOE_BLOCK = 128
EPS = 1e-6

kernel_name = 'hybrid_deltanet_conformer_hiermoe'

def rmsnorm(x, w):
    xf = x.astype(jnp.float32)
    y = xf * lax.rsqrt(jnp.mean(xf * xf, axis=-1, keepdims=True) + EPS)
    return (y * w.astype(jnp.float32)).astype(x.dtype)

def layernorm(x, g, b):
    xf = x.astype(jnp.float32)
    mu = jnp.mean(xf, axis=-1, keepdims=True)
    var = jnp.mean(jnp.square(xf - mu), axis=-1, keepdims=True)
    y = (xf - mu) * lax.rsqrt(var + EPS) * g.astype(jnp.float32) + b.astype(jnp.float32)
    return y.astype(x.dtype)

def l2norm(x):
    return x * lax.rsqrt(jnp.sum(x * x, axis=-1, keepdims=True) + EPS)

def causal_dwconv(x, w):
    K, C = w.shape
    return lax.conv_general_dilated(
        x, w[:, None, :].astype(x.dtype), window_strides=(1,), padding=[(K - 1, 0)],
        dimension_numbers=('NWC', 'WIO', 'NWC'), feature_group_count=C)

def chunked_gated_delta_rule(q, k, v, g, beta):
    Bn, L, H, dk = q.shape
    dv = v.shape[-1]
    N = L // CHUNK
    q = l2norm(q) * (dk ** -0.5)
    k = l2norm(k)

    def to_chunks(t):
        t = t.reshape((Bn, N, CHUNK, H) + t.shape[3:])
        return jnp.moveaxis(t, 3, 1)

    qc, kc, vc, gc, bc = (to_chunks(t) for t in (q, k, v, g, beta))
    gc = jnp.cumsum(gc, axis=-1)
    incl = jnp.tril(jnp.ones((CHUNK, CHUNK), bool))
    strict = jnp.tril(jnp.ones((CHUNK, CHUNK), bool), -1)
    decay = jnp.exp(jnp.where(incl, gc[..., :, None] - gc[..., None, :], -jnp.inf))
    a_mat = jnp.where(strict, bc[..., :, None] * jnp.einsum('bhncd,bhnsd->bhncs', kc, kc) * decay, 0.0)
    rhs = jnp.concatenate([bc[..., None] * vc, (bc * jnp.exp(gc))[..., None] * kc], axis=-1)
    sol = lax.linalg.triangular_solve(a_mat + jnp.eye(CHUNK, dtype=a_mat.dtype), rhs,
                                      left_side=True, lower=True, unit_diagonal=True)
    u_c, w_c = sol[..., :dv], sol[..., dv:]
    qk = jnp.einsum('bhncd,bhnsd->bhncs', qc, kc) * decay
    q_dec = qc * jnp.exp(gc)[..., None]
    k_dec = kc * jnp.exp(gc[..., -1:] - gc)[..., None]
    g_last = jnp.exp(gc[..., -1])
    xs = tuple(jnp.moveaxis(t, 2, 0) for t in (q_dec, k_dec, u_c, w_c, qk, g_last))

    def step(S, inp):
        q_i, k_i, u_i, w_i, qk_i, gl_i = inp
        v_new = u_i - jnp.einsum('bhcd,bhde->bhce', w_i, S)
        o_i = jnp.einsum('bhcd,bhde->bhce', q_i, S) + jnp.einsum('bhcs,bhse->bhce', qk_i, v_new)
        S = S * gl_i[..., None, None] + jnp.einsum('bhcd,bhce->bhde', k_i, v_new)
        return S, o_i

    S0 = jnp.zeros((Bn, H, dk, dv), jnp.float32)
    _, o = lax.scan(step, S0, xs)
    o = jnp.moveaxis(o, 0, 2)
    return jnp.moveaxis(o, 1, 3).reshape(Bn, L, H, dv)

def gated_deltanet(qkv, z, b_logit, a_logit, conv_w, a_log, dt_bias, o_norm):
    Bn, L, _ = qkv.shape
    out_dtype = qkv.dtype
    qkv = jax.nn.silu(causal_dwconv(qkv, conv_w)).astype(jnp.float32)
    q, k, v = jnp.split(qkv, 3, axis=-1)
    hs = (Bn, L, DN_HEADS, DN_HEAD_DIM)
    q, k, v = q.reshape(hs), k.reshape(hs), v.reshape(hs)
    beta = jax.nn.sigmoid(b_logit.astype(jnp.float32))
    g = -jnp.exp(a_log.astype(jnp.float32)) * jax.nn.softplus(
        a_logit.astype(jnp.float32) + dt_bias.astype(jnp.float32))
    o = chunked_gated_delta_rule(q, k, v, g, beta)
    o = o * lax.rsqrt(jnp.mean(o * o, axis=-1, keepdims=True) + EPS) * o_norm.astype(jnp.float32)
    o = o * jax.nn.silu(z.astype(jnp.float32).reshape(hs))
    return o.reshape(Bn, L, DN_WIDTH).astype(out_dtype)

def conformer_conv(u, w_dw, b_dw, ln_g, ln_b):
    glu = u[..., :CONF_WIDTH] * jax.nn.sigmoid(u[..., CONF_WIDTH:])
    c = causal_dwconv(glu, w_dw) + b_dw.astype(glu.dtype)
    c = layernorm(c, ln_g, ln_b)
    return jax.nn.silu(c)

def hier_moe(h, w_rg, b_rg, w_re, b_re, w_gate, w_up, w_down):
    T, D = h.shape
    hf = h.astype(jnp.float32)
    p_grp = jax.nn.softmax(hf @ w_rg.astype(jnp.float32) + b_rg.astype(jnp.float32), axis=-1)
    p_g, g_sel = lax.top_k(p_grp, 1)
    e_logits = (hf @ w_re.astype(jnp.float32) + b_re.astype(jnp.float32)).reshape(
        T, N_GROUPS, EXPERTS_PER_GROUP)
    e_logits = jnp.take_along_axis(e_logits, g_sel[:, :, None], axis=1)[:, 0]
    p_e = jax.nn.softmax(e_logits, axis=-1)
    top_p, top_i = lax.top_k(p_e, TOP_K)
    gates = p_g * top_p / jnp.sum(top_p, axis=-1, keepdims=True)
    expert_id = g_sel * EXPERTS_PER_GROUP + top_i

    A = T * TOP_K
    flat_e = expert_id.reshape(A)
    flat_tok = jnp.repeat(jnp.arange(T, dtype=jnp.int32), TOP_K)
    flat_w = gates.reshape(A)
    order = jnp.argsort(flat_e)
    e_s, tok_s, w_s = flat_e[order], flat_tok[order], flat_w[order]
    counts = jnp.bincount(flat_e, length=N_EXPERTS)
    padded = (counts + MOE_BLOCK - 1) // MOE_BLOCK * MOE_BLOCK
    starts = jnp.cumsum(counts) - counts
    pad_ends = jnp.cumsum(padded)
    pad_starts = pad_ends - padded
    dest = pad_starts[e_s] + jnp.arange(A, dtype=jnp.int32) - starts[e_s]
    n_blocks = -(-(A + N_EXPERTS * MOE_BLOCK) // MOE_BLOCK)
    P = n_blocks * MOE_BLOCK
    slot_tok = jnp.full((P,), T, jnp.int32).at[dest].set(tok_s)
    block_expert = jnp.minimum(
        jnp.searchsorted(pad_ends, jnp.arange(n_blocks, dtype=jnp.int32) * MOE_BLOCK, side='right'),
        N_EXPERTS - 1)
    h_pad = jnp.concatenate([h, jnp.zeros((1, D), h.dtype)], axis=0)

    def run_block(args):
        toks, e = args
        xb = h_pad[toks]
        return (jax.nn.silu(xb @ w_gate[e]) * (xb @ w_up[e])) @ w_down[e]

    y = lax.map(run_block, (slot_tok.reshape(n_blocks, MOE_BLOCK), block_expert)).reshape(P, D)
    return jnp.zeros_like(h).at[tok_s].add(y[dest] * w_s[:, None].astype(h.dtype))

def setup_inputs(seed: int = 0) -> dict:
    key = jax.random.key(seed)
    ks = jax.random.split(key, 21)
    f32 = jnp.float32

    def nrm(k, shape, scale):
        return jax.random.normal(k, shape, f32) * scale

    def gain(k, shape):
        return 1.0 + 0.01 * jax.random.normal(k, shape, f32)

    x = nrm(ks[0], (BATCH, SEQ, D_MODEL), 1.0)
    norm_mix = gain(ks[1], (DEPTH, D_MODEL))
    w_in = nrm(ks[2], (DEPTH, D_MODEL, C_IN), D_MODEL ** -0.5)
    conv_qkv = nrm(ks[3], (DEPTH, SHORT_CONV, 3 * DN_WIDTH), SHORT_CONV ** -0.5)
    a_log = jnp.log(jax.random.uniform(ks[4], (DEPTH, DN_HEADS), f32, 1.0, 16.0))
    dt = jnp.exp(jax.random.uniform(ks[5], (DEPTH, DN_HEADS), f32, math.log(1e-3), math.log(1e-1)))
    dt_bias = dt + jnp.log(-jnp.expm1(-dt))
    o_norm = gain(ks[6], (DEPTH, DN_HEAD_DIM))
    w_dw = nrm(ks[7], (DEPTH, CONF_KERNEL, CONF_WIDTH), CONF_KERNEL ** -0.5)
    b_dw = nrm(ks[8], (DEPTH, CONF_WIDTH), 0.01)
    ln_g = gain(ks[9], (DEPTH, CONF_WIDTH))
    ln_b = nrm(ks[10], (DEPTH, CONF_WIDTH), 0.01)
    w_out = nrm(ks[11], (DEPTH, D_MIX, D_MODEL), D_MIX ** -0.5)
    norm_ffn = gain(ks[12], (DEPTH, D_MODEL))
    w_rg = nrm(ks[13], (DEPTH, D_MODEL, N_GROUPS), D_MODEL ** -0.5)
    b_rg = nrm(ks[14], (DEPTH, N_GROUPS), 0.01)
    w_re = nrm(ks[15], (DEPTH, D_MODEL, N_EXPERTS), D_MODEL ** -0.5)
    b_re = nrm(ks[16], (DEPTH, N_EXPERTS), 0.01)
    w_gate = nrm(ks[17], (DEPTH, N_EXPERTS, D_MODEL, D_EXPERT), D_MODEL ** -0.5)
    w_up = nrm(ks[18], (DEPTH, N_EXPERTS, D_MODEL, D_EXPERT), D_MODEL ** -0.5)
    w_down = nrm(ks[19], (DEPTH, N_EXPERTS, D_EXPERT, D_MODEL), D_EXPERT ** -0.5)
    norm_final = gain(ks[20], (D_MODEL,))
    return {'x': x, 'norm_mix': norm_mix, 'w_in': w_in, 'conv_qkv': conv_qkv, 'a_log': a_log,
            'dt_bias': dt_bias, 'o_norm': o_norm, 'w_dw': w_dw, 'b_dw': b_dw, 'ln_g': ln_g,
            'ln_b': ln_b, 'w_out': w_out, 'norm_ffn': norm_ffn, 'w_rg': w_rg, 'b_rg': b_rg,
            'w_re': w_re, 'b_re': b_re, 'w_gate': w_gate, 'w_up': w_up, 'w_down': w_down,
            'norm_final': norm_final}

def reference(x, norm_mix, w_in, conv_qkv, a_log, dt_bias, o_norm, w_dw, b_dw, ln_g, ln_b,
              w_out, norm_ffn, w_rg, b_rg, w_re, b_re, w_gate, w_up, w_down, norm_final):
    Bn, L, D = x.shape
    o_z = 3 * DN_WIDTH
    o_b = 4 * DN_WIDTH
    o_a = o_b + DN_HEADS
    o_c = o_a + DN_HEADS
    for l in range(DEPTH):
        h = rmsnorm(x, norm_mix[l])
        u = h @ w_in[l]
        y_dn = gated_deltanet(u[..., :o_z], u[..., o_z:o_b], u[..., o_b:o_a], u[..., o_a:o_c],
                              conv_qkv[l], a_log[l], dt_bias[l], o_norm[l])
        y_cf = conformer_conv(u[..., o_c:], w_dw[l], b_dw[l], ln_g[l], ln_b[l])
        x = x + (jnp.concatenate([y_dn, y_cf], axis=-1) @ w_out[l]).astype(x.dtype)
        h = rmsnorm(x, norm_ffn[l])
        y = hier_moe(h.reshape(Bn * L, D), w_rg[l], b_rg[l], w_re[l], b_re[l],
                     w_gate[l], w_up[l], w_down[l])
        x = x + y.reshape(Bn, L, D).astype(x.dtype)
    return rmsnorm(x, norm_final)


_drawn_inputs = setup_inputs


def setup_inputs(seed=0):
    import zlib

    import numpy as np

    out = dict(_drawn_inputs(seed))
    spreads = {}
    factors = {'norm_mix': 2.817,
     'o_norm': 4.316,
     'b_dw': 3.367,
     'ln_g': 4.798,
     'ln_b': 5.158,
     'norm_ffn': 3.16,
     'b_rg': 3.976,
     'b_re': 3.71,
     'norm_final': 5.895}
    for name, (base, spread) in spreads.items():
        noise = np.random.default_rng([zlib.crc32(name.encode()), seed]).standard_normal(out[name].shape)
        drawn = base * np.exp(spread * noise) if base else spread * noise
        out[name] = __import__('jax').numpy.asarray(drawn.astype(out[name].dtype))
    for name, factor in factors.items():
        out[name] = (out[name] * factor).astype(out[name].dtype)
    return out
```

```python
from contextlib import ExitStack

import concourse.bass as bass
from concourse import mybir

F32 = mybir.dt.float32
I32 = mybir.dt.int32
U32 = mybir.dt.uint32
ACT = mybir.ActivationFunctionType
ALU = mybir.AluOpType
AX = mybir.AxisListType

P = 128
D = 1024
SEQ = 2048
KD = D // P
H = 4
DN = H * P
CF = D - DN
DN_COLS = 4 * DN + 2 * H
SHORT = 4
G_TOK = 256
NG = SEQ // G_TOK
NT = SEQ // P
LEVELS = 7
EPS = 1e-6
EXP_LN = "natural_log_exp_and_others"
SILU = "silu_and_others"
SIGMOID = "sigmoid_and_others"
CONF_TAPS = 31
N_GROUPS = 4
EXP_PER_GROUP = 8
N_EXP = N_GROUPS * EXP_PER_GROUP
N_LOGIT = N_GROUPS + N_EXP

C_ID, C_TRI, C_STRICT, C_ONES, C_LVL = 0, 1, 2, 3, 4
N_CONST = 4 + LEVELS


class Signal:

    def __init__(self, sem, per=1, lead=1):
        self.sem, self.per, self.lead = sem, per, lead

    def after(self, eng, rnd, k=None):
        k = self.per if k is None else k
        eng.wait_ge(self.sem, rnd * self.per + k + self.lead)


def bcast(ap, n):
    return ap.unsqueeze(len(ap.shape)).to_broadcast([*ap.shape, n])


def mid(ap, n):
    return ap.unsqueeze(1).to_broadcast([ap.shape[0], n, ap.shape[1]])


def deltanet_pass(nc, ctx, env):
    x, w_in, y_dnT = env["x"], env["w_in"], env["y_dnT"]
    consts, banks = env["consts"], env["banks"]
    own = ctx.enter_context(ExitStack())

    def sb(name, shape, dt=F32):
        return own.enter_context(nc.sbuf_tensor(name, shape, dt))

    def const(c):
        return consts[:, c * P:(c + 1) * P]

    ident, tri, ones = const(C_ID), const(C_TRI), const(C_ONES)

    w_sb = sb("w_dn", [P, KD, DN_COLS])
    nm_bc = sb("norm_mix_rows", [P, D])
    convw = sb("conv_taps", [P, SHORT, 12])
    onorm = sb("o_norm_col", [P, 1])
    dtb = sb("dt_bias_rows", [P, H])
    nega = sb("neg_a_rows", [P, H])
    eps = env["eps"]
    xt = sb("x_group", [P, 2, D])
    junk = sb("square_junk", [P, D])
    xss = sb("x_sumsq", [P, 2])
    xr = sb("x_rstd", [P, 2])
    hT = sb("hT", [P, KD, G_TOK])
    U = sb("u_raw", [P, 12, G_TOK + SHORT - 1])
    QKV = [sb(f"qkv{i}", [P, 12, G_TOK]) for i in range(2)]
    ZS = [sb(f"silu_z{i}", [P, 2, DN]) for i in range(2)]
    ba = sb("ba_raw", [P, 2, 8])
    ga = sb("gate_tmp", [P, 3, 2, H])
    ge = sb("gate_exp", [P, 3, 2, H])
    beta = [sb(f"beta{i}", [P, 2, H]) for i in range(2)]
    gt = [sb(f"log_decay{i}", [P, 2, H]) for i in range(2)]
    sq = sb("qk_squares", [P, 8, P])
    rn = sb("qk_rnorm", [P, 8])
    vec = sb("decay_logs", [P, 12])
    evec = sb("decays", [P, 12])
    fac = sb("row_factors", [P, 4, H])
    Dl = sb("decay_lower", [P, H, P])
    Du = sb("decay_upper", [P, H, P])
    A = sb("a_mat", [P, H, P])
    Aoff = [sb(f"a_level{l}", [P, H, P]) for l in range(LEVELS)]
    M = sb("inverseT", [P, H, P])
    T_ = sb("inverse", [P, H, P])
    X = sb("x_level", [P, H, P])
    QKd = sb("qk_decayed", [P, H, P])
    ktok = sb("k_rows", [P, H, P])
    vb = sb("v_scaled", [P, H, P])
    R = sb("solve_rhs", [P, H, P])
    S = sb("state", [P, H, P])
    vh = sb("v_new", [P, H, P])
    vd = sb("v_new_decayed", [P, H, P])
    o = sb("o_rows", [P, H, P])
    osq = sb("o_squares", [P, H, P])
    oss = sb("o_sumsq", [P, H])
    ors = sb("o_rstd", [P, H])
    Y = [sb(f"y_rows{i}", [P, H, P]) for i in range(2)]
    yT = sb("y_columns", [P, H, G_TOK])

    v4 = lambda b: b[:, :].rearrange("p (h n) -> p h n", h=H)
    ring = banks[0:2]
    bS = banks[2]
    B0, B1, B2, B3, B4 = [v4(b) for b in banks[3:8]]

    sem = env["sem"]
    weights_in = sem("p1_weights_in")
    params_in = sem("p1_params_in")
    x_in = Signal(sem("p1_x_in"), 16)
    y_out = Signal(sem("p1_y_out"), 16)
    once = sem("p1_once")
    bank_full = sem("p1_bank_full")
    bank_taken = sem("p1_bank_taken")
    x_sq = Signal(sem("p1_x_squared"), 2)
    x_ln = Signal(sem("p1_x_ln"))
    x_rs = Signal(sem("p1_x_rstd"))
    x_nrm = Signal(sem("p1_x_normed"), 2)
    conv = Signal(sem("p1_conv"), 6 * 8)
    hist = Signal(sem("p1_history"))
    gate_a = Signal(sem("p1_gate_logits"), 3)
    gate_e = Signal(sem("p1_gate_exps"), 3)
    gate_g = Signal(sem("p1_gates"), 4)
    silu_done = Signal(sem("p1_silu"), 2)
    squares = Signal(sem("p1_squares"))
    scal_full = Signal(sem("p1_scal_full"))
    gcrow_full = Signal(sem("p1_gcrow_full"))
    gram_full = Signal(sem("p1_gram_full"))
    tok_full = Signal(sem("p1_tok_full"), 2)
    a0T_full = Signal(sem("p1_a0T_full"))
    x_full = Signal(sem("p1_xlevel_full"), 6)
    d_full = Signal(sem("p1_delta_full"), 11)
    ks_full = Signal(sem("p1_ks_full"), 2)
    vhat_full = Signal(sem("p1_vhat_full"))
    o2_full = Signal(sem("p1_o2_full"))
    ds_full = Signal(sem("p1_ds_full"))
    r_ln = Signal(sem("p1_rnorm_ln"))
    r_exp = Signal(sem("p1_rnorm"))
    dec_e = Signal(sem("p1_decays"))
    d_exp = Signal(sem("p1_decay_mats"), 2)
    ktok_in = Signal(sem("p1_ktok"))
    x_copied = Signal(sem("p1_xlevel_copied"), 6)
    vh_in = Signal(sem("p1_vnew"))
    o_sq = Signal(sem("p1_o_squared"))
    o_ln = Signal(sem("p1_o_ln"))
    o_rs = Signal(sem("p1_o_rstd"))
    vec_in = Signal(sem("p1_vec"), 2)
    facs = Signal(sem("p1_factors"), 4)
    difs = Signal(sem("p1_differences"), 3)
    a_mat = Signal(sem("p1_a_mat"), 2)
    qk_d = Signal(sem("p1_qk_decayed"))
    vb_in = Signal(sem("p1_v_scaled"))
    inv = Signal(sem("p1_inverse"), 13)
    rhs = Signal(sem("p1_rhs"), 2)
    o_q = Signal(sem("p1_o_state"))
    vd_in = Signal(sem("p1_vnew_decayed"))
    st_dec = Signal(sem("p1_state_decayed"))
    state = Signal(sem("p1_state"))
    o_sum = Signal(sem("p1_o_sum"), 2)
    o_red = Signal(sem("p1_o_reduced"))
    y_rows = Signal(sem("p1_y_rows"), 2)
    du_mask = Signal(sem("p1_upper_masked"))
    a_lvl = Signal(sem("p1_a_levels"), LEVELS)
    ahead = dict(
        sync=[x_in, y_out],
        tensor=[bank_full, scal_full, gcrow_full, gram_full, tok_full, a0T_full, x_full, d_full, ks_full, vhat_full,
                o2_full, ds_full],
        scalar=[bank_taken, x_sq, x_ln, x_rs, gate_e, silu_done, squares, r_ln, r_exp, dec_e, d_exp, ktok_in, x_copied,
                vh_in, o_sq, o_ln, o_rs],
        vector=[x_nrm, conv, hist, gate_a, gate_g, vec_in, facs, difs, a_mat, qk_d, vb_in, inv, rhs, o_q, vd_in, st_dec,
                state, o_sum, o_red, y_rows],
        gpsimd=[du_mask, a_lvl])
    env["p1_done"] = y_out

    N_PROJ = 9
    U_START = 4 + N_PROJ + 4
    U_ITER = N_PROJ + 4 + 2

    def base(g):
        if isinstance(g, int) and g == -1:
            return 4
        return g * U_ITER + U_START - (4 if isinstance(g, int) and g == NG - 1 else 0)

    def units(fill, norm, chain):
        order = []
        if fill:
            order += ["ba"] + [f"c{b}" for b in range(6)]
        if chain:
            order += ["y0"]
        if fill:
            order += ["z0", "z1"]
        if norm:
            order += [f"h{n}" for n in range(4)]
        if chain:
            order += ["y1"]
        return {name: n for n, name in enumerate(order)}

    def bank_of(g_parity_base, n):
        return ring[(g_parity_base + n) % 2]

    class Iter:

        def __init__(self, g, parity, fill=True, norm=True, chain=True):
            self.g, self.p, self.fill, self.norm, self.chain = g, parity, fill, norm, chain
            self.u = units(fill, norm, chain)
            self.base = base(g)
            self.bp = 0 if not chain else (U_START + parity * U_ITER) % 2

        def bank(self, name):
            return ring[(self.bp + self.u[name]) % 2]

        def open_bank(self, eng, name):
            n = self.base + self.u[name]
            eng.wait_ge(bank_taken, n - 1 + 1)

        def full(self, eng, name):
            eng.wait_ge(bank_full, self.base + self.u[name] + 1 + 1)

        def taken(self, eng, name):
            eng.wait_ge(bank_taken, self.base + self.u[name] + 1 + 1)

    def over_groups(eng, body):
        body(Iter(-1, 1, chain=False))
        with eng.Fori(0, (NG - 2) // 2) as i:
            body(Iter(i * 2, 0))
            body(Iter(i * 2 + 1, 1))
        body(Iter(NG - 2, 0, norm=False))
        body(Iter(NG - 1, 1, fill=False, norm=False))

    def tok(g, j=0, n=G_TOK):
        return bass.ds(g * G_TOK + j * P, n)

    def sp(eng):
        eng.dma_start(nm_bc[:, :], env["norm_mix"].partition_broadcast(P)).then_inc(params_in, 16)
        eng.dma_start(convw[:, :, :], env["conv_qkvT"]).then_inc(params_in, 16)
        eng.dma_start(onorm[:, :], env["o_norm"].rearrange("(p a) -> p a", a=1)).then_inc(params_in, 16)
        eng.dma_start(dtb[:, :], env["dt_bias"].partition_broadcast(P)).then_inc(params_in, 16)
        eng.dma_start(nega[:, :], env["a_log"].partition_broadcast(P)).then_inc(params_in, 16)

        def load_x(g):
            eng.dma_start(xt[:, :, :], x[tok(g), :].rearrange("(j p) d -> p j d", p=P)).then_inc(x_in.sem, 16)

        load_x(0)
        for k in range(KD):
            eng.dma_start(w_sb[:, k, :], w_in[k * P:(k + 1) * P, 0:DN_COLS]).then_inc(weights_in, 16)

        def body(it):
            if it.norm:
                if it.chain:
                    eng.wait_ge(bank_full, it.base + 1)
                else:
                    eng.wait_ge(bank_full, 4 + 1)
                load_x(it.g + 2 if it.chain else 1)
            if it.chain:
                it.taken(eng, "y1")
                eng.dma_start(y_dnT[:, tok(it.g)].rearrange("(h p) t -> p h t", p=P), yT[:, :, :]).then_inc(y_out.sem, 16)

        over_groups(eng, body)

    def pe(eng):
        def transposes(it, names, row0):
            for n in range(4):
                j, half = n // 2, n % 2
                if names is None:
                    if n >= 2:
                        eng.wait_ge(bank_taken, n - 1 + 1)
                    dst = ring[n % 2]
                else:
                    it.open_bank(eng, names[n])
                    dst = it.bank(names[n])
                if half == 0:
                    x_nrm.after(eng, row0, j + 1)
                for q in range(4):
                    k = half * 4 + q
                    ins = eng.transpose(dst[:, q * P:(q + 1) * P], xt[:, j, k * P:(k + 1) * P], ident)
                ins.then_inc(bank_full, 1)

        def quarters(it):
            it.open_bank(eng, "ba")
            dst = it.bank("ba")
            for j in range(2):
                for k in range(KD):
                    ins = eng.matmul(dst[:, j * 8:j * 8 + 8], hT[:, k, j * P:(j + 1) * P],
                                     w_sb[:, k, 4 * DN:DN_COLS], start=(k == 0), stop=(k == KD - 1))
            ins.then_inc(bank_full, 1)
            yield
            for b in range(6):
                it.open_bank(eng, f"c{b}")
                dst = it.bank(f"c{b}")
                for q in range(4):
                    c = 2 * b + q // 2
                    for k in range(4 * (q % 2), 4 * (q % 2) + 4):
                        ins = eng.matmul(dst[:, (q // 2) * G_TOK:(q // 2 + 1) * G_TOK],
                                         w_sb[:, k, c * P:(c + 1) * P], hT[:, k, :],
                                         start=(k == 0), stop=(k == KD - 1))
                    if q == 3:
                        ins.then_inc(bank_full, 1)
                    yield
            for j in range(2):
                it.open_bank(eng, f"z{j}")
                dst = it.bank(f"z{j}")
                for q in range(4):
                    for k in (2 * q, 2 * q + 1):
                        ins = eng.matmul(dst[:, :], hT[:, k, j * P:(j + 1) * P], w_sb[:, k, 3 * DN:4 * DN],
                                         start=(k == 0), stop=(k == KD - 1))
                    if q == 3:
                        ins.then_inc(bank_full, 1)
                    yield

        def y_transpose(it, j):
            it.open_bank(eng, f"y{j}")
            y_rows.after(eng, it.g * 2 + j)
            for h in range(H):
                ins = eng.transpose(it.bank(f"y{j}")[:, h * P:(h + 1) * P], Y[j][:, h, :], ident)
            ins.then_inc(bank_full, 1)

        def tile(it, j, fill):
            g, q = it.g, QKV[it.p]
            T = g * 2 + j
            sl = slice(j * P, (j + 1) * P)
            qT = [q[:, h, sl] for h in range(H)]
            kT = [q[:, H + h, sl] for h in range(H)]
            vT = [q[:, 2 * H + h, sl] for h in range(H)]
            squares.after(eng, T)
            gate_g.after(eng, g)
            r_ln.after(eng, T - 1)
            vec_in.after(eng, T - 1)
            for c in range(8):
                eng.matmul(bS[:, c:c + 1], sq[:, c, :], ones[:, 0:1], start=True, stop=True)
            eng.matmul(bS[:, 8:12], tri, gt[it.p][:, j, :], start=True, stop=True)
            eng.matmul(bS[:, 12:16], ones, gt[it.p][:, j, :], start=True, stop=True).then_inc(scal_full.sem, 1)
            o_sum.after(eng, T - 1)
            for h in range(H):
                ins = eng.matmul(B0[:, h, :], gt[it.p][:, j, h:h + 1].to_broadcast([P, P]), tri, start=True, stop=True)
            ins.then_inc(gcrow_full.sem, 1)
            state.after(eng, T - 1)
            for h in range(H):
                eng.matmul(B1[:, h, :], kT[h], kT[h], start=True, stop=True)
            for h in range(H):
                ins = eng.matmul(B2[:, h, :], kT[h], qT[h], start=True, stop=True)
            ins.then_inc(gram_full.sem, 1)
            for h in range(H):
                ins = eng.transpose(B3[:, h, :], kT[h], ident)
            ins.then_inc(tok_full.sem, 1)
            for h in range(H):
                ins = eng.transpose(B4[:, h, :], vT[h], ident)
            ins.then_inc(tok_full.sem, 1)
            fill()
            fill()
            a_lvl.after(eng, T, 1)
            difs.after(eng, T, 1)
            for h in range(H):
                ins = eng.matmul(B0[:, h, :], Aoff[0][:, h, :], ident, start=True, stop=True)
            ins.then_inc(a0T_full.sem, 1)
            fill()
            for l in range(1, LEVELS):
                a_lvl.after(eng, T, l + 1)
                inv.after(eng, T, 2 * l)
                if l > 1:
                    x_copied.after(eng, T, l - 1)
                for h in range(H):
                    ins = eng.matmul(B0[:, h, :], Aoff[l][:, h, :], M[:, h, :], start=True, stop=True)
                ins.then_inc(x_full.sem, 1)
                if l == 1:
                    ktok_in.after(eng, T)
                    vb_in.after(eng, T)
                    for h in range(H):
                        ins = eng.matmul(B3[:, h, :], kT[h], S[:, h, :], start=True, stop=True)
                    ins.then_inc(ks_full.sem, 1)
                    for h in range(H):
                        ins = eng.matmul(B4[:, h, :], qT[h], S[:, h, :], start=True, stop=True)
                    ins.then_inc(ks_full.sem, 1)
                    a_mat.after(eng, T)
                    qk_d.after(eng, T)
                fill()
                if j == 1 and l == 3:
                    y_transpose(it, 0)
                x_copied.after(eng, T, l)
                for h in range(H):
                    ins = eng.matmul(B1[:, h, :], T_[:, h, :], X[:, h, :], start=True, stop=True)
                ins.then_inc(d_full.sem, 1)
                if l < LEVELS - 1:
                    for h in range(H):
                        ins = eng.matmul(B2[:, h, :], X[:, h, :], T_[:, h, :], start=True, stop=True)
                    ins.then_inc(d_full.sem, 1)
                fill()
            inv.after(eng, T)
            rhs.after(eng, T)
            for h in range(H):
                ins = eng.matmul(B3[:, h, :], M[:, h, :], R[:, h, :], start=True, stop=True)
            ins.then_inc(vhat_full.sem, 1)
            fill()
            vh_in.after(eng, T)
            for h in range(H):
                ins = eng.matmul(B0[:, h, :], QKd[:, h, :], vh[:, h, :], start=True, stop=True)
            ins.then_inc(o2_full.sem, 1)
            vd_in.after(eng, T)
            for h in range(H):
                ins = eng.matmul(B1[:, h, :], ktok[:, h, :], vd[:, h, :], start=True, stop=True)
            ins.then_inc(ds_full.sem, 1)
            if j == 0:
                fill()

        def body(it):
            quarter = quarters(it) if it.fill else iter(())
            fill = lambda: next(quarter, None)
            if it.chain:
                silu_done.after(eng, it.g)
                tile(it, 0, fill)
                tile(it, 1, fill)
            for _ in quarter:
                pass
            if it.norm:
                transposes(it, [f"h{n}" for n in range(4)], it.g + 2 if it.chain else 1)
            if it.chain:
                y_transpose(it, 1)

        eng.wait_ge(env["consts_in"], 16)
        eng.wait_ge(once, 3)
        transposes(None, None, 0)
        eng.wait_ge(weights_in, 16 * KD)
        eng.wait_ge(bank_taken, 4 + 1)

        def with_hT(it):
            eng.wait_ge(bank_taken, it.base + 1)
            body(it)

        over_groups(eng, with_hT)

    def act(eng):
        def norm(group):
            eng.wait_ge(x_in.sem, group * 16 + 16 + 1)
            for j in range(2):
                x_sq.after(eng, group, j)
                eng.activation(junk[:, :], xt[:, j, :], ACT.Square, accum_out=xss[:, j:j + 1]).then_inc(x_sq.sem, 1)
            x_sq.after(eng, group)
            eng.activation(xr[:, :], xss[:, :], ACT.Ln, bias=eps[:, 0:1], scale=1.0 / D).then_inc(x_ln.sem, 1)
            x_ln.after(eng, group)
            eng.activation(xr[:, :], xr[:, :], ACT.Exp, scale=-0.5).then_inc(x_rs.sem, 1)

        def take_h(it, names):
            for n in range(4):
                j, half = n // 2, n % 2
                if names is None:
                    eng.wait_ge(bank_full, n + 1 + 1)
                    src = ring[n % 2]
                else:
                    it.full(eng, names[n])
                    src = it.bank(names[n])
                eng.activation(hT[:, 4 * half:4 * half + 4, j * P:(j + 1) * P], v4(src), ACT.Copy).then_inc(bank_taken, 1)

        def take(it, name):
            if not it.fill:
                return
            it.full(eng, name)
            src, nxt = it.bank(name), 1 - it.p
            if name == "ba":
                eng.activation(ba[:, :, :], src[:, 0:16].rearrange("p (j c) -> p j c", j=2), ACT.Copy).then_inc(bank_taken, 1)
            elif name[0] == "c":
                b = int(name[1])
                if b == 0:
                    hist.after(eng, it.g if it.chain else -1)
                eng.activation(U[:, 2 * b:2 * b + 2, SHORT - 1:], src[:, :].rearrange("p (c t) -> p c t", c=2),
                               ACT.Copy).then_inc(bank_taken, 1)
            else:
                j = int(name[1])
                if it.chain and j == 0:
                    y_rows.after(eng, it.g * 2 - 1)
                eng.activation(ZS[nxt][:, j, :], src[:, :], ACT.Copy).then_inc(bank_taken, 1)

        def take_y(it, j):
            it.full(eng, f"y{j}")
            if j == 0:
                y_out.after(eng, it.g - 1)
            eng.activation(yT[:, :, j * P:(j + 1) * P], v4(it.bank(f"y{j}")), ACT.Identity,
                           scale=onorm[:, 0:1]).then_inc(bank_taken, 1)

        def gate_exps(n):
            gate_a.after(eng, n)
            eng.activation(ge[:, 0], ba[:, :, 0:H], ACT.Exp, scale=-1.0).then_inc(gate_e.sem, 1)
            eng.activation(ge[:, 1], ga[:, 1], ACT.Exp, scale=-1.0).then_inc(gate_e.sem, 1)
            gate_e.after(eng, n, 2)
            eng.activation(ge[:, 2], ge[:, 1], ACT.Ln, bias=1.0).then_inc(gate_e.sem, 1)

        def square_tile(g, p, j):
            T = g * 2 + j
            scal_full.after(eng, T - 1)
            eng.activation(sq[:, :, :], QKV[p][:, 0:8, j * P:(j + 1) * P], ACT.Square).then_inc(squares.sem, 1)

        def tile(it, j):
            T = it.g * 2 + j
            scal_full.after(eng, T)
            facs.after(eng, T - 1)
            eng.activation(rn[:, :], bS[:, 0:8], ACT.Ln, bias=eps[:, 0:1]).then_inc(r_ln.sem, 1)
            r_ln.after(eng, T)
            eng.activation(rn[:, :], rn[:, :], ACT.Exp, scale=-0.5).then_inc(r_exp.sem, 1)
            vec_in.after(eng, T)
            eng.activation(evec[:, :], vec[:, :], ACT.Exp).then_inc(dec_e.sem, 1)
            difs.after(eng, T)
            eng.activation(Dl[:, :, :], Dl[:, :, :], ACT.Exp, scale=-1.0).then_inc(d_exp.sem, 1)
            eng.activation(Du[:, :, :], Du[:, :, :], ACT.Exp).then_inc(d_exp.sem, 1)
            tok_full.after(eng, T, 1)
            eng.activation(ktok[:, :, :], B3, ACT.Copy).then_inc(ktok_in.sem, 1)
            if j == 0:
                take(it, "ba")
            if j == 0:
                square_tile(it.g, it.p, 1)
            for l in range(1, LEVELS):
                x_full.after(eng, T, l)
                eng.activation(X[:, :, :], B0, ACT.Copy).then_inc(x_copied.sem, 1)
                for at, name in {0: ((1, "c0"), (3, "c1"), (5, "c2")), 1: ((1, "c4"), (3, "c5"), (5, "z0"))}[j]:
                    if at == l:
                        take(it, name)
                if j == 1 and l == 3:
                    take_y(it, 0)
                if j == 1 and l == 2 and it.fill:
                    gate_exps(it.g + 1)
                if j == 1 and l == 4 and it.norm:
                    norm(it.g + 2)
            vhat_full.after(eng, T)
            eng.activation(vh[:, :, :], B3, ACT.Copy).then_inc(vh_in.sem, 1)
            take(it, "c3" if j == 0 else "z1")
            o_sum.after(eng, T)
            eng.activation(osq[:, :, :], o[:, :, :], ACT.Square).then_inc(o_sq.sem, 1)
            o_red.after(eng, T)
            eng.activation(ors[:, :], oss[:, :], ACT.Ln, bias=eps[:, 0:1], scale=1.0 / P).then_inc(o_ln.sem, 1)
            o_ln.after(eng, T)
            eng.activation(ors[:, :], ors[:, :], ACT.Exp, scale=-0.5).then_inc(o_rs.sem, 1)

        def body(it):
            nxt = it.g + 1 if it.chain else 0
            if it.chain:
                tile(it, 0)
                tile(it, 1)
            else:
                take(it, "ba")
                for b in range(6):
                    take(it, f"c{b}")
                take(it, "z0")
                take(it, "z1")
                gate_exps(0)
                norm(1)
            if it.norm:
                take_h(it, [f"h{n}" for n in range(4)])
            if it.fill:
                eng.preload_act_table_set(SILU)
                conv.after(eng, nxt)
                eng.wait_ge(bank_taken, it.base + it.u["z1"] + 1 + 1)
                p = 1 - it.p
                eng.activation(QKV[p][:, :, :], QKV[p][:, :, :], ACT.Silu).then_inc(silu_done.sem, 1)
                eng.activation(ZS[p][:, :, :], ZS[p][:, :, :], ACT.Silu).then_inc(silu_done.sem, 1)
                eng.preload_act_table_set(EXP_LN)
                silu_done.after(eng, nxt)
                square_tile(nxt, p, 0)
            if it.chain:
                take_y(it, 1)

        eng.preload_act_table_set(EXP_LN)
        eng.wait_ge(env["eps_in"], 1)
        eng.wait_ge(params_in, 16 * 5)
        eng.activation(nega[:, :], nega[:, :], ACT.Exp).then_inc(once, 1)
        norm(0)
        take_h(None, None)
        over_groups(eng, body)

    def dve(eng):
        def normed(group):
            x_rs.after(eng, group)
            for j in range(2):
                eng.scalar_tensor_tensor(out=xt[:, j, :], in0=xt[:, j, :], scalar=xr[:, j:j + 1], in1=nm_bc[:, :],
                                         op0=ALU.mult, op1=ALU.mult).then_inc(x_nrm.sem, 1)

        def convolve(it, b, half):
            if not it.fill:
                return
            n = it.g + 1 if it.chain else 0
            dst = QKV[1 - it.p]
            if half == 0:
                it.taken(eng, f"c{b}")
                if b == 0 and it.chain:
                    ks_full.after(eng, it.g * 2 - 1)
            for tap in (2 * half, 2 * half + 1):
                for c in (2 * b, 2 * b + 1):
                    src = U[:, c, tap:tap + G_TOK]
                    w = convw[:, tap, c:c + 1]
                    if tap == 0:
                        eng.tensor_scalar(dst[:, c, :], src, w, None, ALU.mult).then_inc(conv.sem, 1)
                    else:
                        conv.after(eng, n, b * 8 + 2 * (tap - 1) + c % 2 + 1)
                        eng.scalar_tensor_tensor(out=dst[:, c, :], in0=src, scalar=w, in1=dst[:, c, :],
                                                 op0=ALU.mult, op1=ALU.add).then_inc(conv.sem, 1)
            if b == 5 and half == 1:
                eng.tensor_copy(U[:, :, 0:SHORT - 1], U[:, :, G_TOK:]).then_inc(hist.sem, 1)

        def gates_in(it):
            n = it.g + 1 if it.chain else 0
            it.taken(eng, "ba")
            eng.tensor_tensor(ga[:, 0], ba[:, :, H:2 * H], mid(dtb[:, :], 2), ALU.add).then_inc(gate_a.sem, 1)
            gate_a.after(eng, n, 1)
            eng.scalar_tensor_tensor(out=ga[:, 1], in0=ga[:, 0], scalar=-1.0, in1=ga[:, 0], op0=ALU.mult, op1=ALU.max).then_inc(gate_a.sem, 1)
            eng.tensor_scalar(ga[:, 2], ga[:, 0], 0.0, None, ALU.max).then_inc(gate_a.sem, 1)

        def gates_out(it):
            n = it.g + 1 if it.chain else 0
            p = 1 - it.p
            gate_e.after(eng, n)
            eng.tensor_scalar(ge[:, 0], ge[:, 0], 1.0, None, ALU.add).then_inc(gate_g.sem, 1)
            eng.tensor_tensor(ga[:, 2], ga[:, 2], ge[:, 2], ALU.add).then_inc(gate_g.sem, 1)
            gate_g.after(eng, n, 2)
            eng.reciprocal(beta[p][:, :, :], ge[:, 0]).then_inc(gate_g.sem, 1)
            eng.tensor_tensor(gt[p][:, :, :], ga[:, 2], mid(nega[:, :], 2), ALU.mult).then_inc(gate_g.sem, 1)

        def tile(it, j):
            T = it.g * 2 + j
            egc, egl, dec = evec[:, 0:4], evec[:, 4:8], evec[:, 8:12]
            rb, f, fe, s = fac[:, 0], fac[:, 1], fac[:, 2], fac[:, 3]
            scal_full.after(eng, T)
            dec_e.after(eng, T - 1)
            r_ln.after(eng, T)
            eng.tensor_copy(vec[:, 0:8], bS[:, 8:16]).then_inc(vec_in.sem, 1)
            vec_in.after(eng, T, 1)
            eng.tensor_tensor(vec[:, 8:12], vec[:, 4:8], vec[:, 0:4], ALU.subtract).then_inc(vec_in.sem, 1)
            gcrow_full.after(eng, T)
            eng.tensor_tensor(Du[:, :, :], B0, bcast(vec[:, 0:4], P), ALU.subtract).then_inc(difs.sem, 1)
            difs.after(eng, T, 1)
            eng.tensor_scalar(Dl[:, :, :], Du[:, :, :], 0.0, None, ALU.max).then_inc(difs.sem, 1)
            eng.tensor_scalar(Du[:, :, :], Du[:, :, :], 0.0, None, ALU.min).then_inc(difs.sem, 1)
            r_exp.after(eng, T)
            eng.tensor_tensor(rb, rn[:, 4:8], beta[it.p][:, j, :], ALU.mult).then_inc(facs.sem, 1)
            facs.after(eng, T, 1)
            eng.tensor_tensor(f, rb, rn[:, 4:8], ALU.mult).then_inc(facs.sem, 1)
            facs.after(eng, T, 2)
            dec_e.after(eng, T)
            eng.tensor_tensor(fe, f, egc, ALU.mult).then_inc(facs.sem, 1)
            eng.tensor_scalar(s, rn[:, 0:4], float(P) ** -0.5, None, ALU.mult).then_inc(facs.sem, 1)
            d_exp.after(eng, T, 1)
            gram_full.after(eng, T)
            eng.tensor_tensor(A[:, :, :], B1, Dl[:, :, :], ALU.mult).then_inc(a_mat.sem, 1)
            a_mat.after(eng, T, 1)
            eng.tensor_tensor(A[:, :, :], A[:, :, :], bcast(f, P), ALU.mult).then_inc(a_mat.sem, 1)
            tok_full.after(eng, T)
            eng.tensor_tensor(vb[:, :, :], B4, bcast(rb, P), ALU.mult).then_inc(vb_in.sem, 1)
            du_mask.after(eng, T)
            eng.tensor_tensor(QKd[:, :, :], B2, Du[:, :, :], ALU.mult).then_inc(qk_d.sem, 1)
            a_lvl.after(eng, T, 1)
            eng.tensor_tensor(T_[:, :, :], mid(ident, H), Aoff[0][:, :, :], ALU.subtract).then_inc(inv.sem, 1)
            a0T_full.after(eng, T)
            eng.tensor_tensor(M[:, :, :], mid(ident, H), B0, ALU.subtract).then_inc(inv.sem, 1)
            if j == 1:
                convolve(it, 3, 0)
            for l in range(1, LEVELS):
                if l == 1:
                    ks_full.after(eng, T, 1)
                    facs.after(eng, T)
                    eng.tensor_tensor(R[:, :, :], B3, bcast(fe, P), ALU.mult).then_inc(rhs.sem, 1)
                    ks_full.after(eng, T)
                    eng.tensor_tensor(o[:, :, :], B4, bcast(egc, P), ALU.mult).then_inc(o_q.sem, 1)
                    rhs.after(eng, T, 1)
                    vb_in.after(eng, T)
                    eng.tensor_tensor(R[:, :, :], vb[:, :, :], R[:, :, :], ALU.subtract).then_inc(rhs.sem, 1)
                d_full.after(eng, T, 2 * l - 1)
                inv.after(eng, T, 2 * l)
                eng.tensor_tensor(M[:, :, :], M[:, :, :], B1, ALU.subtract).then_inc(inv.sem, 1)
                if l < LEVELS - 1:
                    d_full.after(eng, T, 2 * l)
                    eng.tensor_tensor(T_[:, :, :], T_[:, :, :], B2, ALU.subtract).then_inc(inv.sem, 1)
                if j == 0 and l >= 2:
                    convolve(it, (l - 2) // 2, l % 2)
                if j == 1 and l == 1:
                    convolve(it, 3, 1)
                    if it.fill:
                        gates_in(it)
                if j == 1 and 2 <= l <= 5:
                    convolve(it, 4 + (l - 2) // 2, l % 2)
                if j == 1 and l == 3 and it.fill:
                    gates_out(it)
                if j == 1 and l == 6 and it.norm:
                    normed(it.g + 2)
                if l == 3:
                    st_dec_op(T, egl)
            vh_in.after(eng, T)
            eng.tensor_tensor(vd[:, :, :], vh[:, :, :], bcast(dec, P), ALU.mult).then_inc(vd_in.sem, 1)
            if j == 0:
                convolve(it, 2, 1)
            o2_full.after(eng, T)
            o_q.after(eng, T)
            eng.tensor_tensor(o[:, :, :], o[:, :, :], B0, ALU.add).then_inc(o_sum.sem, 1)
            ds_full.after(eng, T)
            st_dec.after(eng, T)
            eng.tensor_tensor(S[:, :, :], S[:, :, :], B1, ALU.add).then_inc(state.sem, 1)
            o_sum.after(eng, T, 1)
            eng.tensor_tensor(o[:, :, :], o[:, :, :], bcast(s, P), ALU.mult).then_inc(o_sum.sem, 1)
            o_sq.after(eng, T)
            eng.tensor_reduce(oss[:, :], osq[:, :, :], AX.X, ALU.add).then_inc(o_red.sem, 1)
            o_rs.after(eng, T)
            bank_y_free(it, j)
            eng.tensor_tensor(Y[j][:, :, :], o[:, :, :], bcast(ors[:, :], P), ALU.mult).then_inc(y_rows.sem, 1)
            y_rows.after(eng, T, 1)
            silu_done.after(eng, it.g)
            eng.tensor_tensor(Y[j][:, :, :], Y[j][:, :, :], ZS[it.p][:, j, :].rearrange("p (h n) -> p h n", h=H),
                              ALU.mult).then_inc(y_rows.sem, 1)

        def bank_y_free(it, j):
            eng.wait_ge(bank_full, it.base + 1)

        def st_dec_op(T, egl):
            ks_full.after(eng, T)
            state.after(eng, T - 1)
            eng.tensor_tensor(S[:, :, :], S[:, :, :], bcast(egl, P), ALU.mult).then_inc(st_dec.sem, 1)

        def body(it):
            if it.chain:
                tile(it, 0)
                tile(it, 1)
            else:
                gates_in(it)
                for b in range(6):
                    convolve(it, b, 0)
                    convolve(it, b, 1)
                gates_out(it)
                normed(1)

        eng.memset(U[:, :, 0:SHORT - 1], 0.0).then_inc(once, 1)
        eng.memset(S[:, :, :], 0.0).then_inc(once, 1)
        eng.wait_ge(params_in, 16 * 5)
        eng.wait_ge(once, 3)
        eng.tensor_scalar(nega[:, :], nega[:, :], -1.0, None, ALU.mult).then_inc(once, 1)
        eng.wait_ge(once, 4)
        normed(0)
        over_groups(eng, body)

    def pool(eng):
        def tile(it, j):
            T = it.g * 2 + j
            d_exp.after(eng, T)
            eng.tensor_tensor(Du[:, :, :], Du[:, :, :], mid(tri, H), ALU.mult).then_inc(du_mask.sem, 1)
            a_mat.after(eng, T)
            vhat_full.after(eng, T - 1)
            for l in range(LEVELS):
                eng.tensor_tensor(Aoff[l][:, :, :], A[:, :, :], mid(const(C_LVL + l), H), ALU.mult).then_inc(a_lvl.sem, 1)

        def body(it):
            if it.chain:
                tile(it, 0)
                tile(it, 1)

        over_groups(eng, body)

    def started(name, program):
        def run(eng):
            for s in ahead[name]:
                eng.sem_inc(s.sem if isinstance(s, Signal) else s, 1)
            program(eng)
        return run

    programs = dict(sync=sp, tensor=pe, scalar=act, vector=dve, gpsimd=pool)
    return own, {name: started(name, program) for name, program in programs.items()}


def conformer_pass(nc, ctx, env):
    x, w_in, w_out = env["x"], env["w_in"], env["w_out"]
    consts, banks, eps = env["consts"], env["banks"], env["eps"]
    own = ctx.enter_context(ExitStack())

    def sb(name, shape, dt=F32):
        return own.enter_context(nc.sbuf_tensor(name, shape, dt))

    ident = consts[:, C_ID * P:(C_ID + 1) * P]
    ones = consts[:, C_ONES * P:(C_ONES + 1) * P]
    HIST = CONF_TAPS - 1
    CB = CF // P
    HALF = D // 2

    w_cf = sb("w_cf", [P, KD, 2 * CF])
    w_o = sb("w_out_rows", [P, KD, D])
    w_r = sb("w_router", [P, KD, N_LOGIT])
    b_r = sb("b_router_rows", [P, N_LOGIT])
    nm_bc = sb("norm_mix_rows2", [P, D])
    nf_bc = sb("norm_ffn_rows", [P, D])
    taps = sb("dw_taps", [P, CONF_TAPS, CB])
    cols = sb("cf_columns", [P, 3, CB])
    mean_w = sb("mean_weights", [P, P])
    xt = sb("x2_group", [P, 2, D])
    junk = sb("square_junk2", [P, D])
    xss = sb("x2_sumsq", [P, 2])
    xr = sb("x2_rstd", [P, 2])
    hT = sb("hT2", [P, KD, G_TOK])
    sg = sb("glu_sigmoid", [P, CB, G_TOK])
    G = [sb(f"glu{i}", [P, CB, HIST + G_TOK]) for i in range(2)]
    C = [sb(f"conv_out{i}", [P, CB, G_TOK]) for i in range(2)]
    csq = sb("conv_squares", [P, CB, G_TOK])
    vrs = sb("ln_rstd", [P, G_TOK])
    ycf = sb("y_cf_columns", [P, CB, G_TOK])
    ydn = sb("y_dn_columns", [P, CB, G_TOK])
    res = sb("residual", [P, 2, D])
    x2 = [sb(f"x_mixed{i}", [P, 2, D]) for i in range(2)]
    x2ss = sb("x_mixed_sumsq", [P, 2])
    x2rs = sb("x_mixed_rstd", [P, 2])
    h2 = sb("h_ffn", [P, 2, D])
    h2T = sb("h_ffnT", [P, KD, G_TOK])
    logits = env["logits"]

    v4 = lambda b: b[:, :].rearrange("p (h n) -> p h n", h=4)
    ring, outb, bStat, bLog = banks[0:4], banks[4:6], banks[6], banks[7]
    mean_v, var_v = bStat[:, 0:G_TOK], bStat[:, G_TOK:2 * G_TOK]

    sem = env["sem"]
    params_in, w_cf_in, w_o_in = sem("p2_params_in"), sem("p2_wcf_in"), sem("p2_wout_in")
    mean_w_in = sem("p2_mean_weights")
    x_in, ydn_in, res_in = Signal(sem("p2_x_in"), 16), Signal(sem("p2_ydn_in"), 16), Signal(sem("p2_res_in"), 16)
    x2_out, h2_out = Signal(sem("p2_x2_out"), 16), Signal(sem("p2_h2_out"), 16)
    h_full, glu_full = Signal(sem("p2_h_full"), 4), Signal(sem("p2_glu_full"), 4)
    mean_full, var_full = Signal(sem("p2_mean_full")), Signal(sem("p2_var_full"))
    out_full = Signal(sem("p2_out_full"), 4)
    h2_full, log_full = Signal(sem("p2_h2_full"), 4), Signal(sem("p2_logits_full"))
    x_sq, x_ln, x_rs = Signal(sem("p2_x_sq"), 2), Signal(sem("p2_x_ln")), Signal(sem("p2_x_rstd"))
    h_taken, h2_taken = Signal(sem("p2_h_taken"), 4), Signal(sem("p2_h2_taken"), 4)
    c_sq, v_ln, v_rs = Signal(sem("p2_c_sq")), Signal(sem("p2_v_ln")), Signal(sem("p2_v_rstd"))
    silu_c, sigm = Signal(sem("p2_silu"), 4), Signal(sem("p2_sigmoid"), 4)
    x2_sq, x2_ln, x2_rs = Signal(sem("p2_x2_sq"), 2), Signal(sem("p2_x2_ln")), Signal(sem("p2_x2_rstd"))
    x_nrm, h2_nrm = Signal(sem("p2_x_normed"), 2), Signal(sem("p2_h2_normed"), 2)
    centred, c_nrm = Signal(sem("p2_centred")), Signal(sem("p2_c_normed"))
    glu, conv = Signal(sem("p2_glu"), 4), Signal(sem("p2_conv"), CONF_TAPS * 4)
    x2_sum, logit = Signal(sem("p2_x2_sum"), 4), Signal(sem("p2_logit"))
    hist = Signal(sem("p2_history"))
    ahead = dict(
        sync=[x_in, ydn_in, res_in, x2_out, h2_out],
        tensor=[h_full, glu_full, mean_full, var_full, out_full, h2_full, log_full],
        scalar=[x_sq, x_ln, x_rs, h_taken, h2_taken, c_sq, v_ln, v_rs, silu_c, sigm, x2_sq, x2_ln, x2_rs],
        vector=[x_nrm, h2_nrm, centred, c_nrm, glu, conv, x2_sum, logit, hist],
        gpsimd=[])
    env["x2_out"], env["h2_out"], env["logit"] = x2_out, h2_out, logit

    class Step:

        def __init__(self, s, parity, steady=False):
            self.s, self.p = s, parity
            def has(n):
                return steady or 0 <= s + n < NG
            self.norm, self.proj, self.conv, self.out, self.logits = has(2), has(1), has(0), has(-1), has(-2)
            self.steady = steady

    def over_steps(eng, body):
        for s in (-1, 0, 1):
            body(Step(s, s % 2))
        with eng.Fori(0, (NG - 4) // 2) as i:
            body(Step(i * 2 + 2, 0, True))
            body(Step(i * 2 + 3, 1, True))
        for s in range(NG - 2, NG + 2):
            body(Step(s, s % 2))

    def tok(g, j=0, n=G_TOK):
        return bass.ds(g * G_TOK + j * P, n)

    def by_tile(dram, g):
        return dram[tok(g), :].rearrange("(j p) d -> p j d", p=P)

    def sp(eng):
        def load_x(g):
            eng.dma_start(xt[:, :, :], by_tile(x, g)).then_inc(x_in.sem, 16)

        load_x(0)
        for dst, src in ((nm_bc, env["norm_mix"].partition_broadcast(P)), (nf_bc, env["norm_ffn"].partition_broadcast(P)),
                         (b_r, env["b_router"].partition_broadcast(P))):
            eng.dma_start(dst[:, :], src).then_inc(params_in, 16)
        eng.dma_start(taps[:, :, :], env["w_dw"]).then_inc(params_in, 16)
        eng.dma_start(cols[:, :, :], env["cf_cols"]).then_inc(params_in, 16)
        eng.dma_start(w_r[:, :, :], env["w_router"].rearrange("(k p) n -> p k n", p=P)).then_inc(params_in, 16)
        for k in range(KD):
            eng.dma_start(w_cf[:, k, :], w_in[k * P:(k + 1) * P, DN_COLS:]).then_inc(w_cf_in, 16)
        for k in range(KD):
            eng.dma_start(w_o[:, k, :], w_out[k * P:(k + 1) * P, :]).then_inc(w_o_in, 16)

        def body(it):
            s = it.s
            if it.norm:
                h_full.after(eng, s + 1)
                load_x(s + 2)
            if it.out:
                if it.steady or s >= 2:
                    x2_sum.after(eng, s - 2)
                eng.dma_start(ydn[:, :, :], env["y_dnT"][:, tok(s - 1)].rearrange("(h p) t -> p h t", p=P)).then_inc(ydn_in.sem, 16)
                eng.dma_start(res[:, :, :], by_tile(x, s - 1)).then_inc(res_in.sem, 16)
            if it.logits:
                h2_nrm.after(eng, s - 2)
                eng.dma_start(by_tile(env["h_rows"], s - 2), h2[:, :, :]).then_inc(h2_out.sem, 16)
            if it.out:
                x2_sum.after(eng, s - 1)
                eng.dma_start(by_tile(env["x_rows"], s - 1), x2[1 - it.p][:, :, :]).then_inc(x2_out.sem, 16)

        def first(it):
            if not it.steady and it.s == -1:
                h_full.after(eng, 0)
                load_x(1)
            else:
                body(it)

        over_steps(eng, first)

    def pe(eng):
        def transposes(g, src, full, waits, ready):
            for n in range(4):
                j, half = n // 2, n % 2
                for w in waits:
                    w(n)
                if half == 0:
                    ready.after(eng, g, j + 1)
                for q in range(4):
                    k = half * 4 + q
                    ins = eng.transpose(ring[n][:, q * P:(q + 1) * P], src[:, j, k * P:(k + 1) * P], ident)
                ins.then_inc(full.sem, 1)

        def glu_unit(it, b):
            g = it.s + 1
            if it.logits:
                h2_taken.after(eng, it.s - 2, b + 1)
            for part in range(2):
                c = b + part * CB
                for k in range(KD):
                    ins = eng.matmul(ring[b][:, part * G_TOK:(part + 1) * G_TOK], w_cf[:, k, c * P:(c + 1) * P],
                                     hT[:, k, :], start=(k == 0), stop=(k == KD - 1))
            ins.then_inc(glu_full.sem, 1)

        def body(it):
            s = it.s
            if it.logits:
                if it.steady or s <= NG - 2:
                    free = [lambda n: h_taken.after(eng, s + 1, n + 1)]
                elif s == NG - 1:
                    free = [lambda n: glu.after(eng, NG - 1, n + 1)]
                else:
                    free = [lambda n: h2_taken.after(eng, s - 3, n + 1)]
                transposes(s - 2, h2, h2_full, free, h2_nrm)
            if it.out:
                conv.after(eng, s - 1)
                if it.steady or s >= 2:
                    centred.after(eng, s - 2)
                for b in range(CB):
                    ins = eng.matmul(mean_v, mean_w[:, :], C[1 - it.p][:, b, :], start=(b == 0), stop=(b == CB - 1))
                ins.then_inc(mean_full.sem, 1)
            if it.proj:
                h_taken.after(eng, s + 1)
                glu_unit(it, 0)
            if it.logits:
                h2_taken.after(eng, s - 2)
                if it.steady or s >= 3:
                    logit.after(eng, s - 3)
                for j in range(2):
                    for k in range(KD):
                        ins = eng.matmul(bLog[:, j * N_LOGIT:(j + 1) * N_LOGIT], h2T[:, k, j * P:(j + 1) * P],
                                         w_r[:, k, :], start=(k == 0), stop=(k == KD - 1))
                ins.then_inc(log_full.sem, 1)
            if it.out:
                c_sq.after(eng, s - 1)
                if it.steady or s >= 2:
                    v_ln.after(eng, s - 2)
                for b in range(CB):
                    ins = eng.matmul(var_v, mean_w[:, :], csq[:, b, :], start=(b == 0), stop=(b == CB - 1))
                ins.then_inc(var_full.sem, 1)
            if it.proj:
                for b in range(1, 4):
                    glu_unit(it, b)

            def out_tile(j):
                for half in range(2):
                    if j == 1:
                        x2_sum.after(eng, s - 1, half + 1)
                    elif it.steady or s >= 2:
                        x2_sum.after(eng, s - 2, 3 + half)
                    for k in range(KD):
                        y = ydn if k < CB else ycf
                        ins = eng.matmul(outb[half][:, :], y[:, k % CB, j * P:(j + 1) * P],
                                         w_o[:, k, half * HALF:(half + 1) * HALF], start=(k == 0), stop=(k == KD - 1))
                    ins.then_inc(out_full.sem, 1)

            if it.out:
                if not it.steady and s == 1:
                    eng.wait_ge(w_o_in, 16 * KD)
                ydn_in.after(eng, s - 1)
                silu_c.after(eng, s - 1)
                out_tile(0)
            if it.norm:
                transposes(s + 2, xt, h_full, [lambda n: glu.after(eng, s + 1, n + 1)], x_nrm)
            if it.out:
                out_tile(1)

        eng.wait_ge(params_in, 16 * 6)
        eng.wait_ge(mean_w_in, 1)
        transposes(0, xt, h_full, [], x_nrm)
        eng.wait_ge(w_cf_in, 16 * KD)
        over_steps(eng, body)

    def act(eng):
        def x_norm(g):
            x_in.after(eng, g)
            for j in range(2):
                x_sq.after(eng, g, j)
                eng.activation(junk[:, :], xt[:, j, :], ACT.Square, accum_out=xss[:, j:j + 1]).then_inc(x_sq.sem, 1)
            x_sq.after(eng, g)
            eng.activation(xr[:, :], xss[:, :], ACT.Ln, bias=eps[:, 0:1], scale=1.0 / D).then_inc(x_ln.sem, 1)
            x_ln.after(eng, g)
            eng.activation(xr[:, :], xr[:, :], ACT.Exp, scale=-0.5).then_inc(x_rs.sem, 1)

        def take(g, full, dst, sig):
            for n in range(4):
                j, half = n // 2, n % 2
                full.after(eng, g, n + 1)
                eng.activation(dst[:, 4 * half:4 * half + 4, j * P:(j + 1) * P], v4(ring[n]), ACT.Copy).then_inc(sig.sem, 1)

        def body(it):
            s = it.s
            if not it.steady and s == -1:
                eng.preload_act_table_set(EXP_LN)
                x_norm(1)
            if it.logits:
                x2_sq.after(eng, s - 2)
                eng.activation(x2rs[:, :], x2ss[:, :], ACT.Ln, bias=eps[:, 0:1], scale=1.0 / D).then_inc(x2_ln.sem, 1)
                x2_ln.after(eng, s - 2)
                eng.activation(x2rs[:, :], x2rs[:, :], ACT.Exp, scale=-0.5).then_inc(x2_rs.sem, 1)
            if it.norm and (it.steady or s != -1):
                x_norm(s + 2)
            if it.logits:
                if it.steady or s >= 3:
                    log_full.after(eng, s - 3)
                take(s - 2, h2_full, h2T, h2_taken)
            if it.out:
                centred.after(eng, s - 1)
                eng.activation(csq[:, :, :], C[1 - it.p][:, :, :], ACT.Square).then_inc(c_sq.sem, 1)
                var_full.after(eng, s - 1)
                if it.steady or s >= 2:
                    c_nrm.after(eng, s - 2)
                eng.activation(vrs[:, :], var_v, ACT.Ln, bias=eps[:, 0:1]).then_inc(v_ln.sem, 1)
                v_ln.after(eng, s - 1)
                eng.activation(vrs[:, :], vrs[:, :], ACT.Exp, scale=-0.5).then_inc(v_rs.sem, 1)
                eng.preload_act_table_set(SILU)
                c_nrm.after(eng, s - 1)
                if it.steady or s >= 2:
                    out_full.after(eng, s - 2)
                for b in range(CB):
                    eng.activation(ycf[:, b, :], C[1 - it.p][:, b, :], ACT.Silu, scale=cols[:, 1, b:b + 1],
                                   bias=cols[:, 2, b:b + 1]).then_inc(silu_c.sem, 1)
            if it.proj:
                eng.preload_act_table_set(SIGMOID)
                for b in range(CB):
                    glu_full.after(eng, s + 1, b + 1)
                    if it.conv:
                        glu.after(eng, s, b + 1)
                    eng.activation(sg[:, b, :], ring[b][:, G_TOK:], ACT.Sigmoid).then_inc(sigm.sem, 1)
            if it.norm:
                take(s + 2, h_full, hT, h_taken)
            eng.preload_act_table_set(EXP_LN)
            if it.out:
                for j in range(2):
                    x2_sum.after(eng, s - 1, 2 * j + 2)
                    x2_sq.after(eng, s - 1, j)
                    if it.logits and j == 0:
                        x2_rs.after(eng, s - 2)
                    eng.activation(junk[:, :], x2[1 - it.p][:, j, :], ACT.Square, accum_out=x2ss[:, j:j + 1]).then_inc(x2_sq.sem, 1)

        eng.preload_act_table_set(EXP_LN)
        x_norm(0)
        take(0, h_full, hT, h_taken)
        over_steps(eng, body)

    def dve(eng):
        def normed(g):
            x_rs.after(eng, g)
            for j in range(2):
                eng.scalar_tensor_tensor(out=xt[:, j, :], in0=xt[:, j, :], scalar=xr[:, j:j + 1], in1=nm_bc[:, :],
                                         op0=ALU.mult, op1=ALU.mult).then_inc(x_nrm.sem, 1)

        def glu_unit(it, b):
            if not it.proj:
                return
            g = it.s + 1
            sigm.after(eng, g, b + 1)
            if b == 0 and (it.steady or it.s >= 0):
                if it.steady or it.s >= 1:
                    conv.after(eng, it.s - 1)
                hist.after(eng, it.s)
            eng.tensor_tensor(G[1 - it.p][:, b, HIST:], ring[b][:, 0:G_TOK], sg[:, b, :], ALU.mult).then_inc(glu.sem, 1)

        def convolve(it, t0, n):
            if not it.conv:
                return
            src, dst = G[it.p], C[it.p]
            if t0 == 0:
                glu.after(eng, it.s)
                if it.steady or it.s >= 1:
                    hist.after(eng, it.s - 1)
                if it.steady or it.s >= 2:
                    silu_c.after(eng, it.s - 2)
            for tap in range(t0, t0 + n):
                for b in range(CB):
                    w = taps[:, tap, b:b + 1]
                    if tap == 0:
                        ins = eng.tensor_scalar(dst[:, b, :], src[:, b, tap:tap + G_TOK], w, cols[:, 0, b:b + 1],
                                                ALU.mult, ALU.add)
                    else:
                        conv.after(eng, it.s, CB * (tap - 1) + b + 1)
                        ins = eng.scalar_tensor_tensor(out=dst[:, b, :], in0=src[:, b, tap:tap + G_TOK], scalar=w,
                                                       in1=dst[:, b, :], op0=ALU.mult, op1=ALU.add)
                    ins.then_inc(conv.sem, 1)

        def add_residual(it, j):
            if not it.out:
                return
            g = it.s - 1
            if j == 0:
                res_in.after(eng, g)
                if it.steady or it.s >= 3:
                    x2_out.after(eng, g - 2)
            for half in range(2):
                out_full.after(eng, g, 2 * j + half + 1)
                cs = slice(half * HALF, (half + 1) * HALF)
                eng.tensor_tensor(x2[1 - it.p][:, j, cs], outb[half][:, :], res[:, j, cs], ALU.add).then_inc(x2_sum.sem, 1)

        def body(it):
            s = it.s
            if it.logits:
                x2_rs.after(eng, s - 2)
                if it.steady or s >= 3:
                    h2_out.after(eng, s - 3)
                    h2_full.after(eng, s - 3)
                for j in range(2):
                    eng.scalar_tensor_tensor(out=h2[:, j, :], in0=x2[it.p][:, j, :], scalar=x2rs[:, j:j + 1],
                                             in1=nf_bc[:, :], op0=ALU.mult, op1=ALU.mult).then_inc(h2_nrm.sem, 1)
            if it.out:
                mean_full.after(eng, s - 1)
                c = C[1 - it.p]
                eng.tensor_tensor(c[:, :, :], c[:, :, :], mid(mean_v, CB), ALU.subtract).then_inc(centred.sem, 1)
            if it.conv and it.proj:
                glu.after(eng, s)
                if it.steady or s >= 1:
                    conv.after(eng, s - 1)
                eng.tensor_copy(G[1 - it.p][:, :, 0:HIST], G[it.p][:, :, G_TOK:]).then_inc(hist.sem, 1)
            convolve(it, 0, 4)
            if it.logits:
                log_full.after(eng, s - 2)
                eng.tensor_tensor(logits[:, bass.ds((s - 2) * 2, 2), :],
                                  bLog[:, 0:2 * N_LOGIT].rearrange("p (j n) -> p j n", j=2), mid(b_r[:, :], 2),
                                  ALU.add).then_inc(logit.sem, 1)
            if it.out:
                v_rs.after(eng, s - 1)
                c = C[1 - it.p]
                centred.after(eng, s - 1)
                eng.tensor_tensor(c[:, :, :], c[:, :, :], mid(vrs[:, :], CB), ALU.mult).then_inc(c_nrm.sem, 1)
            convolve(it, 4, 4)
            glu_unit(it, 0)
            convolve(it, 8, 4)
            glu_unit(it, 1)
            convolve(it, 12, 3)
            glu_unit(it, 2)
            if it.norm:
                normed(s + 2)
            convolve(it, 15, 5)
            glu_unit(it, 3)
            convolve(it, 20, 4)
            add_residual(it, 0)
            convolve(it, 24, 4)
            add_residual(it, 1)
            convolve(it, 28, 3)

        eng.memset(G[0][:, :, 0:HIST], 0.0).then_inc(env["g_hist0"], 1)
        eng.wait_ge(env["g_hist0"], 1)
        eng.tensor_scalar(mean_w[:, :], ones, 1.0 / CF, None, ALU.mult).then_inc(mean_w_in, 1)
        eng.wait_ge(params_in, 16 * 6)
        normed(0)
        over_steps(eng, body)

    def started(name, program):
        def run(eng):
            for s in ahead[name]:
                eng.sem_inc(s.sem, 1)
            program(eng)
        return run

    programs = dict(sync=sp, tensor=pe, scalar=act, vector=dve)
    return own, {name: started(name, program) for name, program in programs.items()}


N_BLOCK = SEQ * 2 // P + N_EXP
SLOTS = N_EXP * SEQ
FAR = -1e30
ENTRY = 4


def router_pass(nc, ctx, env):
    consts, banks, logits = env["consts"], env["banks"], env["logits"]
    own = ctx.enter_context(ExitStack())
    NGr, NE = N_GROUPS, EXP_PER_GROUP

    def sb(name, shape, dt=F32):
        return own.enter_context(nc.sbuf_tensor(name, shape, dt))

    strict = consts[:, C_STRICT * P:(C_STRICT + 1) * P]
    ones = consts[:, C_ONES * P:(C_ONES + 1) * P]
    gl = logits[:, :, 0:NGr]
    el = logits[:, :, NGr:].rearrange("p t (g e) -> p t g e", g=NGr)
    down = sb("count_down", [P, NE])
    gmax, gsum, pg = sb("r_gmax", [P, NT]), sb("r_gsum", [P, NT]), sb("r_pg", [P, NT])
    gd, gval, gsel = sb("r_gd", [P, NT, NGr]), sb("r_gval", [P, NT, NGr]), sb("r_gsel", [P, NT, NGr])
    esel4, e8 = sb("r_esel4", [P, NT, NGr, NE]), sb("r_e8", [P, NT, NE])
    m = [sb(f"r_max{k}", [P, NT]) for k in range(2)]
    val, vmax = sb("r_val", [P, NT, NE]), sb("r_vmax", [P, NT])
    one = [sb(f"r_onehot{k}", [P, NT, NE]) for k in range(2)]
    e8b = sb("r_e8b", [P, NT, NE])
    ed, wden = sb("r_exp_diff", [P, NT]), sb("r_wden", [P, NT])
    wt = [sb(f"r_weight{k}", [P, NT]) for k in range(2)]
    OH = [sb(f"r_choice{k}", [P, NT, NGr, NE]) for k in range(2)]
    M = sb("r_chosen", [P, NT, N_EXP])
    cum = sb("r_before", [P, NT + 1, N_EXP])
    region = sb("r_region", [P, N_EXP])
    R = sb("r_rank", [P, NT, N_EXP])
    prod = sb("r_prod", [P, NT, N_EXP])
    slotf = sb("r_slotf", [P, 2, NT])
    slot = sb("r_slot", [P, NT, 2], U32)
    entry = sb("r_entry", [P, NT, 2, ENTRY], I32)
    fill = sb("r_fill", [P, SLOTS // P + 2, ENTRY], I32)
    zero_rows = sb("r_zero_rows", [P, D])
    cnt = sb("r_count", [P, N_EXP])
    cnt_i = sb("r_count_i", [P, N_EXP], I32)
    nbf = sb("r_blocks_f", [P, N_EXP])
    bs = [sb(f"r_base{k}", [P, N_EXP]) for k in range(2)]
    base = sb("r_base", [P, N_EXP])
    step = sb("r_step", [P, N_EXP])
    blk = sb("r_block_no", [P, N_BLOCK + 2])
    reach = sb("r_reach", [P, N_BLOCK + 2, N_EXP])
    first = sb("r_first_slot", [P, N_BLOCK + 2])
    meta = env["meta"]

    sem = env["sem"]
    fill_made, fill_in = sem("r_fill_made"), sem("r_fill_in")
    entries_in = sem("r_entries_in")
    steps = sem("r_steps")
    exps = sem("r_exps")
    ranks = sem("r_ranks")
    iotas = sem("r_iotas")
    entry_ready = sem("r_entry_ready")
    env["meta_in"] = sem("r_meta_in")
    at = {}

    def dve(eng):
        n = [0]

        def op(name, ins):
            ins.then_inc(steps, 1)
            n[0] += 1
            at[name] = n[0]

        def need(*names):
            eng.wait_ge(steps, max(at[x] for x in names))

        eng.wait_ge(iotas, 6)
        env["logit"].after(eng, NG - 1)
        op("gmax", eng.tensor_reduce(gmax[:, :], gl, AX.X, ALU.max))
        need("gmax")
        op("gd", eng.tensor_tensor(gd[:, :, :], gl, bcast(gmax[:, :], NGr), ALU.subtract))
        op("geq", eng.tensor_tensor(gval[:, :, :], gl, bcast(gmax[:, :], NGr), ALU.is_equal))
        need("geq")
        op("gval", eng.tensor_tensor(gval[:, :, :], gval[:, :, :], mid(down[:, NE - NGr:], NT), ALU.mult))
        need("gval")
        op("gtop", eng.tensor_reduce(vmax[:, :], gval[:, :, :], AX.X, ALU.max))
        need("gtop")
        op("gsel", eng.tensor_tensor(gsel[:, :, :], gval[:, :, :], bcast(vmax[:, :], NGr), ALU.is_equal))
        eng.wait_ge(exps, 1)
        op("gsum", eng.tensor_reduce(gsum[:, :], gd[:, :, :], AX.X, ALU.add))
        need("gsum")
        op("pg", eng.reciprocal(pg[:, :], gsum[:, :]))
        op("esel4", eng.tensor_tensor(esel4[:, :, :, :], el, bcast(gsel[:, :, :], NE), ALU.mult))
        need("esel4")
        op("e8", eng.tensor_reduce(e8[:, :, :], esel4[:, :, :, :].rearrange("p t g e -> p t e g"), AX.X, ALU.add))
        for k in range(2):
            src = e8 if k == 0 else e8b
            need("e8" if k == 0 else "e8b")
            op(f"m{k}", eng.tensor_reduce(m[k][:, :], src[:, :, :], AX.X, ALU.max))
            need(f"m{k}")
            op("val", eng.tensor_tensor(val[:, :, :], src[:, :, :], bcast(m[k][:, :], NE), ALU.is_equal))
            need("val")
            op("val", eng.tensor_tensor(val[:, :, :], val[:, :, :], mid(down[:, :], NT), ALU.mult))
            need("val")
            op("vmax", eng.tensor_reduce(vmax[:, :], val[:, :, :], AX.X, ALU.max))
            need("vmax")
            op(f"one{k}", eng.tensor_tensor(one[k][:, :, :], val[:, :, :], bcast(vmax[:, :], NE), ALU.is_equal))
            need(f"one{k}")
            if k == 0:
                op("e8b", eng.scalar_tensor_tensor(out=e8b[:, :, :], in0=one[0][:, :, :], scalar=FAR, in1=e8[:, :, :],
                                                   op0=ALU.mult, op1=ALU.add))
            for g in range(NGr):
                op(f"OH{k}", eng.tensor_tensor(OH[k][:, :, g, :], one[k][:, :, :],
                                               gsel[:, :, g:g + 1].to_broadcast([P, NT, NE]), ALU.mult))
        op("ed", eng.tensor_tensor(ed[:, :], m[1][:, :], m[0][:, :], ALU.subtract))
        need("OH1")
        ch = [OH[k][:, :, :, :].rearrange("p t g e -> p t (g e)") for k in range(2)]
        op("M", eng.tensor_tensor(M[:, :, :], ch[0], ch[1], ALU.add))
        op("cum0", eng.memset(cum[:, 0, :], 0.0))
        need("cum0")
        for t in range(NT):
            op(f"cum{t + 1}", eng.tensor_tensor(cum[:, t + 1, :], cum[:, t, :], M[:, t, :], ALU.add))
            need(f"cum{t + 1}")
        eng.wait_ge(exps, 2)
        op("wden", eng.tensor_scalar(wden[:, :], ed[:, :], 1.0, None, ALU.add))
        need("wden")
        op("wden", eng.reciprocal(wden[:, :], wden[:, :]))
        need("wden")
        op("wt0", eng.tensor_tensor(wt[0][:, :], pg[:, :], wden[:, :], ALU.mult))
        need("wt0")
        op("wt1", eng.tensor_tensor(wt[1][:, :], wt[0][:, :], ed[:, :], ALU.mult))
        eng.wait_ge(ranks, 1)
        op("R", eng.tensor_tensor(R[:, :, :], banks[0][:, :].rearrange("p (t e) -> p t e", t=NT),
                                  mid(region[:, :], NT), ALU.add))
        for k in range(2):
            need("R")
            op("prod", eng.tensor_tensor(prod[:, :, :], ch[k], R[:, :, :], ALU.mult))
            need("prod")
            op("slotf", eng.tensor_reduce(slotf[:, k, :], prod[:, :, :], AX.X, ALU.add))
            need("slotf")
            op("slot", eng.tensor_copy(slot[:, :, k], slotf[:, k, :]))
            need("slot", "wt1")
            op("entry", eng.tensor_copy(entry[:, :, k, 2].bitcast(F32), wt[k][:, :]))
            need("entry")
        eng.sem_inc(entry_ready, 1)
        eng.wait_ge(ranks, 2)
        op("cnt", eng.tensor_scalar(cnt[:, :], banks[1][:, 0:N_EXP], 1.0, float(P - 1), ALU.max, ALU.add))
        need("cnt")
        op("cnt_i", eng.tensor_copy(cnt_i[:, :], cnt[:, :]))
        need("cnt_i")
        op("nblk", eng.tensor_scalar(cnt_i[:, :], cnt_i[:, :], 7, None, ALU.arith_shift_right))
        need("nblk")
        op("nbf", eng.tensor_copy(nbf[:, :], cnt_i[:, :]))
        src, name = nbf, "nbf"
        for i in range(5):
            s, dst = 1 << i, bs[i % 2]
            need(name)
            op("a", eng.tensor_copy(dst[:, 0:s], src[:, 0:s]))
            op(f"bs{i}", eng.tensor_tensor(dst[:, s:], src[:, s:], src[:, 0:N_EXP - s], ALU.add))
            src, name = dst, f"bs{i}"
        need(name)
        op("base", eng.tensor_tensor(base[:, :], src[:, :], nbf[:, :], ALU.subtract))
        op("meta", eng.tensor_copy(meta[:, N_EXP:2 * N_EXP], src[:, :]))
        need("base")
        op("meta", eng.tensor_copy(meta[:, 0:N_EXP], base[:, :]))
        need("base")
        op("step0", eng.memset(step[:, 0:1], 0.0))
        op("step", eng.tensor_scalar(step[:, 1:], nbf[:, 0:N_EXP - 1], -float(P), float(SEQ), ALU.mult, ALU.add))
        op("reach", eng.tensor_tensor(reach[:, :, :], bcast(blk[:, :], N_EXP), mid(base[:, :], N_BLOCK + 2), ALU.is_ge))
        need("reach")
        op("reach", eng.tensor_tensor(reach[:, :, :], reach[:, :, :], mid(step[:, :], N_BLOCK + 2), ALU.mult))
        need("reach")
        op("first", eng.tensor_reduce(first[:, :], reach[:, :, :], AX.X, ALU.add))
        need("first")
        op("first", eng.scalar_tensor_tensor(out=first[:, :], in0=blk[:, :], scalar=float(P), in1=first[:, :],
                                             op0=ALU.mult, op1=ALU.add))
        need("first")
        eng.tensor_copy(meta[:, 2 * N_EXP:2 * N_EXP + N_BLOCK + 2], first[:, :]).then_inc(env["meta_in"], 1)

    def act(eng):
        eng.preload_act_table_set(EXP_LN)
        eng.wait_ge(steps, at["gd"])
        eng.activation(gd[:, :, :], gd[:, :, :], ACT.Exp).then_inc(exps, 1)
        eng.wait_ge(steps, at["ed"])
        eng.activation(ed[:, :], ed[:, :], ACT.Exp).then_inc(exps, 1)

    def pe(eng):
        flat = lambda a: a.rearrange("p t e -> p (t e)")
        eng.wait_ge(steps, at[f"cum{NT}"])
        eng.matmul(banks[0][:, :], strict, flat(M[:, :, :]), start=True, stop=False)
        eng.matmul(banks[0][:, :], ones, flat(cum[:, 0:NT, :]), start=False, stop=True).then_inc(ranks, 1)
        eng.matmul(banks[1][:, 0:N_EXP], ones, cum[:, NT, :], start=True, stop=True).then_inc(ranks, 1)

    def pool(eng):
        eng.iota(down[:, :], [[-1, NE]], base=NE, channel_multiplier=0, allow_small_or_imprecise_dtypes=True).then_inc(iotas, 1)
        eng.iota(region[:, :], [[SEQ, N_EXP]], base=0, channel_multiplier=0, allow_small_or_imprecise_dtypes=True).then_inc(iotas, 1)
        eng.iota(blk[:, :], [[1, N_BLOCK + 2]], base=0, channel_multiplier=0, allow_small_or_imprecise_dtypes=True).then_inc(iotas, 1)
        eng.iota(entry[:, :, :, 0], [[P, NT], [0, 2]], base=0, channel_multiplier=1).then_inc(iotas, 1)
        eng.iota(entry[:, :, :, 1], [[2 * P, NT], [1, 2]], base=0, channel_multiplier=2).then_inc(iotas, 1)
        eng.iota(entry[:, :, :, 3], [[0, NT], [0, 2]], base=0, channel_multiplier=0).then_inc(iotas, 1)
        eng.iota(fill[:, :, 2:], [[0, SLOTS // P + 2], [0, 2]], base=0, channel_multiplier=0).then_inc(fill_made, 1)
        eng.memset(zero_rows[:, :], 0.0).then_inc(fill_made, 1)
        eng.iota(fill[:, :, 0:2], [[1, SLOTS // P + 2], [0, 2]], base=0, channel_multiplier=SLOTS // P + 2).then_inc(fill_made, 1)
        eng.wait_ge(entry_ready, 1)
        eng.wait_ge(fill_in, 16 * 2)
        for t in range(NT):
            for k in range(2):
                eng.indirect_dma_start(out=env["table"][:, :], out_offset=bass.IndirectOffsetOnAxis(ap=slot[:, t, k:k + 1], axis=0),
                                       in_=entry[:, t, k, :], in_offset=None).then_inc(entries_in, 16)
        eng.wait_ge(entries_in, 16 * 2 * NT)

    def sp(eng):
        eng.wait_ge(env["fill_masked"], 2)
        eng.dma_start(env["table"].rearrange("(p j) c -> p j c", p=P), fill[:, :, :]).then_inc(fill_in, 16)
        eng.dma_start(env["h_rows"][SEQ:, :], zero_rows[:, :]).then_inc(fill_in, 16)

    def mask_fill(eng):
        eng.wait_ge(fill_made, 3)
        for word, rows in ((0, SEQ), (1, 2 * SEQ)):
            eng.tensor_scalar(fill[:, :, word], fill[:, :, word], P - 1, rows, ALU.bitwise_and, ALU.bitwise_or).then_inc(env["fill_masked"], 1)

    env["fill_masked"] = sem("r_fill_masked")

    def dve_all(eng):
        mask_fill(eng)
        dve(eng)

    return own, dict(sync=sp, tensor=pe, scalar=act, vector=dve_all, gpsimd=pool)


def expert_pass(nc, ctx, env):
    consts, banks, meta = env["consts"], env["banks"], env["meta"]
    own = ctx.enter_context(ExitStack())
    ident = consts[:, C_ID * P:(C_ID + 1) * P]
    DE = 512
    KE = DE // P
    HALF = D // 2

    def sb(name, shape, dt=F32):
        return own.enter_context(nc.sbuf_tensor(name, shape, dt))

    W = env["expert_w"]
    wg = [w[:, 0, :].rearrange("p (k n) -> p k n", k=KD) for w in W]
    wu = [w[:, 1, :].rearrange("p (k n) -> p k n", k=KD) for w in W]
    wd = [w[:, 2, :].rearrange("p (k n) -> p k n", k=KE) for w in W]
    e_far = sb("entries_far", [P, ENTRY], I32)
    e_next = sb("entries_next", [P, ENTRY], I32)
    e_mid = sb("entries_mid", [P, ENTRY], I32)
    e_cur = sb("entries_now", [P, ENTRY], I32)
    xg = sb("gathered_rows", [P, D])
    xT = sb("gathered_T", [P, KD, P])
    hg = sb("silu_gate", [P, DE])
    ha = sb("hidden", [P, DE])
    haT = sb("hidden_T", [P, KE, P])
    y = sb("expert_out", [P, D])

    bG, bU, bX, bA, bY = banks[0], banks[1], banks[2:4], [banks[4], banks[7]], banks[5:7]
    v4 = lambda b: b[:, :].rearrange("p (h n) -> p h n", h=4)
    sem = env["sem"]
    w_in = [sem(f"m_weight_halves{k}_in") for k in range(2)]
    ent_in, rows_in = Signal(sem("m_entries_in"), 16, 0), Signal(sem("m_rows_in"), 16, 0)
    stored = Signal(sem("m_y_stored"), 16, 16)
    xT_full, gu_full = Signal(sem("m_xT_full"), 2), Signal(sem("m_gate_up_full"), 2)
    hT_full, y_full = Signal(sem("m_hidden_T_full"), 2), Signal(sem("m_y_full"), 2)
    xT_a, xT_v = Signal(sem("m_xT_by_act")), Signal(sem("m_xT_by_dve"))
    silu, hid = Signal(sem("m_silu")), Signal(sem("m_hidden"))
    hT_a, hT_v = Signal(sem("m_hidden_T_by_act")), Signal(sem("m_hidden_T_by_dve"))
    y_a, y_v = Signal(sem("m_y_by_act")), Signal(sem("m_y_by_dve"))
    steps_begun = sem("m_pool_steps_begun")
    e_kept, e_moved, e_set = Signal(sem("m_entries_kept")), Signal(sem("m_entries_moved")), Signal(sem("m_entries_set"))
    ahead = dict(sync=[], tensor=[xT_full, gu_full, hT_full, y_full], scalar=[xT_a, silu, hT_a, y_a],
                 vector=[xT_v, hid, hT_v, y_v, e_kept, e_moved, e_set], gpsimd=[])
    HI = N_BLOCK

    def n_blocks(eng):
        return eng.value_load(meta[0:1, 2 * N_EXP - 1:2 * N_EXP], min_val=N_EXP, max_val=HI)

    def load_expert(eng, e, half):
        run = KD * DE // 2
        for i, src in enumerate((env["w_gate"], env["w_up"], env["w_down"])):
            part = src[bass.ds(e, 1)].rearrange("a (p k) n -> p (a k n)", p=P)
            for c in range(2):
                if not isinstance(e, int) or e > 0 or i > 0:
                    eng.wait_ge(w_in[c], e * 48 + i * 16)
                eng.dma_start(W[half][:, i, c * run:(c + 1) * run], part[:, c * run:(c + 1) * run]).then_inc(w_in[c], 16)

    def sp(eng):
        with eng.Fori(0, N_EXP // 2 - 1) as pair:
            for half in range(2):
                done = eng.value_load(meta[0:1, bass.ds(pair * 2 + (N_EXP + half), 1)], min_val=1, max_val=HI)
                y_full.after(eng, done, 0)
                load_expert(eng, pair * 2 + 2 + half, half)

    def pe(eng):
        def x_transposes(i):
            rows_in.after(eng, i)
            for half in range(2):
                (xT_a if half == 0 else xT_v).after(eng, i - 1)
                for q in range(4):
                    k = 4 * half + q
                    ins = eng.transpose(bX[half][:, q * P:(q + 1) * P], xg[:, k::KD], ident)
                ins.then_inc(xT_full.sem, 1)

        def block(i, pair, half):
            for c in range(2):
                eng.wait_ge(w_in[c], pair * 96 + half * 48 + 48)
            xT_a.after(eng, i)
            xT_v.after(eng, i)
            silu.after(eng, i - 1)
            for k in range(KD):
                ins = eng.matmul(bG[:, :], xT[:, k, :], wg[half][:, k, :], start=(k == 0), stop=(k == KD - 1))
            ins.then_inc(gu_full.sem, 1)
            hid.after(eng, i - 1)
            for k in range(KD):
                ins = eng.matmul(bU[:, :], xT[:, k, :], wu[half][:, k, :], start=(k == 0), stop=(k == KD - 1))
            ins.then_inc(gu_full.sem, 1)
            x_transposes(i + 1)
            hid.after(eng, i)
            for part, taken in enumerate((hT_v, hT_a)):
                taken.after(eng, i - 1)
                for q in range(KE // 2):
                    ins = eng.transpose(bA[part][:, q * P:(q + 1) * P], ha[:, part * (KE // 2) + q::KE], ident)
                ins.then_inc(hT_full.sem, 1)
            hT_v.after(eng, i)
            for n in range(2):
                (y_a if n == 0 else y_v).after(eng, i - 1)
                for q in range(KE):
                    if n == 0 and q == KE // 2:
                        hT_a.after(eng, i)
                    ins = eng.matmul(bY[n][:, :], haT[:, q, :], wd[half][:, q, n * HALF:(n + 1) * HALF],
                                     start=(q == 0), stop=(q == KE - 1))
                ins.then_inc(y_full.sem, 1)

        x_transposes(0)
        with eng.Fori(0, N_EXP // 2) as pair:
            for half in range(2):
                e = pair * 2 + half
                start = eng.value_load(meta[0:1, bass.ds(e, 1)], min_val=0, max_val=HI)
                end = eng.value_load(meta[0:1, bass.ds(e + N_EXP, 1)], min_val=1, max_val=HI)
                with eng.Fori(start, end) as i:
                    block(i, pair, half)

    def act(eng):
        def take_x(i):
            xT_full.after(eng, i, 1)
            gu_full.after(eng, i - 1)
            eng.activation(xT[:, 0:4, :], v4(bX[0]), ACT.Copy).then_inc(xT_a.sem, 1)

        eng.preload_act_table_set(SILU)
        take_x(0)
        with eng.Fori(0, n_blocks(eng)) as i:
            gu_full.after(eng, i, 1)
            hid.after(eng, i - 1)
            eng.activation(hg[:, :], bG[:, :], ACT.Silu).then_inc(silu.sem, 1)
            take_x(i + 1)
            hT_full.after(eng, i)
            y_full.after(eng, i - 1)
            eng.activation(haT[:, 2:4, :], bA[1][:, 0:2 * P].rearrange("p (h n) -> p h n", h=2), ACT.Copy).then_inc(hT_a.sem, 1)
            y_full.after(eng, i, 1)
            e_set.after(eng, i)
            stored.after(eng, i - 1)
            eng.activation(y[:, 0:HALF], bY[0][:, :], ACT.Identity, scale=e_cur[:, 2:3].bitcast(F32)).then_inc(y_a.sem, 1)

    def dve(eng):
        def take_x(i):
            xT_full.after(eng, i)
            gu_full.after(eng, i - 1)
            eng.tensor_copy(xT[:, 4:8, :], v4(bX[1])).then_inc(xT_v.sem, 1)

        def move(i):
            ent_in.after(eng, i)
            eng.tensor_copy(e_next[:, :], e_far[:, :]).then_inc(e_moved.sem, 1)

        move(0)
        take_x(0)
        with eng.Fori(0, n_blocks(eng)) as i:
            e_set.after(eng, i - 1)
            e_moved.after(eng, i)
            eng.tensor_copy(e_mid[:, :], e_next[:, :]).then_inc(e_kept.sem, 1)
            e_kept.after(eng, i)
            move(i + 1)
            silu.after(eng, i)
            hT_full.after(eng, i - 1)
            gu_full.after(eng, i)
            eng.tensor_tensor(ha[:, :], hg[:, :], bU[:, :], ALU.mult).then_inc(hid.sem, 1)
            hT_full.after(eng, i, 1)
            y_full.after(eng, i - 1)
            eng.tensor_copy(haT[:, 0:2, :], bA[0][:, 0:2 * P].rearrange("p (h n) -> p h n", h=2)).then_inc(hT_v.sem, 1)
            stored.after(eng, i - 1)
            y_a.after(eng, i - 1)
            e_kept.after(eng, i)
            eng.tensor_copy(e_cur[:, :], e_mid[:, :]).then_inc(e_set.sem, 1)
            take_x(i + 1)
            y_full.after(eng, i)
            e_set.after(eng, i)
            eng.tensor_scalar(y[:, HALF:], bY[1][:, :], e_cur[:, 2:3].bitcast(F32), None, ALU.mult).then_inc(y_v.sem, 1)

    def pool(eng):
        def settle():
            eng.sem_inc(steps_begun, 1)

        def entries(slot):
            eng.dma_start(e_far[:, :], env["table"][bass.ds(slot, P), :]).then_inc(ent_in.sem, 16)

        def gather(i):
            e_moved.after(eng, i)
            settle()
            eng.indirect_dma_start(out=xg[:, :], out_offset=None, in_=env["h_rows"][:, :],
                                   in_offset=bass.IndirectOffsetOnAxis(ap=e_next[:, 0:1].bitcast(U32), axis=0)).then_inc(rows_in.sem, 16)

        def slot_of(i):
            return eng.value_load(meta[0:1, bass.ds(i + 2 * N_EXP, 1)], min_val=0, max_val=SLOTS + P)

        eng.dma_start(e_cur[:, :], env["table"][SLOTS:SLOTS + P, :]).then_inc(stored.sem, 16)
        entries(0)
        gather(0)
        entries(slot_of(1))
        with eng.Fori(0, n_blocks(eng)) as i:
            xT_full.after(eng, i)
            gather(i + 1)
            entries(slot_of(i + 2))
            y_a.after(eng, i)
            y_v.after(eng, i)
            settle()
            eng.indirect_dma_start(out=env["y_rows"][:, :], out_offset=bass.IndirectOffsetOnAxis(ap=e_cur[:, 1:2].bitcast(U32), axis=0),
                                   in_=y[:, :], in_offset=None).then_inc(stored.sem, 16)
        stored.after(eng, n_blocks(eng) - 1)
        settle()

    def started(name, program):
        def run(eng):
            for s in ahead[name]:
                eng.sem_inc(s.sem, 1)
            program(eng)
        return run

    def first_experts(eng):
        load_expert(eng, 0, 0)
        load_expert(eng, 1, 1)

    env["first_experts"] = first_experts
    programs = dict(sync=sp, tensor=pe, scalar=act, vector=dve, gpsimd=pool)
    return own, {name: started(name, program) for name, program in programs.items()}


def final_pass(nc, ctx, env):
    own = ctx.enter_context(ExitStack())
    F, BUF = 2, 3
    NF = NT // F

    def sb(name, shape, dt=F32):
        return own.enter_context(nc.sbuf_tensor(name, shape, dt))

    nfin = sb("norm_final_rows", [P, D])
    xf = [sb(f"final_x{k}", [P, F, D]) for k in range(BUF)]
    yf = [sb(f"final_y{k}", [P, F, 2, D]) for k in range(BUF)]
    junk = sb("final_junk", [P, D])
    ss = [sb(f"final_sumsq{k}", [P, F]) for k in range(BUF)]
    sem = env["sem"]
    w_in = sem("f_weight_in")
    x_in = [sem(f"f_x_in{k}") for k in range(BUF)]
    out = [sem(f"f_out{k}") for k in range(BUF)]
    sq, ln, rs = sem("f_sq"), sem("f_ln"), sem("f_rstd")
    pair, total, nrm = sem("f_pair_sums"), sem("f_sums"), sem("f_normed")

    def rows(dram, n):
        return dram[n * F * P:(n + 1) * F * P, :].rearrange("(j p) d -> p j d", p=P)

    def sp(eng):
        def load(n):
            if n >= BUF:
                eng.wait_ge(out[n % BUF], 16 * (n // BUF))
            eng.dma_start(xf[n % BUF][:, :, :], rows(env["x_rows"], n)).then_inc(x_in[n % BUF], 16)
            pairs = env["y_rows"][2 * n * F * P:2 * (n + 1) * F * P, :]
            eng.dma_start(yf[n % BUF][:, :, :, :].rearrange("p j c d -> p j (c d)"),
                          pairs.rearrange("(j p c) d -> p j (c d)", p=P, c=2)).then_inc(x_in[n % BUF], 16)

        eng.dma_start(nfin[:, :], env["norm_final"].partition_broadcast(P)).then_inc(w_in, 16)
        for n in range(BUF - 1):
            load(n)
        for n in range(NF):
            if n + BUF - 1 < NF:
                load(n + BUF - 1)
            eng.wait_ge(nrm, F * (n + 1))
            eng.dma_start(rows(env["out"], n), xf[n % BUF][:, :, :]).then_inc(out[n % BUF], 16)
        for k in range(BUF):
            eng.wait_ge(out[k], 16 * len(range(k, NF, BUF)))

    def act(eng):
        eng.preload_act_table_set(EXP_LN)
        for n in range(NF):
            b = n % BUF
            if n >= BUF:
                eng.wait_ge(nrm, F * (n - BUF + 1))
            for j in range(F):
                eng.wait_ge(total, F * n + j + 1)
                if n or j:
                    eng.wait_ge(sq, F * n + j)
                eng.activation(junk[:, :], xf[b][:, j, :], ACT.Square, accum_out=ss[b][:, j:j + 1]).then_inc(sq, 1)
            eng.wait_ge(sq, F * (n + 1))
            eng.activation(ss[b][:, :], ss[b][:, :], ACT.Ln, bias=env["eps"][:, 0:1], scale=1.0 / D).then_inc(ln, 1)
            eng.wait_ge(ln, n + 1)
            eng.activation(ss[b][:, :], ss[b][:, :], ACT.Exp, scale=-0.5).then_inc(rs, 1)

    def dve(eng):
        def add(n):
            b = n % BUF
            eng.wait_ge(x_in[b], 32 * (n // BUF + 1))
            for j in range(F):
                eng.tensor_tensor(yf[b][:, j, 0, :], yf[b][:, j, 0, :], yf[b][:, j, 1, :], ALU.add).then_inc(pair, 1)
            for j in range(F):
                eng.wait_ge(pair, F * n + j + 1)
                eng.tensor_tensor(xf[b][:, j, :], xf[b][:, j, :], yf[b][:, j, 0, :], ALU.add).then_inc(total, 1)

        def norm(n):
            b = n % BUF
            eng.wait_ge(rs, n + 1)
            for j in range(F):
                eng.scalar_tensor_tensor(out=xf[b][:, j, :], in0=xf[b][:, j, :], scalar=ss[b][:, j:j + 1],
                                         in1=nfin[:, :], op0=ALU.mult, op1=ALU.mult).then_inc(nrm, 1)

        eng.wait_ge(w_in, 16)
        add(0)
        for n in range(NF):
            if n + 1 < NF:
                add(n + 1)
            norm(n)

    idle = lambda eng: None
    return own, dict(sync=sp, tensor=idle, scalar=act, vector=dve, gpsimd=idle)


def build(nc, t):
    with ExitStack() as ctx:
        count = [0]

        def sem(name):
            count[0] += 1
            return ctx.enter_context(nc.semaphore(name))

        env = dict(t)
        env["sem"] = sem
        env["consts"] = ctx.enter_context(nc.sbuf_tensor("consts", [P, N_CONST * P], F32))
        env["eps"] = ctx.enter_context(nc.sbuf_tensor("eps", [P, 1], F32))
        env["banks"] = [ctx.enter_context(nc.psum_tensor(f"bank{i}", [P, 512], F32)) for i in range(8)]
        env["consts_in"] = sem("consts_in")
        env["eps_in"] = sem("eps_in")
        env["g_hist0"] = sem("p2_history_of_first")
        env["logits"] = ctx.enter_context(nc.sbuf_tensor("logits", [P, NT, N_LOGIT], F32))
        env["meta"] = ctx.enter_context(nc.sbuf_tensor("block_table", [P, 2 * N_EXP + N_BLOCK + 2], I32))
        over = [sem(f"pass{n}_over") for n in range(1, 5)]
        block = ctx.enter_context(nc.Block())
        passes = []
        own, programs = deltanet_pass(nc, ctx, env)
        passes.append(programs)
        own.close()
        own, programs = conformer_pass(nc, ctx, env)
        passes.append(programs)
        own.close()
        weights = ctx.enter_context(ExitStack())
        env["expert_w"] = [weights.enter_context(nc.sbuf_tensor(f"expert_w{k}", [P, 3, KD * 512], F32)) for k in range(2)]
        own, programs = router_pass(nc, ctx, env)
        passes.append(programs)
        own.close()
        own, programs = expert_pass(nc, ctx, env)
        passes.append(programs)
        own.close()
        weights.close()
        own, programs = final_pass(nc, ctx, env)
        passes.append(programs)

        def meet(eng, n):
            eng.drain()
            eng.sem_inc(over[n - 1], 1)
            eng.wait_ge(over[n - 1], 5)

        @block.vector
        def _(eng):
            eng.wait_ge(env["consts_in"], 16)
            passes[0]["vector"](eng)
            meet(eng, 1)
            passes[1]["vector"](eng)
            meet(eng, 2)
            passes[2]["vector"](eng)
            meet(eng, 3)
            eng.wait_ge(env["meta_in"], 1)
            passes[3]["vector"](eng)
            meet(eng, 4)
            passes[4]["vector"](eng)

        @block.sync
        def _(eng):
            eng.dma_start(env["consts"][:, :], t["shape_consts"]).then_inc(env["consts_in"], 16)
            passes[0]["sync"](eng)
            env["p1_done"].after(eng, NG - 1)
            meet(eng, 1)
            passes[1]["sync"](eng)
            env["x2_out"].after(eng, NG - 1)
            env["h2_out"].after(eng, NG - 1)
            meet(eng, 2)
            passes[2]["sync"](eng)
            env["first_experts"](eng)
            meet(eng, 3)
            eng.wait_ge(env["meta_in"], 1)
            passes[3]["sync"](eng)
            meet(eng, 4)
            passes[4]["sync"](eng)

        @block.gpsimd
        def _(eng):
            eng.memset(env["eps"][:, :], EPS).then_inc(env["eps_in"], 1)
            eng.wait_ge(env["consts_in"], 16)
            passes[0]["gpsimd"](eng)
            meet(eng, 1)
            meet(eng, 2)
            passes[2]["gpsimd"](eng)
            meet(eng, 3)
            eng.wait_ge(env["meta_in"], 1)
            passes[3]["gpsimd"](eng)
            meet(eng, 4)

        @block.scalar
        def _(eng):
            passes[0]["scalar"](eng)
            meet(eng, 1)
            passes[1]["scalar"](eng)
            meet(eng, 2)
            passes[2]["scalar"](eng)
            meet(eng, 3)
            eng.wait_ge(env["meta_in"], 1)
            passes[3]["scalar"](eng)
            meet(eng, 4)
            passes[4]["scalar"](eng)

        @block.tensor
        def _(eng):
            passes[0]["tensor"](eng)
            meet(eng, 1)
            passes[1]["tensor"](eng)
            meet(eng, 2)
            passes[2]["tensor"](eng)
            meet(eng, 3)
            eng.wait_ge(env["meta_in"], 1)
            passes[3]["tensor"](eng)
            meet(eng, 4)


def kernel(**inputs):
    import numpy as _np
    import concourse.bacc as _bacc
    from concourse import mybir as _mybir
    from concourse.bass_utils import run_bass_kernel_spmd as _run

    nc = _bacc.Bacc("TRN2", target_bir_lowering=False, num_devices=1)
    n = _np.arange(P)
    row, col = n[:, None], n[None, :]
    parts = [row == col, row <= col, row < col, row >= 0 * col]
    for l in range(LEVELS):
        parts.append((row > col) & ((row ^ col) >> l == 1))
    shape_consts = _np.concatenate([m.astype(_np.float32) for m in parts], axis=1)
    arrays = {"shape_consts": shape_consts}
    for name, a in inputs.items():
        a = _np.asarray(a)
        arrays[name] = _np.ascontiguousarray(a.reshape(a.shape[1:]) if a.ndim > 1 and a.shape[0] == 1 else a)
    arrays["conv_qkv"] = _np.ascontiguousarray(arrays["conv_qkv"].reshape(4, 12, 128).transpose(2, 0, 1))
    arrays["w_dw"] = _np.ascontiguousarray(arrays["w_dw"].reshape(CONF_TAPS, 4, 128).transpose(2, 0, 1))
    arrays["cf_cols"] = _np.ascontiguousarray(
        _np.stack([arrays.pop(n).reshape(4, 128) for n in ("b_dw", "ln_g", "ln_b")]).transpose(2, 0, 1))
    arrays["w_router"] = _np.concatenate([arrays.pop("w_rg"), arrays.pop("w_re")], axis=1)
    arrays["b_router"] = _np.concatenate([arrays.pop("b_rg"), arrays.pop("b_re")])
    t = {}
    for name, a in arrays.items():
        t[name] = nc.dram_tensor(f"in_{name}", a.shape, _mybir.dt.from_np(a.dtype), kind="ExternalInput").ap()
    t["conv_qkvT"] = t["conv_qkv"]
    t["y_dnT"] = nc.dram_tensor("y_dnT", (DN, SEQ), F32).ap()
    out = nc.dram_tensor("out", (SEQ, D), F32, kind="ExternalOutput").ap()
    t["h_rows"] = nc.dram_tensor("h_rows", (SEQ + P, D), F32).ap()
    t["x_rows"] = nc.dram_tensor("x_rows", (SEQ, D), F32).ap()
    t["y_rows"] = nc.dram_tensor("y_rows", (2 * SEQ + P, D), F32).ap()
    t["table"] = nc.dram_tensor("slot_table", (SLOTS + 2 * P, ENTRY), I32).ap()
    t["out"] = out
    build(nc, t)
    r = _run(nc, [{f"in_{k}": v for k, v in arrays.items()}], core_ids=[0])
    return r.results[0]["out"].reshape(1, SEQ, D)
```

```python
from contextlib import ExitStack

import concourse.bass as bass
from concourse import mybir

F32 = mybir.dt.float32
I32 = mybir.dt.int32
U32 = mybir.dt.uint32
ACT = mybir.ActivationFunctionType
ALU = mybir.AluOpType
AX = mybir.AxisListType

P = 128
D = 1024
SEQ = 2048
KD = D // P
H = 4
DN = H * P
CF = D - DN
DN_COLS = 4 * DN + 2 * H
SHORT = 4
G_TOK = 256
NG = SEQ // G_TOK
NT = SEQ // P
LEVELS = 7
EPS = 1e-6
EXP_LN = "natural_log_exp_and_others"
SILU = "silu_and_others"
SIGMOID = "sigmoid_and_others"
CONF_TAPS = 31
N_GROUPS = 4
EXP_PER_GROUP = 8
N_EXP = N_GROUPS * EXP_PER_GROUP
N_LOGIT = N_GROUPS + N_EXP

C_ID, C_TRI, C_STRICT, C_ONES, C_LVL = 0, 1, 2, 3, 4
N_CONST = 4 + LEVELS


class Signal:

    def __init__(self, sem, per=1, lead=1):
        self.sem, self.per, self.lead = sem, per, lead

    def after(self, eng, rnd, k=None):
        k = self.per if k is None else k
        eng.wait_ge(self.sem, rnd * self.per + k + self.lead)


def bcast(ap, n):
    return ap.unsqueeze(len(ap.shape)).to_broadcast([*ap.shape, n])


def mid(ap, n):
    return ap.unsqueeze(1).to_broadcast([ap.shape[0], n, ap.shape[1]])


def deltanet_pass(nc, ctx, env):
    x, w_in, y_dnT = env["x"], env["w_in"], env["y_dnT"]
    consts, banks = env["consts"], env["banks"]
    own = ctx.enter_context(ExitStack())

    def sb(name, shape, dt=F32):
        return own.enter_context(nc.sbuf_tensor(name, shape, dt))

    def const(c):
        return consts[:, c * P:(c + 1) * P]

    ident, tri, ones = const(C_ID), const(C_TRI), const(C_ONES)

    w_sb = env["weights"][:, :].rearrange("p (k c) -> p k c", k=KD)
    nm_bc, xt = env["norm_mix_rows"], env["x_group"]
    convw = sb("conv_taps", [P, SHORT, 12])
    onorm = sb("o_norm_col", [P, 1])
    dtb = sb("dt_bias_rows", [P, H])
    nega = sb("neg_a_rows", [P, H])
    eps = env["eps"]
    junk = sb("square_junk", [P, D])
    ez = junk[:, :].rearrange("p (j n) -> p j n", j=2)
    xss = sb("x_sumsq", [P, 2])
    xr = sb("x_rstd", [P, 2])
    hT = sb("hT", [P, KD, G_TOK])
    U = sb("u_raw", [P, 12, G_TOK + SHORT - 1])
    QKV = [sb(f"qkv{i}", [P, 12, G_TOK]) for i in range(2)]
    ZS = [sb(f"silu_z{i}", [P, 2, DN]) for i in range(2)]
    ba = sb("ba_raw", [P, 2, 8])
    ga = sb("gate_tmp", [P, 3, 2, H])
    ge = sb("gate_exp", [P, 3, 2, H])
    beta = [sb(f"beta{i}", [P, 2, H]) for i in range(2)]
    gt = [sb(f"log_decay{i}", [P, 2, H]) for i in range(2)]
    sq = sb("qk_squares", [P, 8, P])
    rn = sb("qk_rnorm", [P, 8])
    vec = sb("decay_logs", [P, 12])
    evec = sb("decays", [P, 12])
    fac = sb("row_factors", [P, 4, H])
    Dl = sb("decay_lower", [P, H, P])
    Du = sb("decay_upper", [P, H, P])
    A = sb("a_mat", [P, H, P])
    Aoff = [sb(f"a_level{l}", [P, H, P]) for l in range(LEVELS)]
    M = sb("inverseT", [P, H, P])
    T_ = sb("inverse", [P, H, P])
    X = {l: sb(f"x_level{l}", [P, H, P]) for l in range(1, LEVELS - 1)}
    X_last = sb("x_last_level", [P, H * P // 2])
    QKd = sb("qk_decayed", [P, H, P])
    ktok = sb("k_rows", [P, H, P])
    vb = sb("v_scaled", [P, H, P])
    R = sb("solve_rhs", [P, H, P])
    S = sb("state", [P, H, P])
    vh = sb("v_new", [P, H, P])
    vd = sb("v_new_decayed", [P, H, P])
    o = sb("o_rows", [P, H, P])
    osq = sb("o_squares", [P, H, P])
    oss = sb("o_sumsq", [P, H])
    ors = sb("o_rstd", [P, H])
    Y = [sb(f"y_rows{i}", [P, H, P]) for i in range(2)]
    yT = sb("y_columns", [P, H, G_TOK])

    v4 = lambda b: b[:, :].rearrange("p (h n) -> p h n", h=H)

    def half_cols(t, h, l, second):
        return t[:, h, :].rearrange("p (b two s) -> p b two s", two=2, s=1 << l)[:, :, second, :]

    def half_all(t, l, second):
        return t[:, :, :].rearrange("p h (b two s) -> p (h b) two s", two=2, s=1 << l)[:, :, second, :]

    def packed(bank, l):
        return bank[:, 0:H * P // 2].rearrange("p (a s) -> p a s", s=1 << l)

    def packed_head(t, h):
        return t[:, h * P // 2:(h + 1) * P // 2]

    ring = banks[0:2]
    bS = banks[2]
    bX, bM, bT = banks[3:6]
    B0, B1, B2, B3, B4 = [v4(b) for b in banks[3:8]]

    sem = env["sem"]
    PIECES = [(4 * DN, DN_COLS)] + [(n * DN, (n + 1) * DN) for n in range(4)]
    weights_in = [sem(f"p1_weights_in{n}") for n in range(len(PIECES))]
    params_in = sem("p1_params_in")
    x_in = Signal(sem("p1_x_in"), 16)
    y_out = Signal(sem("p1_y_out"), 16)
    once = sem("p1_once")
    bank_full = sem("p1_bank_full")
    bank_taken = sem("p1_bank_taken")
    x_sq = Signal(sem("p1_x_squared"), 2)
    x_ln = Signal(sem("p1_x_ln"))
    x_rs = Signal(sem("p1_x_rstd"))
    x_nrm = Signal(sem("p1_x_normed"), 2)
    conv = Signal(sem("p1_conv"), 6 * 8)
    hist = Signal(sem("p1_history"))
    gate_a = Signal(sem("p1_gate_logits"), 3)
    gate_e = Signal(sem("p1_gate_exps"), 3)
    gate_g = Signal(sem("p1_gates"), 4)
    silu_done = Signal(sem("p1_silu"))
    z_exp = Signal(sem("p1_z_exp"))
    z_silu = Signal(sem("p1_z_silu"), 3)
    squares = Signal(sem("p1_squares"))
    scal_full = Signal(sem("p1_scal_full"))
    gcrow_full = Signal(sem("p1_gcrow_full"))
    gram_full = Signal(sem("p1_gram_full"))
    tok_full = Signal(sem("p1_tok_full"), 2)
    a0T_full = Signal(sem("p1_a0T_full"))
    x_full = Signal(sem("p1_xlevel_full"), 6)
    d_full = Signal(sem("p1_delta_full"), 11)
    ks_full = Signal(sem("p1_ks_full"), 2)
    vhat_full = Signal(sem("p1_vhat_full"))
    o2_full = Signal(sem("p1_o2_full"))
    ds_full = Signal(sem("p1_ds_full"))
    r_ln = Signal(sem("p1_rnorm_ln"))
    r_exp = Signal(sem("p1_rnorm"))
    dec_e = Signal(sem("p1_decays"))
    d_exp = Signal(sem("p1_decay_mats"), 2)
    ktok_in = Signal(sem("p1_ktok"))
    x_copied = Signal(sem("p1_xlevel_copied"), 6)
    vh_in = Signal(sem("p1_vnew"))
    o_sq = Signal(sem("p1_o_squared"))
    o_ln = Signal(sem("p1_o_ln"))
    o_rs = Signal(sem("p1_o_rstd"))
    vec_in = Signal(sem("p1_vec"), 2)
    facs = Signal(sem("p1_factors"), 4)
    difs = Signal(sem("p1_differences"), 3)
    a_mat = Signal(sem("p1_a_mat"), 2)
    qk_d = Signal(sem("p1_qk_decayed"))
    vb_in = Signal(sem("p1_v_scaled"))
    inv = Signal(sem("p1_inverse"), 13)
    rhs = Signal(sem("p1_rhs"), 2)
    o_q = Signal(sem("p1_o_state"))
    vd_in = Signal(sem("p1_vnew_decayed"))
    st_dec = Signal(sem("p1_state_decayed"))
    state = Signal(sem("p1_state"))
    o_sum = Signal(sem("p1_o_sum"), 2)
    o_red = Signal(sem("p1_o_reduced"))
    y_rows = Signal(sem("p1_y_rows"), 2)
    du_mask = Signal(sem("p1_upper_masked"))
    a_lvl = Signal(sem("p1_a_levels"), LEVELS)
    ahead = dict(
        sync=[x_in, y_out],
        tensor=[bank_full, scal_full, gcrow_full, gram_full, tok_full, a0T_full, x_full, d_full, ks_full, vhat_full,
                o2_full, ds_full],
        scalar=[bank_taken, x_sq, x_ln, x_rs, gate_e, silu_done, z_exp, squares, r_ln, r_exp, dec_e, d_exp, ktok_in, x_copied,
                vh_in, o_sq, o_ln, o_rs],
        vector=[x_nrm, conv, hist, gate_a, gate_g, z_silu, vec_in, facs, difs, a_mat, qk_d, vb_in, inv, rhs, o_q, vd_in, st_dec,
                state, o_sum, o_red, y_rows],
        gpsimd=[du_mask, a_lvl])
    env["p1_done"] = y_out

    def units(g):
        order = []
        if g < NG - 1:
            order += [f"h{n}" for n in range(4)]
        if g > 0:
            order += ["y1"]
        if g < NG - 1:
            order += ["ba"] + [f"c{b}" for b in range(6)]
        if g >= 0:
            order += ["y0"]
        if g < NG - 1:
            order += ["z0", "z1"]
        return {name: n for n, name in enumerate(order)}

    U_ITER = len(units(1))
    U_FIRST = len(units(-1)) + len(units(0))
    ONCE = 1 + 2 + LEVELS - 2

    class Iter:

        def __init__(self, g, like):
            self.g, self.p = g, like % 2
            self.chain, self.fill, self.norm, self.y_before = like >= 0, like < NG - 1, like < NG - 1, like > 0
            self.u = units(like)
            if like > 0:
                self.base = g * U_ITER + (U_FIRST - U_ITER)
                self.bp = (like * U_ITER + U_FIRST - U_ITER) % 2
            else:
                self.base = self.bp = 0 if like < 0 else len(units(-1))

        def bank(self, name):
            return ring[(self.bp + self.u[name]) % 2]

        def open_bank(self, eng, name):
            n = self.base + self.u[name]
            if isinstance(n, int) and n < 2:
                return
            eng.wait_ge(bank_taken, n - 1 + 1)

        def full(self, eng, name):
            eng.wait_ge(bank_full, self.base + self.u[name] + 1 + 1)

        def taken(self, eng, name):
            eng.wait_ge(bank_taken, self.base + self.u[name] + 1 + 1)

    last = Iter(NG - 1, NG - 1)
    last.base, last.bp, last.u = last.base + len(last.u), (last.bp + len(last.u)) % 2, {"y1": 0}

    def over_groups(eng, body):
        body(Iter(-1, -1))
        body(Iter(0, 0))
        with eng.Fori(0, (NG - 4) // 2) as i:
            body(Iter(i * 2 + 1, 1))
            body(Iter(i * 2 + 2, 2))
        for g in range(NG - 3, NG):
            body(Iter(g, g))

    def tok(g, j=0, n=G_TOK):
        return bass.ds(g * G_TOK + j * P, n)

    def sp(eng):
        eng.dma_start(nm_bc[:, :], env["norm_mix"].partition_broadcast(P)).then_inc(params_in, 16)
        eng.dma_start(convw[:, :, :], env["conv_qkvT"]).then_inc(params_in, 16)
        eng.dma_start(onorm[:, :], env["o_norm"].rearrange("(p a) -> p a", a=1)).then_inc(params_in, 16)
        eng.dma_start(dtb[:, :], env["dt_bias"].partition_broadcast(P)).then_inc(params_in, 16)
        eng.dma_start(nega[:, :], env["a_log"].partition_broadcast(P)).then_inc(params_in, 16)

        def load_x(g):
            eng.dma_start(xt[:, :, :], x[tok(0 if isinstance(g, int) and g == NG else g), :]
                          .rearrange("(j p) d -> p j d", p=P)).then_inc(x_in.sem, 16)

        load_x(0)
        for piece, (lo, hi) in enumerate(PIECES):
            eng.dma_start(w_sb[:, :, lo:hi], w_in[:, lo:hi].rearrange("(k p) c -> p k c", p=P)).then_inc(weights_in[piece], 16)

        def body(it):
            if it.norm:
                it.full(eng, "h3")
                load_x(it.g + 2)
            if not it.fill:
                eng.wait_ge(bank_full, it.base + 1)
                for k in range(KD):
                    eng.dma_start(env["w_cf"][:, k, :], w_in[k * P:(k + 1) * P, DN_COLS:]).then_inc(env["w_cf_in"], 16)
                for k in range(KD):
                    eng.dma_start(env["w_o"][:, k, :], env["w_out"][k * P:(k + 1) * P, :]).then_inc(env["w_o_in"], 16)
            if it.y_before:
                it.taken(eng, "y1")
                store_y(it.g - 1)

        def store_y(g):
            eng.dma_start(y_dnT[:, tok(g)].rearrange("(h p) t -> p h t", p=P), yT[:, :, :]).then_inc(y_out.sem, 16)

        over_groups(eng, body)
        last.taken(eng, "y1")
        store_y(NG - 1)

    def pe(eng):
        def transposes(it):
            for n in range(4):
                j, half = n // 2, n % 2
                it.open_bank(eng, f"h{n}")
                if half == 0:
                    x_nrm.after(eng, it.g + 1, j + 1)
                for q in range(4):
                    k = half * 4 + q
                    ins = eng.transpose(it.bank(f"h{n}")[:, q * P:(q + 1) * P], xt[:, j, k * P:(k + 1) * P], ident)
                ins.then_inc(bank_full, 1)

        def quarters(it):
            it.taken(eng, "h3")
            it.open_bank(eng, "ba")
            first = not it.chain
            if first:
                eng.wait_ge(weights_in[0], 16)
            dst = it.bank("ba")
            for j in range(2):
                for k in range(KD):
                    ins = eng.matmul(dst[:, j * 8:j * 8 + 8], hT[:, k, j * P:(j + 1) * P],
                                     w_sb[:, k, 4 * DN:DN_COLS], start=(k == 0), stop=(k == KD - 1))
            ins.then_inc(bank_full, 1)
            yield
            for b in range(6):
                it.open_bank(eng, f"c{b}")
                if first and b % 2 == 0:
                    eng.wait_ge(weights_in[1 + b // 2], 16)
                dst = it.bank(f"c{b}")
                for q in range(4):
                    c = 2 * b + q // 2
                    for k in range(4 * (q % 2), 4 * (q % 2) + 4):
                        ins = eng.matmul(dst[:, (q // 2) * G_TOK:(q // 2 + 1) * G_TOK],
                                         w_sb[:, k, c * P:(c + 1) * P], hT[:, k, :],
                                         start=(k == 0), stop=(k == KD - 1))
                    if q == 3:
                        ins.then_inc(bank_full, 1)
                    yield
            for j in range(2):
                it.open_bank(eng, f"z{j}")
                if first and j == 0:
                    eng.wait_ge(weights_in[4], 16)
                dst = it.bank(f"z{j}")
                for q in range(4):
                    for k in (2 * q, 2 * q + 1):
                        ins = eng.matmul(dst[:, :], hT[:, k, j * P:(j + 1) * P], w_sb[:, k, 3 * DN:4 * DN],
                                         start=(k == 0), stop=(k == KD - 1))
                    if q == 3:
                        ins.then_inc(bank_full, 1)
                    yield

        def y_transpose(it, g, j):
            it.open_bank(eng, f"y{j}")
            y_rows.after(eng, g * 2 + j)
            for h in range(H):
                ins = eng.transpose(it.bank(f"y{j}")[:, h * P:(h + 1) * P], Y[j][:, h, :], ident)
            ins.then_inc(bank_full, 1)

        def tile(it, j, fill):
            g, q = it.g, QKV[it.p]
            T = g * 2 + j
            sl = slice(j * P, (j + 1) * P)
            qT = [q[:, h, sl] for h in range(H)]
            kT = [q[:, H + h, sl] for h in range(H)]
            vT = [q[:, 2 * H + h, sl] for h in range(H)]
            squares.after(eng, T)
            gate_g.after(eng, g)
            r_ln.after(eng, T - 1)
            vec_in.after(eng, T - 1)
            for c in range(8):
                eng.matmul(bS[:, c:c + 1], sq[:, c, :], ones[:, 0:1], start=True, stop=True)
            eng.matmul(bS[:, 8:12], tri, gt[it.p][:, j, :], start=True, stop=True)
            eng.matmul(bS[:, 12:16], ones, gt[it.p][:, j, :], start=True, stop=True).then_inc(scal_full.sem, 1)
            o_sum.after(eng, T - 1)
            for h in range(H):
                ins = eng.matmul(B0[:, h, :], gt[it.p][:, j, h:h + 1].to_broadcast([P, P]), tri, start=True, stop=True)
            ins.then_inc(gcrow_full.sem, 1)
            state.after(eng, T - 1)
            for h in range(H):
                eng.matmul(B1[:, h, :], kT[h], kT[h], start=True, stop=True)
            for h in range(H):
                ins = eng.matmul(B2[:, h, :], kT[h], qT[h], start=True, stop=True)
            ins.then_inc(gram_full.sem, 1)
            for h in range(H):
                ins = eng.transpose(B3[:, h, :], kT[h], ident)
            ins.then_inc(tok_full.sem, 1)
            for h in range(H):
                ins = eng.transpose(B4[:, h, :], vT[h], ident)
            ins.then_inc(tok_full.sem, 1)
            if j == 0 and it.fill:
                transposes(it)
            if j == 0 and it.y_before:
                y_transpose(it, g - 1, 1)
            fill()
            fill()
            a_lvl.after(eng, T, 1)
            difs.after(eng, T, 1)
            for h in range(H):
                ins = eng.matmul(B0[:, h, :], Aoff[0][:, h, :], ident, start=True, stop=True)
            ins.then_inc(a0T_full.sem, 1)
            fill()
            for l in range(1, LEVELS):
                a_lvl.after(eng, T, l + 1)
                inv.after(eng, T, 2 * l)
                if l > 1:
                    x_copied.after(eng, T, l - 1)
                for h in range(H):
                    ins = eng.matmul(packed_head(bX, h), Aoff[l][:, h, :], half_cols(M, h, l, 1), start=True, stop=True)
                ins.then_inc(x_full.sem, 1)
                if l == 1:
                    ktok_in.after(eng, T)
                    vb_in.after(eng, T)
                    for h in range(H):
                        ins = eng.matmul(B3[:, h, :], kT[h], S[:, h, :], start=True, stop=True)
                    ins.then_inc(ks_full.sem, 1)
                    for h in range(H):
                        ins = eng.matmul(B4[:, h, :], qT[h], S[:, h, :], start=True, stop=True)
                    ins.then_inc(ks_full.sem, 1)
                    a_mat.after(eng, T)
                    qk_d.after(eng, T)
                fill()
                if j == 1 and l == 3:
                    y_transpose(it, g, 0)
                x_copied.after(eng, T, l)
                for h in range(H):
                    x_cols = half_cols(X[l], h, l, 1) if l < LEVELS - 1 else packed_head(X_last, h)
                    ins = eng.matmul(packed_head(bM, h), T_[:, h, :], x_cols, start=True, stop=True)
                ins.then_inc(d_full.sem, 1)
                if l < LEVELS - 1:
                    for h in range(H):
                        ins = eng.matmul(packed_head(bT, h), X[l][:, h, :], half_cols(T_, h, l, 0), start=True, stop=True)
                    ins.then_inc(d_full.sem, 1)
                fill()
            inv.after(eng, T)
            rhs.after(eng, T)
            for h in range(H):
                ins = eng.matmul(B3[:, h, :], M[:, h, :], R[:, h, :], start=True, stop=True)
            ins.then_inc(vhat_full.sem, 1)
            fill()
            vh_in.after(eng, T)
            for h in range(H):
                ins = eng.matmul(B0[:, h, :], QKd[:, h, :], vh[:, h, :], start=True, stop=True)
            ins.then_inc(o2_full.sem, 1)
            vd_in.after(eng, T)
            for h in range(H):
                ins = eng.matmul(B1[:, h, :], ktok[:, h, :], vd[:, h, :], start=True, stop=True)
            ins.then_inc(ds_full.sem, 1)
            if j == 0:
                fill()

        def body(it):
            quarter = quarters(it) if it.fill else iter(())
            fill = lambda: next(quarter, None)
            if it.chain:
                silu_done.after(eng, it.g)
                tile(it, 0, fill)
                tile(it, 1, fill)
            else:
                transposes(it)
            for _ in quarter:
                pass

        eng.wait_ge(env["consts_in"], 16)
        eng.wait_ge(once, ONCE)
        over_groups(eng, body)
        y_transpose(last, NG - 1, 1)

    def act(eng):
        def norm(group):
            eng.wait_ge(x_in.sem, group * 16 + 16 + 1)
            if not isinstance(group, int) or group > 1:
                z_silu.after(eng, group - 2)
            for j in range(2):
                x_sq.after(eng, group, j)
                eng.activation(junk[:, :], xt[:, j, :], ACT.Square, accum_out=xss[:, j:j + 1]).then_inc(x_sq.sem, 1)
            x_sq.after(eng, group)
            eng.activation(xr[:, :], xss[:, :], ACT.Ln, bias=eps[:, 0:1], scale=1.0 / D).then_inc(x_ln.sem, 1)
            x_ln.after(eng, group)
            eng.activation(xr[:, :], xr[:, :], ACT.Exp, scale=-0.5).then_inc(x_rs.sem, 1)

        def take_h(it):
            for n in range(4):
                j, half = n // 2, n % 2
                it.full(eng, f"h{n}")
                eng.activation(hT[:, 4 * half:4 * half + 4, j * P:(j + 1) * P], v4(it.bank(f"h{n}")),
                               ACT.Copy).then_inc(bank_taken, 1)

        def take(it, name):
            if not it.fill:
                return
            it.full(eng, name)
            src, nxt = it.bank(name), 1 - it.p
            if name == "ba":
                eng.activation(ba[:, :, :], src[:, 0:16].rearrange("p (j c) -> p j c", j=2), ACT.Copy).then_inc(bank_taken, 1)
            elif name[0] == "c":
                b = int(name[1])
                if b == 0:
                    hist.after(eng, it.g)
                eng.activation(U[:, 2 * b:2 * b + 2, SHORT - 1:], src[:, :].rearrange("p (c t) -> p c t", c=2),
                               ACT.Copy).then_inc(bank_taken, 1)
            else:
                j = int(name[1])
                if it.chain and j == 0:
                    y_rows.after(eng, it.g * 2 - 1)
                eng.activation(ZS[nxt][:, j, :], src[:, :], ACT.Copy).then_inc(bank_taken, 1)

        def take_y(it, j):
            it.full(eng, f"y{j}")
            if j == 0:
                y_out.after(eng, it.g - 1)
            eng.activation(yT[:, :, j * P:(j + 1) * P], v4(it.bank(f"y{j}")), ACT.Identity,
                           scale=onorm[:, 0:1]).then_inc(bank_taken, 1)

        def gate_exps(n):
            gate_a.after(eng, n)
            eng.activation(ge[:, 0], ba[:, :, 0:H], ACT.Exp, scale=-1.0).then_inc(gate_e.sem, 1)
            eng.activation(ge[:, 1], ga[:, 1], ACT.Exp, scale=-1.0).then_inc(gate_e.sem, 1)
            gate_e.after(eng, n, 2)
            eng.activation(ge[:, 2], ge[:, 1], ACT.Ln, bias=1.0).then_inc(gate_e.sem, 1)

        def square_tile(g, p, j):
            T = g * 2 + j
            scal_full.after(eng, T - 1)
            eng.activation(sq[:, :, :], QKV[p][:, 0:8, j * P:(j + 1) * P], ACT.Square).then_inc(squares.sem, 1)

        def tile(it, j):
            T = it.g * 2 + j
            scal_full.after(eng, T)
            facs.after(eng, T - 1)
            eng.activation(rn[:, :], bS[:, 0:8], ACT.Ln, bias=eps[:, 0:1]).then_inc(r_ln.sem, 1)
            r_ln.after(eng, T)
            eng.activation(rn[:, :], rn[:, :], ACT.Exp, scale=-0.5).then_inc(r_exp.sem, 1)
            vec_in.after(eng, T)
            eng.activation(evec[:, :], vec[:, :], ACT.Exp).then_inc(dec_e.sem, 1)
            if j == 0 and it.fill:
                take_h(it)
            difs.after(eng, T)
            eng.activation(Dl[:, :, :], Dl[:, :, :], ACT.Exp, scale=-1.0).then_inc(d_exp.sem, 1)
            eng.activation(Du[:, :, :], Du[:, :, :], ACT.Exp).then_inc(d_exp.sem, 1)
            tok_full.after(eng, T, 1)
            eng.activation(ktok[:, :, :], B3, ACT.Copy).then_inc(ktok_in.sem, 1)
            if j == 0:
                if it.y_before:
                    take_y(it, 1)
                take(it, "ba")
                square_tile(it.g, it.p, 1)
                y_rows.after(eng, T - 1)
                eng.activation(ez[:, :, :], ZS[it.p][:, :, :], ACT.Exp, scale=-1.0).then_inc(z_exp.sem, 1)
            for l in range(1, LEVELS):
                x_full.after(eng, T, l)
                if l < LEVELS - 1:
                    eng.activation(half_all(X[l], l, 1), packed(bX, l), ACT.Copy).then_inc(x_copied.sem, 1)
                else:
                    eng.activation(X_last[:, :], bX[:, 0:H * P // 2], ACT.Copy).then_inc(x_copied.sem, 1)
                for at, name in {0: ((1, "c0"), (3, "c1"), (5, "c2")), 1: ((1, "c4"), (3, "c5"), (5, "z0"))}[j]:
                    if at == l:
                        take(it, name)
                if j == 1 and l == 3:
                    take_y(it, 0)
                if j == 1 and l == 2 and it.fill:
                    gate_exps(it.g + 1)
                if j == 1 and l == 4 and it.norm:
                    norm(it.g + 2)
            if j == 1 and it.fill:
                silu(it)
            vhat_full.after(eng, T)
            eng.activation(vh[:, :, :], B3, ACT.Copy).then_inc(vh_in.sem, 1)
            if j == 1 and it.fill:
                after_silu(it)
            take(it, "c3" if j == 0 else "z1")
            o_sum.after(eng, T)
            eng.activation(osq[:, :, :], o[:, :, :], ACT.Square).then_inc(o_sq.sem, 1)
            o_red.after(eng, T)
            eng.activation(ors[:, :], oss[:, :], ACT.Ln, bias=eps[:, 0:1], scale=1.0 / P).then_inc(o_ln.sem, 1)
            o_ln.after(eng, T)
            eng.activation(ors[:, :], ors[:, :], ACT.Exp, scale=-0.5).then_inc(o_rs.sem, 1)

        def silu(it):
            eng.preload_act_table_set(SILU)
            conv.after(eng, it.g + 1)
            p = 1 - it.p
            eng.activation(QKV[p][:, :, :], QKV[p][:, :, :], ACT.Silu).then_inc(silu_done.sem, 1)

        def after_silu(it):
            eng.preload_act_table_set(EXP_LN)
            silu_done.after(eng, it.g + 1)
            square_tile(it.g + 1, 1 - it.p, 0)

        def body(it):
            if it.chain:
                tile(it, 0)
                tile(it, 1)
                return
            take_h(it)
            take(it, "ba")
            take(it, "c0")
            gate_exps(0)
            for b in range(1, 6):
                take(it, f"c{b}")
                if b == 2:
                    norm(1)
            take(it, "z0")
            silu(it)
            after_silu(it)
            take(it, "z1")

        eng.preload_act_table_set(EXP_LN)
        eng.wait_ge(env["eps_in"], 1)
        norm(0)
        eng.wait_ge(params_in, 16 * 5)
        eng.activation(nega[:, :], nega[:, :], ACT.Exp).then_inc(once, 1)
        over_groups(eng, body)
        take_y(last, 1)

    def dve(eng):
        def normed(group, tiles=(0, 1)):
            x_rs.after(eng, group)
            for j in tiles:
                eng.scalar_tensor_tensor(out=xt[:, j, :], in0=xt[:, j, :], scalar=xr[:, j:j + 1], in1=nm_bc[:, :],
                                         op0=ALU.mult, op1=ALU.mult).then_inc(x_nrm.sem, 1)

        def convolve(it, b, half):
            if not it.fill:
                return
            n = it.g + 1
            dst = QKV[1 - it.p]
            if half == 0:
                it.taken(eng, f"c{b}")
                if b == 0 and it.chain:
                    ks_full.after(eng, it.g * 2 - 1)
            for tap in (2 * half, 2 * half + 1):
                for c in (2 * b, 2 * b + 1):
                    src = U[:, c, tap:tap + G_TOK]
                    w = convw[:, tap, c:c + 1]
                    if tap == 0:
                        eng.tensor_scalar(dst[:, c, :], src, w, None, ALU.mult).then_inc(conv.sem, 1)
                    else:
                        conv.after(eng, n, b * 8 + 2 * (tap - 1) + c % 2 + 1)
                        eng.scalar_tensor_tensor(out=dst[:, c, :], in0=src, scalar=w, in1=dst[:, c, :],
                                                 op0=ALU.mult, op1=ALU.add).then_inc(conv.sem, 1)
            if b == 5 and half == 1:
                eng.tensor_copy(U[:, :, 0:SHORT - 1], U[:, :, G_TOK:]).then_inc(hist.sem, 1)

        def gates_in(it):
            n = it.g + 1
            it.taken(eng, "ba")
            eng.tensor_tensor(ga[:, 0], ba[:, :, H:2 * H], mid(dtb[:, :], 2), ALU.add).then_inc(gate_a.sem, 1)
            gate_a.after(eng, n, 1)
            eng.scalar_tensor_tensor(out=ga[:, 1], in0=ga[:, 0], scalar=-1.0, in1=ga[:, 0], op0=ALU.mult, op1=ALU.max).then_inc(gate_a.sem, 1)
            eng.tensor_scalar(ga[:, 2], ga[:, 0], 0.0, None, ALU.max).then_inc(gate_a.sem, 1)

        def gates_out(it):
            n = it.g + 1
            p = 1 - it.p
            gate_e.after(eng, n)
            eng.tensor_scalar(ge[:, 0], ge[:, 0], 1.0, None, ALU.add).then_inc(gate_g.sem, 1)
            eng.tensor_tensor(ga[:, 2], ga[:, 2], ge[:, 2], ALU.add).then_inc(gate_g.sem, 1)
            gate_g.after(eng, n, 2)
            eng.reciprocal(beta[p][:, :, :], ge[:, 0]).then_inc(gate_g.sem, 1)
            eng.tensor_tensor(gt[p][:, :, :], ga[:, 2], mid(nega[:, :], 2), ALU.mult).then_inc(gate_g.sem, 1)

        def tile(it, j):
            T = it.g * 2 + j
            egc, egl, dec = evec[:, 0:4], evec[:, 4:8], evec[:, 8:12]
            rb, f, fe, s = fac[:, 0], fac[:, 1], fac[:, 2], fac[:, 3]
            scal_full.after(eng, T)
            dec_e.after(eng, T - 1)
            r_ln.after(eng, T)
            eng.tensor_copy(vec[:, 0:8], bS[:, 8:16]).then_inc(vec_in.sem, 1)
            vec_in.after(eng, T, 1)
            eng.tensor_tensor(vec[:, 8:12], vec[:, 4:8], vec[:, 0:4], ALU.subtract).then_inc(vec_in.sem, 1)
            gcrow_full.after(eng, T)
            eng.tensor_tensor(Du[:, :, :], B0, bcast(vec[:, 0:4], P), ALU.subtract).then_inc(difs.sem, 1)
            difs.after(eng, T, 1)
            eng.tensor_scalar(Dl[:, :, :], Du[:, :, :], 0.0, None, ALU.max).then_inc(difs.sem, 1)
            eng.tensor_scalar(Du[:, :, :], Du[:, :, :], 0.0, None, ALU.min).then_inc(difs.sem, 1)
            r_exp.after(eng, T)
            eng.tensor_tensor(rb, rn[:, 4:8], beta[it.p][:, j, :], ALU.mult).then_inc(facs.sem, 1)
            facs.after(eng, T, 1)
            eng.tensor_tensor(f, rb, rn[:, 4:8], ALU.mult).then_inc(facs.sem, 1)
            facs.after(eng, T, 2)
            dec_e.after(eng, T)
            eng.tensor_tensor(fe, f, egc, ALU.mult).then_inc(facs.sem, 1)
            eng.tensor_scalar(s, rn[:, 0:4], float(P) ** -0.5, None, ALU.mult).then_inc(facs.sem, 1)
            d_exp.after(eng, T, 1)
            gram_full.after(eng, T)
            eng.tensor_tensor(A[:, :, :], B1, Dl[:, :, :], ALU.mult).then_inc(a_mat.sem, 1)
            a_mat.after(eng, T, 1)
            eng.tensor_tensor(A[:, :, :], A[:, :, :], bcast(f, P), ALU.mult).then_inc(a_mat.sem, 1)
            tok_full.after(eng, T)
            eng.tensor_tensor(vb[:, :, :], B4, bcast(rb, P), ALU.mult).then_inc(vb_in.sem, 1)
            du_mask.after(eng, T)
            eng.tensor_tensor(QKd[:, :, :], B2, Du[:, :, :], ALU.mult).then_inc(qk_d.sem, 1)
            a_lvl.after(eng, T, 1)
            eng.tensor_tensor(T_[:, :, :], mid(ident, H), Aoff[0][:, :, :], ALU.subtract).then_inc(inv.sem, 1)
            a0T_full.after(eng, T)
            eng.tensor_tensor(M[:, :, :], mid(ident, H), B0, ALU.subtract).then_inc(inv.sem, 1)
            if j == 1:
                convolve(it, 3, 0)
            for l in range(1, LEVELS):
                if l == 1:
                    ks_full.after(eng, T, 1)
                    facs.after(eng, T)
                    eng.tensor_tensor(R[:, :, :], B3, bcast(fe, P), ALU.mult).then_inc(rhs.sem, 1)
                    ks_full.after(eng, T)
                    eng.tensor_tensor(o[:, :, :], B4, bcast(egc, P), ALU.mult).then_inc(o_q.sem, 1)
                    rhs.after(eng, T, 1)
                    vb_in.after(eng, T)
                    eng.tensor_tensor(R[:, :, :], vb[:, :, :], R[:, :, :], ALU.subtract).then_inc(rhs.sem, 1)
                if j == 1 and l >= 5 and it.norm:
                    normed(it.g + 2, (l - 5,))
                d_full.after(eng, T, 2 * l - 1)
                inv.after(eng, T, 2 * l)
                eng.tensor_tensor(half_all(M, l, 1), half_all(M, l, 1), packed(bM, l), ALU.subtract).then_inc(inv.sem, 1)
                if l < LEVELS - 1:
                    d_full.after(eng, T, 2 * l)
                    eng.tensor_tensor(half_all(T_, l, 0), half_all(T_, l, 0), packed(bT, l), ALU.subtract).then_inc(inv.sem, 1)
                if j == 0 and l >= 2:
                    convolve(it, (l - 2) // 2, l % 2)
                if j == 1 and l == 1:
                    convolve(it, 3, 1)
                    if it.fill:
                        gates_in(it)
                if j == 1 and 2 <= l <= 5:
                    convolve(it, 4 + (l - 2) // 2, l % 2)
                if j == 1 and l == 3 and it.fill:
                    gates_out(it)
                if j == 0 and l <= 3:
                    silu_z(it, l)
                if l == 3:
                    st_dec_op(T, egl)
            vh_in.after(eng, T)
            eng.tensor_tensor(vd[:, :, :], vh[:, :, :], bcast(dec, P), ALU.mult).then_inc(vd_in.sem, 1)
            if j == 0:
                convolve(it, 2, 1)
            o2_full.after(eng, T)
            o_q.after(eng, T)
            eng.tensor_tensor(o[:, :, :], o[:, :, :], B0, ALU.add).then_inc(o_sum.sem, 1)
            ds_full.after(eng, T)
            st_dec.after(eng, T)
            eng.tensor_tensor(S[:, :, :], S[:, :, :], B1, ALU.add).then_inc(state.sem, 1)
            o_sum.after(eng, T, 1)
            eng.tensor_tensor(o[:, :, :], o[:, :, :], bcast(s, P), ALU.mult).then_inc(o_sum.sem, 1)
            o_sq.after(eng, T)
            eng.tensor_reduce(oss[:, :], osq[:, :, :], AX.X, ALU.add).then_inc(o_red.sem, 1)
            o_rs.after(eng, T)
            if j == 0:
                eng.wait_ge(bank_full, it.base + 1)
            elif it.y_before:
                it.full(eng, "y1")
            eng.tensor_tensor(Y[j][:, :, :], o[:, :, :], bcast(ors[:, :], P), ALU.mult).then_inc(y_rows.sem, 1)
            y_rows.after(eng, T, 1)
            z_silu.after(eng, it.g)
            eng.tensor_tensor(Y[j][:, :, :], Y[j][:, :, :], ZS[it.p][:, j, :].rearrange("p (h n) -> p h n", h=H),
                              ALU.mult).then_inc(y_rows.sem, 1)

        def silu_z(it, step):
            if step == 1:
                z_exp.after(eng, it.g)
                ins = eng.tensor_scalar(ez[:, :, :], ez[:, :, :], 1.0, None, ALU.add)
            else:
                z_silu.after(eng, it.g, step - 1)
                if step == 2:
                    ins = eng.reciprocal(ez[:, :, :], ez[:, :, :])
                else:
                    ins = eng.tensor_tensor(ZS[it.p][:, :, :], ZS[it.p][:, :, :], ez[:, :, :], ALU.mult)
            ins.then_inc(z_silu.sem, 1)

        def st_dec_op(T, egl):
            ks_full.after(eng, T)
            state.after(eng, T - 1)
            eng.tensor_tensor(S[:, :, :], S[:, :, :], bcast(egl, P), ALU.mult).then_inc(st_dec.sem, 1)

        def body(it):
            if it.chain:
                tile(it, 0)
                tile(it, 1)
            else:
                gates_in(it)
                for b in range(6):
                    convolve(it, b, 0)
                    convolve(it, b, 1)
                    if b == 0:
                        gates_out(it)
                normed(1)

        eng.memset(U[:, :, 0:SHORT - 1], 0.0).then_inc(once, 1)
        eng.memset(S[:, :, :], 0.0).then_inc(once, 1)
        for l in range(1, LEVELS - 1):
            eng.memset(X[l][:, :, :], 0.0).then_inc(once, 1)
        eng.wait_ge(params_in, 16 * 5)
        eng.wait_ge(once, ONCE)
        eng.tensor_scalar(nega[:, :], nega[:, :], -1.0, None, ALU.mult).then_inc(once, 1)
        eng.wait_ge(once, ONCE + 1)
        normed(0)
        over_groups(eng, body)

    def pool(eng):
        def tile(it, j):
            T = it.g * 2 + j
            d_exp.after(eng, T)
            eng.tensor_tensor(Du[:, :, :], Du[:, :, :], mid(tri, H), ALU.mult).then_inc(du_mask.sem, 1)
            a_mat.after(eng, T)
            vhat_full.after(eng, T - 1)
            for l in range(LEVELS):
                eng.tensor_tensor(Aoff[l][:, :, :], A[:, :, :], mid(const(C_LVL + l), H), ALU.mult).then_inc(a_lvl.sem, 1)

        def body(it):
            if it.chain:
                tile(it, 0)
                tile(it, 1)

        over_groups(eng, body)

    def started(name, program):
        def run(eng):
            for s in ahead[name]:
                eng.sem_inc(s.sem if isinstance(s, Signal) else s, 1)
            program(eng)
        return run

    programs = dict(sync=sp, tensor=pe, scalar=act, vector=dve, gpsimd=pool)
    return own, {name: started(name, program) for name, program in programs.items()}


def conformer_pass(nc, ctx, env):
    x, w_in, w_out = env["x"], env["w_in"], env["w_out"]
    consts, banks, eps = env["consts"], env["banks"], env["eps"]
    own = ctx.enter_context(ExitStack())

    def sb(name, shape, dt=F32):
        return own.enter_context(nc.sbuf_tensor(name, shape, dt))

    ident = consts[:, C_ID * P:(C_ID + 1) * P]
    ones = consts[:, C_ONES * P:(C_ONES + 1) * P]
    N_PARAMS = 5
    HIST = CONF_TAPS - 1
    CB = CF // P
    HALF = D // 2

    w_cf, w_o = env["w_cf"], env["w_o"]
    nm_bc, xt = env["norm_mix_rows"], env["x_group"]
    w_r = sb("w_router", [P, KD, N_LOGIT])
    b_r = sb("b_router_rows", [P, N_LOGIT])
    nf_bc = sb("norm_ffn_rows", [P, D])
    taps = sb("dw_taps", [P, CONF_TAPS, CB])
    cols = sb("cf_columns", [P, 3, CB])
    mean_w = sb("mean_weights", [P, P])
    junk = sb("square_junk2", [P, D])
    xss = sb("x2_sumsq", [P, 2])
    xr = sb("x2_rstd", [P, 2])
    hT = sb("hT2", [P, KD, G_TOK])
    sg = sb("glu_sigmoid", [P, CB, G_TOK])
    G = [sb(f"glu{i}", [P, CB, HIST + G_TOK]) for i in range(2)]
    C = [sb(f"conv_out{i}", [P, CB, G_TOK]) for i in range(2)]
    csq = sb("conv_squares", [P, CB, G_TOK])
    vrs = sb("ln_rstd", [P, G_TOK])
    ycf = sb("y_cf_columns", [P, CB, G_TOK])
    ydn = sb("y_dn_columns", [P, CB, G_TOK])
    res = sb("residual", [P, 2, D])
    x2 = [sb(f"x_mixed{i}", [P, 2, D]) for i in range(2)]
    x2ss = sb("x_mixed_sumsq", [P, 2])
    x2rs = sb("x_mixed_rstd", [P, 2])
    h2 = sb("h_ffn", [P, 2, D])
    h2T = sb("h_ffnT", [P, KD, G_TOK])
    logits = env["logits"]

    v4 = lambda b: b[:, :].rearrange("p (h n) -> p h n", h=4)
    ring, outb, bStat, bLog = banks[0:4], banks[4:6], banks[6], banks[7]
    mean_v, var_v = bStat[:, 0:G_TOK], bStat[:, G_TOK:2 * G_TOK]

    sem = env["sem"]
    params_in, w_cf_in, w_o_in = sem("p2_params_in"), env["w_cf_in"], env["w_o_in"]
    mean_w_in = sem("p2_mean_weights")
    x_in, ydn_in, res_in = Signal(sem("p2_x_in"), 16, 1 - 16), Signal(sem("p2_ydn_in"), 16), Signal(sem("p2_res_in"), 16)
    x2_out, h2_out = Signal(sem("p2_x2_out"), 16), Signal(sem("p2_h2_out"), 16)
    h_full, glu_full = Signal(sem("p2_h_full"), 4), Signal(sem("p2_glu_full"), 4)
    mean_full, var_full = Signal(sem("p2_mean_full")), Signal(sem("p2_var_full"))
    out_full = Signal(sem("p2_out_full"), 4)
    h2_full, log_full = Signal(sem("p2_h2_full"), 4), Signal(sem("p2_logits_full"))
    x_sq, x_ln, x_rs = Signal(sem("p2_x_sq"), 2, 1 - 2), Signal(sem("p2_x_ln"), 1, 0), Signal(sem("p2_x_rstd"), 1, 0)
    h_taken, h2_taken = Signal(sem("p2_h_taken"), 4), Signal(sem("p2_h2_taken"), 4)
    c_sq, v_ln, v_rs = Signal(sem("p2_c_sq")), Signal(sem("p2_v_ln")), Signal(sem("p2_v_rstd"))
    silu_c, sigm = Signal(sem("p2_silu"), 4), Signal(sem("p2_sigmoid"), 4)
    x2_sq, x2_ln, x2_rs = Signal(sem("p2_x2_sq"), 2), Signal(sem("p2_x2_ln")), Signal(sem("p2_x2_rstd"))
    x_nrm, h2_nrm = Signal(sem("p2_x_normed"), 2, 1 - 2), Signal(sem("p2_h2_normed"), 2)
    centred, c_nrm = Signal(sem("p2_centred")), Signal(sem("p2_c_normed"))
    glu, conv = Signal(sem("p2_glu"), 4), Signal(sem("p2_conv"), CONF_TAPS * 4)
    x2_sum, logit = Signal(sem("p2_x2_sum"), 4), Signal(sem("p2_logit"))
    hist = Signal(sem("p2_history"))
    ahead = dict(
        sync=[x_in, ydn_in, res_in, x2_out, h2_out],
        tensor=[h_full, glu_full, mean_full, var_full, out_full, h2_full, log_full],
        scalar=[x_sq, x_ln, x_rs, h_taken, h2_taken, c_sq, v_ln, v_rs, silu_c, sigm, x2_sq, x2_ln, x2_rs],
        vector=[x_nrm, h2_nrm, centred, c_nrm, glu, conv, x2_sum, logit, hist],
        gpsimd=[])
    env["x2_out"], env["h2_out"], env["logit"] = x2_out, h2_out, logit

    class Step:

        def __init__(self, s, parity, steady=False):
            self.s, self.p = s, parity
            def has(n):
                return steady or 0 <= s + n < NG
            self.norm, self.proj, self.conv, self.out, self.logits = has(2), has(1), has(0), has(-1), has(-2)
            self.steady = steady

    def over_steps(eng, body):
        for s in (-1, 0, 1):
            body(Step(s, s % 2))
        with eng.Fori(0, (NG - 4) // 2) as i:
            body(Step(i * 2 + 2, 0, True))
            body(Step(i * 2 + 3, 1, True))
        for s in range(NG - 2, NG + 2):
            body(Step(s, s % 2))

    def tok(g, j=0, n=G_TOK):
        return bass.ds(g * G_TOK + j * P, n)

    def by_tile(dram, g):
        return dram[tok(g), :].rearrange("(j p) d -> p j d", p=P)

    def sp(eng):
        def load_x(g):
            eng.dma_start(xt[:, :, :], by_tile(x, g)).then_inc(x_in.sem, 16)

        h_full.after(eng, 0)
        load_x(1)
        for dst, src in ((nf_bc, env["norm_ffn"].partition_broadcast(P)), (b_r, env["b_router"].partition_broadcast(P))):
            eng.dma_start(dst[:, :], src).then_inc(params_in, 16)
        eng.dma_start(taps[:, :, :], env["w_dw"]).then_inc(params_in, 16)
        eng.dma_start(cols[:, :, :], env["cf_cols"]).then_inc(params_in, 16)
        eng.dma_start(w_r[:, :, :], env["w_router"].rearrange("(k p) n -> p k n", p=P)).then_inc(params_in, 16)
        def body(it):
            s = it.s
            if it.norm:
                h_full.after(eng, s + 1)
                load_x(s + 2)
            if it.out:
                if it.steady or s >= 2:
                    x2_sum.after(eng, s - 2)
                eng.dma_start(ydn[:, :, :], env["y_dnT"][:, tok(s - 1)].rearrange("(h p) t -> p h t", p=P)).then_inc(ydn_in.sem, 16)
                eng.dma_start(res[:, :, :], by_tile(x, s - 1)).then_inc(res_in.sem, 16)
            if it.logits:
                h2_nrm.after(eng, s - 2)
                eng.dma_start(by_tile(env["h_rows"], s - 2), h2[:, :, :]).then_inc(h2_out.sem, 16)
            if it.out:
                x2_sum.after(eng, s - 1)
                eng.dma_start(by_tile(env["x_rows"], s - 1), x2[1 - it.p][:, :, :]).then_inc(x2_out.sem, 16)

        def first(it):
            if it.steady or it.s > -1:
                body(it)

        over_steps(eng, first)

    def pe(eng):
        def transposes(g, src, full, waits, ready):
            for n in range(4):
                j, half = n // 2, n % 2
                for w in waits:
                    w(n)
                if half == 0 and ready:
                    ready.after(eng, g, j + 1)
                for q in range(4):
                    k = half * 4 + q
                    ins = eng.transpose(ring[n][:, q * P:(q + 1) * P], src[:, j, k * P:(k + 1) * P], ident)
                ins.then_inc(full.sem, 1)

        def glu_unit(it, b):
            for part in range(2):
                c = b + part * CB
                for k in range(KD):
                    ins = eng.matmul(ring[b][:, part * G_TOK:(part + 1) * G_TOK], w_cf[:, k, c * P:(c + 1) * P],
                                     hT[:, k, :], start=(k == 0), stop=(k == KD - 1))
            ins.then_inc(glu_full.sem, 1)

        def body(it):
            s = it.s
            if it.out:
                conv.after(eng, s - 1)
                if it.steady or s >= 2:
                    centred.after(eng, s - 2)
                for b in range(CB):
                    ins = eng.matmul(mean_v, mean_w[:, :], C[1 - it.p][:, b, :], start=(b == 0), stop=(b == CB - 1))
                ins.then_inc(mean_full.sem, 1)
            if it.proj:
                h_taken.after(eng, s + 1)
                glu_unit(it, 0)
            if it.out:
                c_sq.after(eng, s - 1)
                if it.steady or s >= 2:
                    v_ln.after(eng, s - 2)
                for b in range(CB):
                    ins = eng.matmul(var_v, mean_w[:, :], csq[:, b, :], start=(b == 0), stop=(b == CB - 1))
                ins.then_inc(var_full.sem, 1)
            if it.proj:
                for b in range(1, 4):
                    glu_unit(it, b)

            def out_tile(j):
                for half in range(2):
                    if j == 1:
                        x2_sum.after(eng, s - 1, half + 1)
                    elif it.steady or s >= 2:
                        x2_sum.after(eng, s - 2, 3 + half)
                    for k in range(KD):
                        y = ydn if k < CB else ycf
                        ins = eng.matmul(outb[half][:, :], y[:, k % CB, j * P:(j + 1) * P],
                                         w_o[:, k, half * HALF:(half + 1) * HALF], start=(k == 0), stop=(k == KD - 1))
                    ins.then_inc(out_full.sem, 1)

            if it.out:
                if not it.steady and s == 1:
                    eng.wait_ge(w_o_in, 16 * KD)
                    eng.wait_ge(params_in, 16 * N_PARAMS)
                ydn_in.after(eng, s - 1)
                silu_c.after(eng, s - 1)
                out_tile(0)
            if it.logits:
                free = (lambda n: glu.after(eng, s + 1, n + 1)) if it.proj else (lambda n: h2_taken.after(eng, s - 3, n + 1))
                transposes(s - 2, h2, h2_full, [free], h2_nrm)
            if it.out:
                out_tile(1)
            if it.norm:
                if it.logits:
                    free = lambda n: h2_taken.after(eng, s - 2, n + 1)
                else:
                    free = lambda n: glu.after(eng, s + 1, n + 1)
                transposes(s + 2, xt, h_full, [free], x_nrm)
            if it.logits:
                h2_taken.after(eng, s - 2)
                if it.steady or s >= 3:
                    logit.after(eng, s - 3)
                for j in range(2):
                    for k in range(KD):
                        ins = eng.matmul(bLog[:, j * N_LOGIT:(j + 1) * N_LOGIT], h2T[:, k, j * P:(j + 1) * P],
                                         w_r[:, k, :], start=(k == 0), stop=(k == KD - 1))
                ins.then_inc(log_full.sem, 1)

        eng.wait_ge(mean_w_in, 1)
        transposes(0, xt, h_full, [], None)
        eng.wait_ge(w_cf_in, 16 * KD)
        over_steps(eng, body)

    def act(eng):
        def x_norm(g):
            x_in.after(eng, g)
            for j in range(2):
                x_sq.after(eng, g, j)
                eng.activation(junk[:, :], xt[:, j, :], ACT.Square, accum_out=xss[:, j:j + 1]).then_inc(x_sq.sem, 1)
            x_sq.after(eng, g)
            eng.activation(xr[:, :], xss[:, :], ACT.Ln, bias=eps[:, 0:1], scale=1.0 / D).then_inc(x_ln.sem, 1)
            x_ln.after(eng, g)
            eng.activation(xr[:, :], xr[:, :], ACT.Exp, scale=-0.5).then_inc(x_rs.sem, 1)

        def take(g, full, dst, sig):
            for n in range(4):
                j, half = n // 2, n % 2
                full.after(eng, g, n + 1)
                eng.activation(dst[:, 4 * half:4 * half + 4, j * P:(j + 1) * P], v4(ring[n]), ACT.Copy).then_inc(sig.sem, 1)

        def square_x2(it, j):
            g = it.s - 1
            x2_sum.after(eng, g, 2 * j + 2)
            x2_sq.after(eng, g, j)
            if it.logits and j == 0:
                x2_rs.after(eng, g - 1)
            eng.activation(junk[:, :], x2[1 - it.p][:, j, :], ACT.Square, accum_out=x2ss[:, j:j + 1]).then_inc(x2_sq.sem, 1)

        def body(it):
            s = it.s
            if it.logits:
                x2_sq.after(eng, s - 2)
                eng.activation(x2rs[:, :], x2ss[:, :], ACT.Ln, bias=eps[:, 0:1], scale=1.0 / D).then_inc(x2_ln.sem, 1)
                x2_ln.after(eng, s - 2)
                eng.activation(x2rs[:, :], x2rs[:, :], ACT.Exp, scale=-0.5).then_inc(x2_rs.sem, 1)
            if it.out:
                centred.after(eng, s - 1)
                eng.activation(csq[:, :, :], C[1 - it.p][:, :, :], ACT.Square).then_inc(c_sq.sem, 1)
            if it.norm:
                x_norm(s + 2)
            if it.out:
                var_full.after(eng, s - 1)
                if it.steady or s >= 2:
                    c_nrm.after(eng, s - 2)
                eng.activation(vrs[:, :], var_v, ACT.Ln, bias=eps[:, 0:1]).then_inc(v_ln.sem, 1)
                v_ln.after(eng, s - 1)
                eng.activation(vrs[:, :], vrs[:, :], ACT.Exp, scale=-0.5).then_inc(v_rs.sem, 1)
                eng.preload_act_table_set(SILU)
                c_nrm.after(eng, s - 1)
                if it.steady or s >= 2:
                    out_full.after(eng, s - 2)
                for b in range(CB):
                    eng.activation(ycf[:, b, :], C[1 - it.p][:, b, :], ACT.Silu, scale=cols[:, 1, b:b + 1],
                                   bias=cols[:, 2, b:b + 1]).then_inc(silu_c.sem, 1)
            if it.proj:
                eng.preload_act_table_set(SIGMOID)
                for b in range(CB):
                    glu_full.after(eng, s + 1, b + 1)
                    if it.conv:
                        glu.after(eng, s, b + 1)
                    eng.activation(sg[:, b, :], ring[b][:, G_TOK:], ACT.Sigmoid).then_inc(sigm.sem, 1)
            eng.preload_act_table_set(EXP_LN)
            if it.logits:
                if it.steady or s >= 3:
                    log_full.after(eng, s - 3)
                take(s - 2, h2_full, h2T, h2_taken)
            if it.out:
                square_x2(it, 0)
            if it.norm:
                take(s + 2, h_full, hT, h_taken)
            if it.out:
                square_x2(it, 1)

        eng.preload_act_table_set(EXP_LN)
        take(0, h_full, hT, h_taken)
        over_steps(eng, body)

    def dve(eng):
        def normed(g):
            x_rs.after(eng, g)
            for j in range(2):
                eng.scalar_tensor_tensor(out=xt[:, j, :], in0=xt[:, j, :], scalar=xr[:, j:j + 1], in1=nm_bc[:, :],
                                         op0=ALU.mult, op1=ALU.mult).then_inc(x_nrm.sem, 1)

        def glu_unit(it, b):
            if not it.proj:
                return
            g = it.s + 1
            sigm.after(eng, g, b + 1)
            if b == 0 and (it.steady or it.s >= 0):
                if it.steady or it.s >= 1:
                    conv.after(eng, it.s - 1)
                hist.after(eng, it.s)
            eng.tensor_tensor(G[1 - it.p][:, b, HIST:], ring[b][:, 0:G_TOK], sg[:, b, :], ALU.mult).then_inc(glu.sem, 1)

        def convolve(it, t0, n):
            if not it.conv:
                return
            src, dst = G[it.p], C[it.p]
            if t0 == 0:
                glu.after(eng, it.s)
                if it.steady or it.s >= 1:
                    hist.after(eng, it.s - 1)
                if it.steady or it.s >= 2:
                    silu_c.after(eng, it.s - 2)
            for tap in range(t0, t0 + n):
                for b in range(CB):
                    w = taps[:, tap, b:b + 1]
                    if tap == 0:
                        ins = eng.tensor_scalar(dst[:, b, :], src[:, b, tap:tap + G_TOK], w, cols[:, 0, b:b + 1],
                                                ALU.mult, ALU.add)
                    else:
                        conv.after(eng, it.s, CB * (tap - 1) + b + 1)
                        ins = eng.scalar_tensor_tensor(out=dst[:, b, :], in0=src[:, b, tap:tap + G_TOK], scalar=w,
                                                       in1=dst[:, b, :], op0=ALU.mult, op1=ALU.add)
                    ins.then_inc(conv.sem, 1)

        def add_residual(it, j, half):
            if not it.out:
                return
            g = it.s - 1
            if j == 0 and half == 0:
                res_in.after(eng, g)
                if it.steady or it.s >= 3:
                    x2_out.after(eng, g - 2)
            out_full.after(eng, g, 2 * j + half + 1)
            cs = slice(half * HALF, (half + 1) * HALF)
            eng.tensor_tensor(x2[1 - it.p][:, j, cs], outb[half][:, :], res[:, j, cs], ALU.add).then_inc(x2_sum.sem, 1)

        def body(it):
            s = it.s
            if it.logits:
                x2_rs.after(eng, s - 2)
                if it.steady or s >= 3:
                    h2_out.after(eng, s - 3)
                    h2_full.after(eng, s - 3)
                for j in range(2):
                    eng.scalar_tensor_tensor(out=h2[:, j, :], in0=x2[it.p][:, j, :], scalar=x2rs[:, j:j + 1],
                                             in1=nf_bc[:, :], op0=ALU.mult, op1=ALU.mult).then_inc(h2_nrm.sem, 1)
            if it.out:
                mean_full.after(eng, s - 1)
                c = C[1 - it.p]
                eng.tensor_tensor(c[:, :, :], c[:, :, :], mid(mean_v, CB), ALU.subtract).then_inc(centred.sem, 1)
            if it.conv and it.proj:
                glu.after(eng, s)
                if it.steady or s >= 1:
                    conv.after(eng, s - 1)
                eng.tensor_copy(G[1 - it.p][:, :, 0:HIST], G[it.p][:, :, G_TOK:]).then_inc(hist.sem, 1)
            convolve(it, 0, 4)
            if it.out:
                v_rs.after(eng, s - 1)
                c = C[1 - it.p]
                centred.after(eng, s - 1)
                eng.tensor_tensor(c[:, :, :], c[:, :, :], mid(vrs[:, :], CB), ALU.mult).then_inc(c_nrm.sem, 1)
            convolve(it, 4, 4)
            glu_unit(it, 0)
            convolve(it, 8, 3)
            glu_unit(it, 1)
            convolve(it, 11, 2)
            glu_unit(it, 2)
            if it.norm:
                normed(s + 2)
            convolve(it, 13, 2)
            glu_unit(it, 3)
            convolve(it, 15, 4)
            add_residual(it, 0, 0)
            convolve(it, 19, 4)
            add_residual(it, 0, 1)
            convolve(it, 23, 5)
            add_residual(it, 1, 0)
            convolve(it, 28, 3)
            add_residual(it, 1, 1)
            if it.logits:
                log_full.after(eng, s - 2)
                eng.tensor_tensor(logits[:, bass.ds((s - 2) * 2, 2), :],
                                  bLog[:, 0:2 * N_LOGIT].rearrange("p (j n) -> p j n", j=2), mid(b_r[:, :], 2),
                                  ALU.add).then_inc(logit.sem, 1)

        eng.memset(G[0][:, :, 0:HIST], 0.0).then_inc(env["g_hist0"], 1)
        eng.wait_ge(env["g_hist0"], 1)
        eng.tensor_scalar(mean_w[:, :], ones, 1.0 / CF, None, ALU.mult).then_inc(mean_w_in, 1)
        eng.wait_ge(params_in, 16 * N_PARAMS)
        over_steps(eng, body)

    def started(name, program):
        def run(eng):
            for s in ahead[name]:
                eng.sem_inc(s.sem, 1)
            program(eng)
        return run

    programs = dict(sync=sp, tensor=pe, scalar=act, vector=dve)
    return own, {name: started(name, program) for name, program in programs.items()}


N_BLOCK = SEQ * 2 // P + N_EXP
SLOTS = N_EXP * SEQ
FAR = -1e30
ENTRY = 2


def router_pass(nc, ctx, env):
    consts, banks, logits = env["consts"], env["banks"], env["logits"]
    own = ctx.enter_context(ExitStack())
    NGr, NE = N_GROUPS, EXP_PER_GROUP

    def sb(name, shape, dt=F32):
        return own.enter_context(nc.sbuf_tensor(name, shape, dt))

    strict = consts[:, C_STRICT * P:(C_STRICT + 1) * P]
    ones = consts[:, C_ONES * P:(C_ONES + 1) * P]
    gl = logits[:, :, 0:NGr]
    el = logits[:, :, NGr:].rearrange("p t (g e) -> p t g e", g=NGr)
    down = sb("count_down", [P, NE])
    gmax, gsum, pg = sb("r_gmax", [P, NT]), sb("r_gsum", [P, NT]), sb("r_pg", [P, NT])
    gd, gval, gsel = sb("r_gd", [P, NT, NGr]), sb("r_gval", [P, NT, NGr]), sb("r_gsel", [P, NT, NGr])
    esel4, e8 = sb("r_esel4", [P, NT, NGr, NE]), sb("r_e8", [P, NT, NE])
    m = [sb(f"r_max{k}", [P, NT]) for k in range(2)]
    val, vmax = sb("r_val", [P, NT, NE]), sb("r_vmax", [P, NT])
    one = [sb(f"r_onehot{k}", [P, NT, NE]) for k in range(2)]
    e8b = sb("r_e8b", [P, NT, NE])
    ed, wden = sb("r_exp_diff", [P, NT]), sb("r_wden", [P, NT])
    wt = [sb(f"r_weight{k}", [P, NT]) for k in range(2)]
    OH = [sb(f"r_choice{k}", [P, NT, NGr, NE]) for k in range(2)]
    M = sb("r_chosen", [P, NT, N_EXP])
    cum = sb("r_before", [P, NT + 1, N_EXP])
    region = sb("r_region", [P, N_EXP])
    R = sb("r_rank", [P, NT, N_EXP])
    prod = sb("r_prod", [P, NT, N_EXP])
    slotf = sb("r_slotf", [P, 2, NT])
    slot = sb("r_slot", [P, NT, 2], U32)
    entry = sb("r_entry", [P, NT, 2, ENTRY], I32)
    fill = sb("r_fill", [P, SLOTS // P + 2, ENTRY], I32)
    zero_rows = sb("r_zero_rows", [P, D])
    cnt = sb("r_count", [P, N_EXP])
    cnt_i = sb("r_count_i", [P, N_EXP], I32)
    nbf = sb("r_blocks_f", [P, N_EXP])
    bs = [sb(f"r_base{k}", [P, N_EXP]) for k in range(2)]
    base = sb("r_base", [P, N_EXP])
    step = sb("r_step", [P, N_EXP])
    blk = sb("r_block_no", [P, N_BLOCK + 2])
    reach = sb("r_reach", [P, N_BLOCK + 2, N_EXP])
    first = sb("r_first_slot", [P, N_BLOCK + 2])
    meta = env["meta"]

    sem = env["sem"]
    fill_made, fill_in = sem("r_fill_made"), sem("r_fill_in")
    entries_in = sem("r_entries_in")
    steps = sem("r_steps")
    exps = sem("r_exps")
    ranks = sem("r_ranks")
    iotas = sem("r_iotas")
    entry_ready = sem("r_entry_ready")
    env["meta_in"] = sem("r_meta_in")
    at = {}

    def dve(eng):
        n = [0]

        def op(name, ins):
            ins.then_inc(steps, 1)
            n[0] += 1
            at[name] = n[0]

        def need(*names):
            eng.wait_ge(steps, max(at[x] for x in names))

        eng.wait_ge(iotas, 4)
        env["logit"].after(eng, NG - 1)
        op("gmax", eng.tensor_reduce(gmax[:, :], gl, AX.X, ALU.max))
        need("gmax")
        op("gd", eng.tensor_tensor(gd[:, :, :], gl, bcast(gmax[:, :], NGr), ALU.subtract))
        op("geq", eng.tensor_tensor(gval[:, :, :], gl, bcast(gmax[:, :], NGr), ALU.is_equal))
        need("geq")
        op("gval", eng.tensor_tensor(gval[:, :, :], gval[:, :, :], mid(down[:, NE - NGr:], NT), ALU.mult))
        need("gval")
        op("gtop", eng.tensor_reduce(vmax[:, :], gval[:, :, :], AX.X, ALU.max))
        need("gtop")
        op("gsel", eng.tensor_tensor(gsel[:, :, :], gval[:, :, :], bcast(vmax[:, :], NGr), ALU.is_equal))
        eng.wait_ge(exps, 1)
        op("gsum", eng.tensor_reduce(gsum[:, :], gd[:, :, :], AX.X, ALU.add))
        need("gsum")
        op("pg", eng.reciprocal(pg[:, :], gsum[:, :]))
        op("esel4", eng.tensor_tensor(esel4[:, :, :, :], el, bcast(gsel[:, :, :], NE), ALU.mult))
        need("esel4")
        op("e8", eng.tensor_reduce(e8[:, :, :], esel4[:, :, :, :].rearrange("p t g e -> p t e g"), AX.X, ALU.add))
        for k in range(2):
            src = e8 if k == 0 else e8b
            need("e8" if k == 0 else "e8b")
            op(f"m{k}", eng.tensor_reduce(m[k][:, :], src[:, :, :], AX.X, ALU.max))
            need(f"m{k}")
            op("val", eng.tensor_tensor(val[:, :, :], src[:, :, :], bcast(m[k][:, :], NE), ALU.is_equal))
            need("val")
            op("val", eng.tensor_tensor(val[:, :, :], val[:, :, :], mid(down[:, :], NT), ALU.mult))
            need("val")
            op("vmax", eng.tensor_reduce(vmax[:, :], val[:, :, :], AX.X, ALU.max))
            need("vmax")
            op(f"one{k}", eng.tensor_tensor(one[k][:, :, :], val[:, :, :], bcast(vmax[:, :], NE), ALU.is_equal))
            need(f"one{k}")
            if k == 0:
                op("e8b", eng.scalar_tensor_tensor(out=e8b[:, :, :], in0=one[0][:, :, :], scalar=FAR, in1=e8[:, :, :],
                                                   op0=ALU.mult, op1=ALU.add))
            for g in range(NGr):
                op(f"OH{k}", eng.tensor_tensor(OH[k][:, :, g, :], one[k][:, :, :],
                                               gsel[:, :, g:g + 1].to_broadcast([P, NT, NE]), ALU.mult))
        op("ed", eng.tensor_tensor(ed[:, :], m[1][:, :], m[0][:, :], ALU.subtract))
        need("OH1")
        ch = [OH[k][:, :, :, :].rearrange("p t g e -> p t (g e)") for k in range(2)]
        op("M", eng.tensor_tensor(M[:, :, :], ch[0], ch[1], ALU.add))
        op("cum0", eng.memset(cum[:, 0, :], 0.0))
        need("cum0")
        for t in range(NT):
            op(f"cum{t + 1}", eng.tensor_tensor(cum[:, t + 1, :], cum[:, t, :], M[:, t, :], ALU.add))
            need(f"cum{t + 1}")
        eng.wait_ge(exps, 2)
        op("wden", eng.tensor_scalar(wden[:, :], ed[:, :], 1.0, None, ALU.add))
        need("wden")
        op("wden", eng.reciprocal(wden[:, :], wden[:, :]))
        need("wden")
        op("wt0", eng.tensor_tensor(wt[0][:, :], pg[:, :], wden[:, :], ALU.mult))
        need("wt0")
        op("wt1", eng.tensor_tensor(wt[1][:, :], wt[0][:, :], ed[:, :], ALU.mult))
        eng.wait_ge(ranks, 1)
        op("R", eng.tensor_tensor(R[:, :, :], banks[0][:, :].rearrange("p (t e) -> p t e", t=NT),
                                  mid(region[:, :], NT), ALU.add))
        for k in range(2):
            need("R")
            op("prod", eng.tensor_tensor(prod[:, :, :], ch[k], R[:, :, :], ALU.mult))
            need("prod")
            op("slotf", eng.tensor_reduce(slotf[:, k, :], prod[:, :, :], AX.X, ALU.add))
            need("slotf")
            op("slot", eng.tensor_copy(slot[:, :, k], slotf[:, k, :]))
            need("slot", "wt1")
            op("entry", eng.tensor_copy(entry[:, :, k, 1].bitcast(F32), wt[k][:, :]))
            need("entry")
        eng.sem_inc(entry_ready, 1)
        eng.wait_ge(ranks, 2)
        op("cnt", eng.tensor_scalar(cnt[:, :], banks[1][:, 0:N_EXP], 1.0, float(P - 1), ALU.max, ALU.add))
        need("cnt")
        op("cnt_i", eng.tensor_copy(cnt_i[:, :], cnt[:, :]))
        need("cnt_i")
        op("nblk", eng.tensor_scalar(cnt_i[:, :], cnt_i[:, :], 7, None, ALU.arith_shift_right))
        need("nblk")
        op("nbf", eng.tensor_copy(nbf[:, :], cnt_i[:, :]))
        src, name = nbf, "nbf"
        for i in range(5):
            s, dst = 1 << i, bs[i % 2]
            need(name)
            op("a", eng.tensor_copy(dst[:, 0:s], src[:, 0:s]))
            op(f"bs{i}", eng.tensor_tensor(dst[:, s:], src[:, s:], src[:, 0:N_EXP - s], ALU.add))
            src, name = dst, f"bs{i}"
        need(name)
        op("base", eng.tensor_tensor(base[:, :], src[:, :], nbf[:, :], ALU.subtract))
        op("meta", eng.tensor_copy(meta[:, N_EXP:2 * N_EXP], src[:, :]))
        need("base")
        op("meta", eng.tensor_copy(meta[:, 0:N_EXP], base[:, :]))
        need("base")
        op("step0", eng.memset(step[:, 0:1], 0.0))
        op("step", eng.tensor_scalar(step[:, 1:], nbf[:, 0:N_EXP - 1], -float(P), float(SEQ), ALU.mult, ALU.add))
        op("reach", eng.tensor_tensor(reach[:, :, :], bcast(blk[:, :], N_EXP), mid(base[:, :], N_BLOCK + 2), ALU.is_ge))
        need("reach")
        op("reach", eng.tensor_tensor(reach[:, :, :], reach[:, :, :], mid(step[:, :], N_BLOCK + 2), ALU.mult))
        need("reach")
        op("first", eng.tensor_reduce(first[:, :], reach[:, :, :], AX.X, ALU.add))
        need("first")
        op("first", eng.scalar_tensor_tensor(out=first[:, :], in0=blk[:, :], scalar=float(P), in1=first[:, :],
                                             op0=ALU.mult, op1=ALU.add))
        need("first")
        eng.tensor_copy(meta[:, 2 * N_EXP:2 * N_EXP + N_BLOCK + 2], first[:, :]).then_inc(env["meta_in"], 1)

    def act(eng):
        eng.preload_act_table_set(EXP_LN)
        eng.wait_ge(steps, at["gd"])
        eng.activation(gd[:, :, :], gd[:, :, :], ACT.Exp).then_inc(exps, 1)
        eng.wait_ge(steps, at["ed"])
        eng.activation(ed[:, :], ed[:, :], ACT.Exp).then_inc(exps, 1)

    def pe(eng):
        flat = lambda a: a.rearrange("p t e -> p (t e)")
        eng.wait_ge(steps, at[f"cum{NT}"])
        eng.matmul(banks[0][:, :], strict, flat(M[:, :, :]), start=True, stop=False)
        eng.matmul(banks[0][:, :], ones, flat(cum[:, 0:NT, :]), start=False, stop=True).then_inc(ranks, 1)
        eng.matmul(banks[1][:, 0:N_EXP], ones, cum[:, NT, :], start=True, stop=True).then_inc(ranks, 1)

    def pool(eng):
        eng.iota(down[:, :], [[-1, NE]], base=NE, channel_multiplier=0, allow_small_or_imprecise_dtypes=True).then_inc(iotas, 1)
        eng.iota(region[:, :], [[SEQ, N_EXP]], base=0, channel_multiplier=0, allow_small_or_imprecise_dtypes=True).then_inc(iotas, 1)
        eng.iota(blk[:, :], [[1, N_BLOCK + 2]], base=0, channel_multiplier=0, allow_small_or_imprecise_dtypes=True).then_inc(iotas, 1)
        eng.iota(entry[:, :, :, 0], [[P, NT], [0, 2]], base=0, channel_multiplier=1).then_inc(iotas, 1)
        eng.iota(fill[:, :, 1], [[0, SLOTS // P + 2]], base=0, channel_multiplier=0).then_inc(fill_made, 1)
        eng.memset(zero_rows[:, :], 0.0).then_inc(fill_made, 1)
        eng.iota(fill[:, :, 0], [[1, SLOTS // P + 2]], base=0, channel_multiplier=SLOTS // P + 2).then_inc(fill_made, 1)
        eng.wait_ge(entry_ready, 1)
        eng.wait_ge(fill_in, 16 * 3)
        for t in range(NT):
            for k in range(2):
                eng.indirect_dma_start(out=env["table"][:, :], out_offset=bass.IndirectOffsetOnAxis(ap=slot[:, t, k:k + 1], axis=0),
                                       in_=entry[:, t, k, :], in_offset=None).then_inc(entries_in, 16)
        eng.wait_ge(entries_in, 16 * 2 * NT)

    def sp(eng):
        eng.wait_ge(env["fill_masked"], 1)
        eng.dma_start(env["table"].rearrange("(p j) c -> p j c", p=P), fill[:, :, :]).then_inc(fill_in, 16)
        for rows in ("h_rows", "x_rows"):
            eng.dma_start(env[rows][SEQ:, :], zero_rows[:, :]).then_inc(fill_in, 16)

    def mask_fill(eng):
        eng.wait_ge(fill_made, 3)
        eng.tensor_scalar(fill[:, :, 0], fill[:, :, 0], P - 1, SEQ, ALU.bitwise_and, ALU.bitwise_or).then_inc(env["fill_masked"], 1)

    env["fill_masked"] = sem("r_fill_masked")

    def dve_all(eng):
        mask_fill(eng)
        dve(eng)

    return own, dict(sync=sp, tensor=pe, scalar=act, vector=dve_all, gpsimd=pool)


def expert_pass(nc, ctx, env):
    consts, banks, meta = env["consts"], env["banks"], env["meta"]
    own = ctx.enter_context(ExitStack())
    ident = consts[:, C_ID * P:(C_ID + 1) * P]
    DE = 512
    KE = DE // P
    HALF = D // 2

    def sb(name, shape, dt=F32):
        return own.enter_context(nc.sbuf_tensor(name, shape, dt))

    W = env["expert_w"]
    wg = [w[:, 0, :].rearrange("p (k n) -> p k n", k=KD) for w in W]
    wu = [w[:, 1, :].rearrange("p (k n) -> p k n", k=KD) for w in W]
    wd = [w[:, 2, :].rearrange("p (k n) -> p k n", k=KE) for w in W]
    e_far = sb("entries_far", [P, ENTRY], I32)
    e_next = sb("entries_next", [P, ENTRY], I32)
    e_mid = sb("entries_mid", [P, ENTRY], I32)
    e_cur = sb("entries_now", [P, ENTRY], I32)
    xg = sb("gathered_rows", [P, D])
    xT = sb("gathered_T", [P, KD, P])
    hg = sb("silu_gate", [P, DE])
    ha = sb("hidden", [P, DE])
    haT = sb("hidden_T", [P, KE, P])
    y = sb("expert_out", [P, D])

    bG, bU, bX, bA, bY = banks[0], banks[1], banks[2:4], [banks[4], banks[7]], banks[5:7]
    v4 = lambda b: b[:, :].rearrange("p (h n) -> p h n", h=4)
    sem = env["sem"]
    w_in = [sem(f"m_weight_halves{k}_in") for k in range(2)]
    ent_in, rows_in = Signal(sem("m_entries_in"), 16, 0), Signal(sem("m_rows_in"), 16, 0)
    stored = Signal(sem("m_y_stored"), 16, 16)
    xT_full, gu_full = Signal(sem("m_xT_full"), 2), Signal(sem("m_gate_up_full"), 2)
    hT_full, y_full = Signal(sem("m_hidden_T_full"), 2), Signal(sem("m_y_full"), 2)
    xT_a, xT_v = Signal(sem("m_xT_by_act")), Signal(sem("m_xT_by_dve"))
    silu, hid = Signal(sem("m_silu")), Signal(sem("m_hidden"))
    hT_a, hT_v = Signal(sem("m_hidden_T_by_act")), Signal(sem("m_hidden_T_by_dve"))
    y_a, y_v = Signal(sem("m_y_by_act")), Signal(sem("m_y_by_dve"))
    steps_begun = sem("m_pool_steps_begun")
    e_kept, e_moved, e_set = Signal(sem("m_entries_kept")), Signal(sem("m_entries_moved")), Signal(sem("m_entries_set"))
    ahead = dict(sync=[], tensor=[xT_full, gu_full, hT_full, y_full], scalar=[xT_a, silu, hT_a, y_a],
                 vector=[xT_v, hid, hT_v, y_v, e_kept, e_moved, e_set], gpsimd=[])
    HI = N_BLOCK

    def n_blocks(eng):
        return eng.value_load(meta[0:1, 2 * N_EXP - 1:2 * N_EXP], min_val=N_EXP, max_val=HI)

    def load_expert(eng, e, half):
        run = KD * DE // 2
        for i, src in enumerate((env["w_gate"], env["w_up"], env["w_down"])):
            part = src[bass.ds(e, 1)].rearrange("a (p k) n -> p (a k n)", p=P)
            for c in range(2):
                if not isinstance(e, int) or e > 0 or i > 0:
                    eng.wait_ge(w_in[c], e * 48 + i * 16)
                eng.dma_start(W[half][:, i, c * run:(c + 1) * run], part[:, c * run:(c + 1) * run]).then_inc(w_in[c], 16)

    def sp(eng):
        with eng.Fori(0, N_EXP // 2 - 1) as pair:
            for half in range(2):
                done = eng.value_load(meta[0:1, bass.ds(pair * 2 + (N_EXP + half), 1)], min_val=1, max_val=HI)
                y_full.after(eng, done, 0)
                load_expert(eng, pair * 2 + 2 + half, half)

    def pe(eng):
        def x_transposes(i):
            rows_in.after(eng, i)
            for half in range(2):
                (xT_a if half == 0 else xT_v).after(eng, i - 1)
                for q in range(4):
                    k = 4 * half + q
                    ins = eng.transpose(bX[half][:, q * P:(q + 1) * P], xg[:, k::KD], ident)
                ins.then_inc(xT_full.sem, 1)

        def block(i, pair, half):
            for c in range(2):
                eng.wait_ge(w_in[c], pair * 96 + half * 48 + 48)
            xT_a.after(eng, i)
            xT_v.after(eng, i)
            silu.after(eng, i - 1)
            for k in range(KD):
                ins = eng.matmul(bG[:, :], xT[:, k, :], wg[half][:, k, :], start=(k == 0), stop=(k == KD - 1))
            ins.then_inc(gu_full.sem, 1)
            hid.after(eng, i - 1)
            for k in range(KD):
                ins = eng.matmul(bU[:, :], xT[:, k, :], wu[half][:, k, :], start=(k == 0), stop=(k == KD - 1))
            ins.then_inc(gu_full.sem, 1)
            x_transposes(i + 1)
            hid.after(eng, i)
            for part, taken in enumerate((hT_v, hT_a)):
                taken.after(eng, i - 1)
                for q in range(KE // 2):
                    ins = eng.transpose(bA[part][:, q * P:(q + 1) * P], ha[:, part * (KE // 2) + q::KE], ident)
                ins.then_inc(hT_full.sem, 1)
            hT_v.after(eng, i)
            for n in range(2):
                (y_a if n == 0 else y_v).after(eng, i - 1)
                for q in range(KE):
                    if n == 0 and q == KE // 2:
                        hT_a.after(eng, i)
                    ins = eng.matmul(bY[n][:, :], haT[:, q, :], wd[half][:, q, n * HALF:(n + 1) * HALF],
                                     start=(q == 0), stop=(q == KE - 1))
                ins.then_inc(y_full.sem, 1)

        x_transposes(0)
        with eng.Fori(0, N_EXP // 2) as pair:
            for half in range(2):
                e = pair * 2 + half
                start = eng.value_load(meta[0:1, bass.ds(e, 1)], min_val=0, max_val=HI)
                end = eng.value_load(meta[0:1, bass.ds(e + N_EXP, 1)], min_val=1, max_val=HI)
                with eng.Fori(start, end) as i:
                    block(i, pair, half)

    def act(eng):
        def take_x(i):
            xT_full.after(eng, i, 1)
            gu_full.after(eng, i - 1)
            eng.activation(xT[:, 0:4, :], v4(bX[0]), ACT.Copy).then_inc(xT_a.sem, 1)

        eng.preload_act_table_set(SILU)
        take_x(0)
        with eng.Fori(0, n_blocks(eng)) as i:
            gu_full.after(eng, i, 1)
            hid.after(eng, i - 1)
            eng.activation(hg[:, :], bG[:, :], ACT.Silu).then_inc(silu.sem, 1)
            take_x(i + 1)
            hT_full.after(eng, i)
            y_full.after(eng, i - 1)
            eng.activation(haT[:, 2:4, :], bA[1][:, 0:2 * P].rearrange("p (h n) -> p h n", h=2), ACT.Copy).then_inc(hT_a.sem, 1)
            y_full.after(eng, i, 1)
            e_set.after(eng, i)
            stored.after(eng, i - 1)
            eng.activation(y[:, 0:HALF], bY[0][:, :], ACT.Identity, scale=e_cur[:, 1:2].bitcast(F32)).then_inc(y_a.sem, 1)

    def dve(eng):
        def take_x(i):
            xT_full.after(eng, i)
            gu_full.after(eng, i - 1)
            eng.tensor_copy(xT[:, 4:8, :], v4(bX[1])).then_inc(xT_v.sem, 1)

        def move(i):
            ent_in.after(eng, i)
            eng.tensor_copy(e_next[:, :], e_far[:, :]).then_inc(e_moved.sem, 1)

        move(0)
        take_x(0)
        with eng.Fori(0, n_blocks(eng)) as i:
            e_set.after(eng, i - 1)
            e_moved.after(eng, i)
            eng.tensor_copy(e_mid[:, :], e_next[:, :]).then_inc(e_kept.sem, 1)
            e_kept.after(eng, i)
            move(i + 1)
            silu.after(eng, i)
            hT_full.after(eng, i - 1)
            gu_full.after(eng, i)
            eng.tensor_tensor(ha[:, :], hg[:, :], bU[:, :], ALU.mult).then_inc(hid.sem, 1)
            hT_full.after(eng, i, 1)
            y_full.after(eng, i - 1)
            eng.tensor_copy(haT[:, 0:2, :], bA[0][:, 0:2 * P].rearrange("p (h n) -> p h n", h=2)).then_inc(hT_v.sem, 1)
            stored.after(eng, i - 1)
            y_a.after(eng, i - 1)
            e_kept.after(eng, i)
            eng.tensor_copy(e_cur[:, :], e_mid[:, :]).then_inc(e_set.sem, 1)
            take_x(i + 1)
            y_full.after(eng, i)
            e_set.after(eng, i)
            eng.tensor_scalar(y[:, HALF:], bY[1][:, :], e_cur[:, 1:2].bitcast(F32), None, ALU.mult).then_inc(y_v.sem, 1)

    def pool(eng):
        def settle():
            eng.sem_inc(steps_begun, 1)

        def entries(slot):
            eng.dma_start(e_far[:, :], env["table"][bass.ds(slot, P), :]).then_inc(ent_in.sem, 16)

        def gather(i):
            e_moved.after(eng, i)
            settle()
            eng.indirect_dma_start(out=xg[:, :], out_offset=None, in_=env["h_rows"][:, :],
                                   in_offset=bass.IndirectOffsetOnAxis(ap=e_next[:, 0:1].bitcast(U32), axis=0)).then_inc(rows_in.sem, 16)

        def slot_of(i):
            return eng.value_load(meta[0:1, bass.ds(i + 2 * N_EXP, 1)], min_val=0, max_val=SLOTS + P)

        eng.dma_start(e_cur[:, :], env["table"][SLOTS:SLOTS + P, :]).then_inc(stored.sem, 16)
        entries(0)
        gather(0)
        entries(slot_of(1))
        with eng.Fori(0, n_blocks(eng)) as i:
            xT_full.after(eng, i)
            gather(i + 1)
            entries(slot_of(i + 2))
            y_a.after(eng, i)
            y_v.after(eng, i)
            settle()
            eng.indirect_dma_start(out=env["x_rows"][:, :], out_offset=bass.IndirectOffsetOnAxis(ap=e_cur[:, 0:1].bitcast(U32), axis=0),
                                   in_=y[:, :], in_offset=None, compute_op=ALU.add).then_inc(stored.sem, 16)
        stored.after(eng, n_blocks(eng) - 1)
        settle()

    def started(name, program):
        def run(eng):
            for s in ahead[name]:
                eng.sem_inc(s.sem, 1)
            program(eng)
        return run

    def first_experts(eng):
        load_expert(eng, 0, 0)
        load_expert(eng, 1, 1)

    env["first_experts"] = first_experts
    programs = dict(sync=sp, tensor=pe, scalar=act, vector=dve, gpsimd=pool)
    return own, {name: started(name, program) for name, program in programs.items()}


def final_pass(nc, ctx, env):
    own = ctx.enter_context(ExitStack())
    F = 2
    NF = NT // F

    def sb(name, shape, dt=F32):
        return own.enter_context(nc.sbuf_tensor(name, shape, dt))

    nfin = sb("norm_final_rows", [P, D])
    xf = [sb(f"final_x{n}", [P, F, D]) for n in range(NF)]
    junk = sb("final_junk", [P, D])
    ss = [sb(f"final_sumsq{n}", [P, F]) for n in range(NF)]
    sem = env["sem"]
    w_in, out = sem("f_weight_in"), sem("f_out")
    x_in = [sem(f"f_x_in{n}") for n in range(NF)]
    sq, ln, rs, nrm = sem("f_sq"), sem("f_ln"), sem("f_rstd"), sem("f_normed")

    def rows(dram, n):
        return dram[n * F * P:(n + 1) * F * P, :].rearrange("(j p) d -> p j d", p=P)

    def sp(eng):
        for n in range(NF):
            eng.dma_start(xf[n][:, :, :], rows(env["x_rows"], n)).then_inc(x_in[n], 16)
            if n == 0:
                eng.dma_start(nfin[:, :], env["norm_final"].partition_broadcast(P)).then_inc(w_in, 16)
        for n in range(NF):
            eng.wait_ge(nrm, F * (n + 1))
            eng.dma_start(rows(env["out"], n), xf[n][:, :, :]).then_inc(out, 16)
        eng.wait_ge(out, 16 * NF)

    def act(eng):
        eng.preload_act_table_set(EXP_LN)
        for n in range(NF):
            eng.wait_ge(x_in[n], 16)
            for j in range(F):
                if n or j:
                    eng.wait_ge(sq, F * n + j)
                eng.activation(junk[:, :], xf[n][:, j, :], ACT.Square, accum_out=ss[n][:, j:j + 1]).then_inc(sq, 1)
            eng.wait_ge(sq, F * (n + 1))
            eng.activation(ss[n][:, :], ss[n][:, :], ACT.Ln, bias=env["eps"][:, 0:1], scale=1.0 / D).then_inc(ln, 1)
            eng.wait_ge(ln, n + 1)
            eng.activation(ss[n][:, :], ss[n][:, :], ACT.Exp, scale=-0.5).then_inc(rs, 1)

    def dve(eng):
        eng.wait_ge(w_in, 16)
        for n in range(NF):
            eng.wait_ge(rs, n + 1)
            for j in range(F):
                eng.scalar_tensor_tensor(out=xf[n][:, j, :], in0=xf[n][:, j, :], scalar=ss[n][:, j:j + 1],
                                         in1=nfin[:, :], op0=ALU.mult, op1=ALU.mult).then_inc(nrm, 1)

    idle = lambda eng: None
    return own, dict(sync=sp, tensor=idle, scalar=act, vector=dve, gpsimd=idle)


def build(nc, t):
    with ExitStack() as ctx:
        count = [0]

        def sem(name):
            count[0] += 1
            return ctx.enter_context(nc.semaphore(name))

        env = dict(t)
        env["sem"] = sem
        env["consts"] = ctx.enter_context(nc.sbuf_tensor("consts", [P, N_CONST * P], F32))
        env["eps"] = ctx.enter_context(nc.sbuf_tensor("eps", [P, 1], F32))
        env["banks"] = [ctx.enter_context(nc.psum_tensor(f"bank{i}", [P, 512], F32)) for i in range(8)]
        env["consts_in"] = sem("consts_in")
        env["eps_in"] = sem("eps_in")
        env["g_hist0"] = sem("p2_history_of_first")
        env["logits"] = ctx.enter_context(nc.sbuf_tensor("logits", [P, NT, N_LOGIT], F32))
        env["meta"] = ctx.enter_context(nc.sbuf_tensor("block_table", [P, 2 * N_EXP + N_BLOCK + 2], I32))
        over = [sem(f"pass{n}_over") for n in range(1, 5)]
        block = ctx.enter_context(nc.Block())
        passes = []
        shared = ctx.enter_context(ExitStack())
        env["weights"] = shared.enter_context(nc.sbuf_tensor("mixer_weights", [P, KD * DN_COLS], F32))
        half = KD * 2 * CF
        env["w_cf"] = env["weights"][:, 0:half].rearrange("p (k c) -> p k c", k=KD)
        env["w_o"] = env["weights"][:, half:half + KD * D].rearrange("p (k c) -> p k c", k=KD)
        env["norm_mix_rows"] = shared.enter_context(nc.sbuf_tensor("norm_mix_rows", [P, D], F32))
        env["x_group"] = shared.enter_context(nc.sbuf_tensor("x_group", [P, 2, D], F32))
        env["w_cf_in"], env["w_o_in"] = sem("p2_wcf_in"), sem("p2_wout_in")
        own, programs = deltanet_pass(nc, ctx, env)
        passes.append(programs)
        own.close()
        own, programs = conformer_pass(nc, ctx, env)
        passes.append(programs)
        own.close()
        shared.close()
        weights = ctx.enter_context(ExitStack())
        env["expert_w"] = [weights.enter_context(nc.sbuf_tensor(f"expert_w{k}", [P, 3, KD * 512], F32)) for k in range(2)]
        own, programs = router_pass(nc, ctx, env)
        passes.append(programs)
        own.close()
        own, programs = expert_pass(nc, ctx, env)
        passes.append(programs)
        own.close()
        weights.close()
        own, programs = final_pass(nc, ctx, env)
        passes.append(programs)

        def meet(eng, n):
            eng.drain()
            eng.sem_inc(over[n - 1], 1)
            eng.wait_ge(over[n - 1], 5)

        @block.vector
        def _(eng):
            eng.wait_ge(env["consts_in"], 16)
            passes[0]["vector"](eng)
            meet(eng, 1)
            passes[1]["vector"](eng)
            meet(eng, 2)
            passes[2]["vector"](eng)
            meet(eng, 3)
            eng.wait_ge(env["meta_in"], 1)
            passes[3]["vector"](eng)
            meet(eng, 4)
            passes[4]["vector"](eng)

        @block.sync
        def _(eng):
            eng.dma_start(env["consts"][:, :], t["shape_consts"]).then_inc(env["consts_in"], 16)
            passes[0]["sync"](eng)
            env["p1_done"].after(eng, NG - 1)
            meet(eng, 1)
            passes[1]["sync"](eng)
            env["x2_out"].after(eng, NG - 1)
            env["h2_out"].after(eng, NG - 1)
            meet(eng, 2)
            passes[2]["sync"](eng)
            env["first_experts"](eng)
            meet(eng, 3)
            eng.wait_ge(env["meta_in"], 1)
            passes[3]["sync"](eng)
            meet(eng, 4)
            passes[4]["sync"](eng)

        @block.gpsimd
        def _(eng):
            eng.memset(env["eps"][:, :], EPS).then_inc(env["eps_in"], 1)
            eng.wait_ge(env["consts_in"], 16)
            passes[0]["gpsimd"](eng)
            meet(eng, 1)
            meet(eng, 2)
            passes[2]["gpsimd"](eng)
            meet(eng, 3)
            eng.wait_ge(env["meta_in"], 1)
            passes[3]["gpsimd"](eng)
            meet(eng, 4)

        @block.scalar
        def _(eng):
            passes[0]["scalar"](eng)
            meet(eng, 1)
            passes[1]["scalar"](eng)
            meet(eng, 2)
            passes[2]["scalar"](eng)
            meet(eng, 3)
            eng.wait_ge(env["meta_in"], 1)
            passes[3]["scalar"](eng)
            meet(eng, 4)
            passes[4]["scalar"](eng)

        @block.tensor
        def _(eng):
            passes[0]["tensor"](eng)
            meet(eng, 1)
            passes[1]["tensor"](eng)
            meet(eng, 2)
            passes[2]["tensor"](eng)
            meet(eng, 3)
            eng.wait_ge(env["meta_in"], 1)
            passes[3]["tensor"](eng)
            meet(eng, 4)


def kernel(**inputs):
    import numpy as _np
    import concourse.bacc as _bacc
    from concourse import mybir as _mybir
    from concourse.bass_utils import run_bass_kernel_spmd as _run

    nc = _bacc.Bacc("TRN2", target_bir_lowering=False, num_devices=1)
    n = _np.arange(P)
    row, col = n[:, None], n[None, :]
    parts = [row == col, row <= col, row < col, row >= 0 * col]
    for l in range(LEVELS):
        parts.append((row > col) & ((row ^ col) >> l == 1))
    shape_consts = _np.concatenate([m.astype(_np.float32) for m in parts], axis=1)
    arrays = {"shape_consts": shape_consts}
    for name, a in inputs.items():
        a = _np.asarray(a)
        arrays[name] = _np.ascontiguousarray(a.reshape(a.shape[1:]) if a.ndim > 1 and a.shape[0] == 1 else a)
    arrays["conv_qkv"] = _np.ascontiguousarray(arrays["conv_qkv"].reshape(4, 12, 128).transpose(2, 0, 1))
    arrays["w_dw"] = _np.ascontiguousarray(arrays["w_dw"].reshape(CONF_TAPS, 4, 128).transpose(2, 0, 1))
    arrays["cf_cols"] = _np.ascontiguousarray(
        _np.stack([arrays.pop(n).reshape(4, 128) for n in ("b_dw", "ln_g", "ln_b")]).transpose(2, 0, 1))
    arrays["w_router"] = _np.concatenate([arrays.pop("w_rg"), arrays.pop("w_re")], axis=1)
    arrays["b_router"] = _np.concatenate([arrays.pop("b_rg"), arrays.pop("b_re")])
    t = {}
    for name, a in arrays.items():
        t[name] = nc.dram_tensor(f"in_{name}", a.shape, _mybir.dt.from_np(a.dtype), kind="ExternalInput").ap()
    t["conv_qkvT"] = t["conv_qkv"]
    t["y_dnT"] = nc.dram_tensor("y_dnT", (DN, SEQ), F32).ap()
    out = nc.dram_tensor("out", (SEQ, D), F32, kind="ExternalOutput").ap()
    t["h_rows"] = nc.dram_tensor("h_rows", (SEQ + P, D), F32).ap()
    t["x_rows"] = nc.dram_tensor("x_rows", (SEQ + P, D), F32).ap()
    t["table"] = nc.dram_tensor("slot_table", (SLOTS + 2 * P, ENTRY), I32).ap()
    t["out"] = out
    build(nc, t)
    r = _run(nc, [{f"in_{k}": v for k, v in arrays.items()}], core_ids=[0])
    return r.results[0]["out"].reshape(1, SEQ, D)
```

```python
from contextlib import ExitStack

import concourse.bass as bass
from concourse import mybir

F32 = mybir.dt.float32
I32 = mybir.dt.int32
U32 = mybir.dt.uint32
ACT = mybir.ActivationFunctionType
ALU = mybir.AluOpType
AX = mybir.AxisListType

P = 128
D = 1024
SEQ = 2048
KD = D // P
H = 4
DN = H * P
CF = D - DN
DN_COLS = 4 * DN + 2 * H
SHORT = 4
G_TOK = 256
NG = SEQ // G_TOK
NT = SEQ // P
LEVELS = 7
EPS = 1e-6
EXP_LN = "natural_log_exp_and_others"
SILU = "silu_and_others"
SIGMOID = "sigmoid_and_others"
CONF_TAPS = 31
N_GROUPS = 4
EXP_PER_GROUP = 8
N_EXP = N_GROUPS * EXP_PER_GROUP
N_LOGIT = N_GROUPS + N_EXP

C_ID, C_TRI, C_STRICT, C_ONES, C_LVL = 0, 1, 2, 3, 4
N_CONST = 4 + LEVELS


class Signal:

    def __init__(self, sem, per=1, lead=1):
        self.sem, self.per, self.lead = sem, per, lead

    def after(self, eng, rnd, k=None):
        k = self.per if k is None else k
        eng.wait_ge(self.sem, rnd * self.per + k + self.lead)


def bcast(ap, n):
    return ap.unsqueeze(len(ap.shape)).to_broadcast([*ap.shape, n])


def mid(ap, n):
    return ap.unsqueeze(1).to_broadcast([ap.shape[0], n, ap.shape[1]])


def deltanet_pass(nc, ctx, env):
    x, w_in, y_dnT = env["x"], env["w_in"], env["y_dnT"]
    consts, banks = env["consts"], env["banks"]
    own = ctx.enter_context(ExitStack())

    def sb(name, shape, dt=F32):
        return own.enter_context(nc.sbuf_tensor(name, shape, dt))

    def const(c):
        return consts[:, c * P:(c + 1) * P]

    ident, tri, ones = const(C_ID), const(C_TRI), const(C_ONES)

    w_sb = env["weights"][:, :].rearrange("p (k c) -> p k c", k=KD)
    nm_bc, xt = env["norm_mix_rows"], env["x_group"]
    convw = sb("conv_taps", [P, SHORT, 12])
    onorm = sb("o_norm_col", [P, 1])
    dtb = sb("dt_bias_rows", [P, H])
    nega = sb("neg_a_rows", [P, H])
    eps = env["eps"]
    junk = sb("square_junk", [P, D])
    ez = junk[:, :].rearrange("p (j n) -> p j n", j=2)
    xss = sb("x_sumsq", [P, 2])
    xr = sb("x_rstd", [P, 2])
    hT = env["hT"]
    U = sb("u_raw", [P, 12, G_TOK + SHORT - 1])
    QKV = [env["qkv0"], sb("qkv1", [P, 12, G_TOK])]
    glu0, glu_exp = env["glu0"], env["glu_exp"]
    ZS = [env["conv0"][:, :, :].rearrange("p b t -> p (b t)").rearrange("p (j n) -> p j n", j=2), sb("silu_z1", [P, 2, DN])]
    conv0, dw_taps, cf_cols = env["conv0"], env["dw_taps"], env["cf_columns"]
    ba = sb("ba_raw", [P, 2, 8])
    ga = sb("gate_tmp", [P, 3, 2, H])
    ge = sb("gate_exp", [P, 3, 2, H])
    beta = [sb(f"beta{i}", [P, 2, H]) for i in range(2)]
    gt = [sb(f"log_decay{i}", [P, 2, H]) for i in range(2)]
    sq = sb("qk_squares", [P, 8, P])
    rn = sb("qk_rnorm", [P, 8])
    vec = sb("decay_logs", [P, 12])
    evec = sb("decays", [P, 12])
    fac = sb("row_factors", [P, 4, H])
    Dl = sb("decay_lower", [P, H, P])
    Du = sb("decay_upper", [P, H, P])
    A = sb("a_mat", [P, H, P])
    Aoff = [sb(f"a_level{l}", [P, H, P]) for l in range(LEVELS)]
    M = sb("inverseT", [P, H, P])
    T_ = sb("inverse", [P, H, P])
    X = {l: sb(f"x_level{l}", [P, H, P]) for l in range(1, LEVELS - 1)}
    X_last = sb("x_last_level", [P, H * P // 2])
    QKd = sb("qk_decayed", [P, H, P])
    ktok = sb("k_rows", [P, H, P])
    vb = sb("v_scaled", [P, H, P])
    R = sb("solve_rhs", [P, H, P])
    S = sb("state", [P, H, P])
    vh = sb("v_new", [P, H, P])
    vd = sb("v_new_decayed", [P, H, P])
    o = sb("o_rows", [P, H, P])
    osq = sb("o_squares", [P, H, P])
    oss = sb("o_sumsq", [P, H])
    ors = sb("o_rstd", [P, H])
    Y = [sb(f"y_rows{i}", [P, H, P]) for i in range(2)]
    yT = sb("y_columns", [P, H, G_TOK])

    v4 = lambda b: b[:, :].rearrange("p (h n) -> p h n", h=H)

    def half_cols(t, h, l, second):
        return t[:, h, :].rearrange("p (b two s) -> p b two s", two=2, s=1 << l)[:, :, second, :]

    def half_all(t, l, second):
        return t[:, :, :].rearrange("p h (b two s) -> p (h b) two s", two=2, s=1 << l)[:, :, second, :]

    def packed(bank, l):
        return bank[:, 0:H * P // 2].rearrange("p (a s) -> p a s", s=1 << l)

    def packed_head(t, h):
        return t[:, h * P // 2:(h + 1) * P // 2]

    ring = banks[0:2]
    bS = banks[2]
    bX, bM, bT = banks[3:6]
    B0, B1, B2, B3, B4 = [v4(b) for b in banks[3:8]]

    sem = env["sem"]
    PIECES = [(4 * DN, DN_COLS)] + [(n * DN, (n + 1) * DN) for n in range(4)]
    weights_in = [sem(f"p1_weights_in{n}") for n in range(len(PIECES))]
    params_in = sem("p1_params_in")
    x_in = Signal(sem("p1_x_in"), 16)
    y_out = Signal(sem("p1_y_out"), 16)
    once = sem("p1_once")
    glu_val, glu_sig = sem("p1_glu_values"), sem("p1_glu_sigmoid")
    glu_made, conv_early = sem("p1_glu_made"), sem("p1_cf_conv")
    bank_full = sem("p1_bank_full")
    bank_taken = sem("p1_bank_taken")
    x_sq = Signal(sem("p1_x_squared"), 2)
    x_ln = Signal(sem("p1_x_ln"))
    x_rs = Signal(sem("p1_x_rstd"))
    x_nrm = Signal(sem("p1_x_normed"), 2)
    conv = Signal(sem("p1_conv"), 6 * 8)
    hist = Signal(sem("p1_history"))
    gate_a = Signal(sem("p1_gate_logits"), 3)
    gate_e = Signal(sem("p1_gate_exps"), 3)
    gate_g = Signal(sem("p1_gates"), 4)
    silu_done = Signal(sem("p1_silu"))
    z_exp = Signal(sem("p1_z_exp"))
    z_silu = Signal(sem("p1_z_silu"), 3)
    squares = Signal(sem("p1_squares"))
    scal_full = Signal(sem("p1_scal_full"))
    gcrow_full = Signal(sem("p1_gcrow_full"))
    gram_full = Signal(sem("p1_gram_full"))
    tok_full = Signal(sem("p1_tok_full"), 2)
    a0T_full = Signal(sem("p1_a0T_full"))
    x_full = Signal(sem("p1_xlevel_full"), 6)
    d_full = Signal(sem("p1_delta_full"), 11)
    ks_full = Signal(sem("p1_ks_full"), 2)
    vhat_full = Signal(sem("p1_vhat_full"))
    o2_full = Signal(sem("p1_o2_full"))
    ds_full = Signal(sem("p1_ds_full"))
    r_ln = Signal(sem("p1_rnorm_ln"))
    r_exp = Signal(sem("p1_rnorm"))
    dec_e = Signal(sem("p1_decays"))
    d_exp = Signal(sem("p1_decay_mats"), 2)
    ktok_in = Signal(sem("p1_ktok"))
    x_copied = Signal(sem("p1_xlevel_copied"), 6)
    vh_in = Signal(sem("p1_vnew"))
    o_sq = Signal(sem("p1_o_squared"))
    o_ln = Signal(sem("p1_o_ln"))
    o_rs = Signal(sem("p1_o_rstd"))
    vec_in = Signal(sem("p1_vec"), 2)
    facs = Signal(sem("p1_factors"), 4)
    difs = Signal(sem("p1_differences"), 3)
    a_mat = Signal(sem("p1_a_mat"), 2)
    qk_d = Signal(sem("p1_qk_decayed"))
    vb_in = Signal(sem("p1_v_scaled"))
    inv = Signal(sem("p1_inverse"), 13)
    rhs = Signal(sem("p1_rhs"), 2)
    o_q = Signal(sem("p1_o_state"))
    vd_in = Signal(sem("p1_vnew_decayed"))
    st_dec = Signal(sem("p1_state_decayed"))
    state = Signal(sem("p1_state"))
    o_sum = Signal(sem("p1_o_sum"), 2)
    o_red = Signal(sem("p1_o_reduced"))
    y_rows = Signal(sem("p1_y_rows"), 2)
    du_mask = Signal(sem("p1_upper_masked"))
    a_lvl = Signal(sem("p1_a_levels"), LEVELS)
    ahead = dict(
        sync=[x_in, y_out],
        tensor=[bank_full, scal_full, gcrow_full, gram_full, tok_full, a0T_full, x_full, d_full, ks_full, vhat_full,
                o2_full, ds_full],
        scalar=[bank_taken, x_sq, x_ln, x_rs, gate_e, silu_done, z_exp, squares, r_ln, r_exp, dec_e, d_exp, ktok_in, x_copied,
                vh_in, o_sq, o_ln, o_rs],
        vector=[x_nrm, conv, hist, gate_a, gate_g, z_silu, vec_in, facs, difs, a_mat, qk_d, vb_in, inv, rhs, o_q, vd_in, st_dec,
                state, o_sum, o_red, y_rows],
        gpsimd=[du_mask, a_lvl])
    env["p1_done"] = y_out

    def units(g):
        order = [f"h{n}" for n in range(4)]
        if g > 0:
            order += ["y1"]
        if g < NG - 1:
            order += ["ba"] + [f"c{b}" for b in range(6)]
        else:
            order += ["g0", "g1", "g2"]
        if g >= 0:
            order += ["y0"]
        order += ["z0", "z1"] if g < NG - 1 else ["g3"]
        return {name: n for n, name in enumerate(order)}

    U_ITER = len(units(1))
    U_FIRST = len(units(-1)) + len(units(0))
    ONCE = 1 + 2 + LEVELS - 2

    class Iter:

        def __init__(self, g, like):
            self.g, self.p = g, like % 2
            self.chain, self.fill, self.y_before = like >= 0, like < NG - 1, like > 0
            self.u = units(like)
            if like > 0:
                self.base = g * U_ITER + (U_FIRST - U_ITER)
                self.bp = (like * U_ITER + U_FIRST - U_ITER) % 2
            else:
                self.base = self.bp = 0 if like < 0 else len(units(-1))

        def bank(self, name):
            return ring[(self.bp + self.u[name]) % 2]

        def open_bank(self, eng, name):
            n = self.base + self.u[name]
            if isinstance(n, int) and n < 2:
                return
            eng.wait_ge(bank_taken, n - 1 + 1)

        def full(self, eng, name):
            eng.wait_ge(bank_full, self.base + self.u[name] + 1 + 1)

        def taken(self, eng, name):
            eng.wait_ge(bank_taken, self.base + self.u[name] + 1 + 1)

    last = Iter(NG - 1, NG - 1)
    last.base, last.bp, last.u = last.base + len(last.u), (last.bp + len(last.u)) % 2, {"y1": 0}

    def over_groups(eng, body):
        body(Iter(-1, -1))
        body(Iter(0, 0))
        with eng.Fori(0, (NG - 4) // 2) as i:
            body(Iter(i * 2 + 1, 1))
            body(Iter(i * 2 + 2, 2))
        for g in range(NG - 3, NG):
            body(Iter(g, g))

    def tok(g, j=0, n=G_TOK):
        return bass.ds(g * G_TOK + j * P, n)

    def sp(eng):
        eng.dma_start(nm_bc[:, :], env["norm_mix"].partition_broadcast(P)).then_inc(params_in, 16)
        eng.dma_start(convw[:, :, :], env["conv_qkvT"]).then_inc(params_in, 16)
        eng.dma_start(onorm[:, :], env["o_norm"].rearrange("(p a) -> p a", a=1)).then_inc(params_in, 16)
        eng.dma_start(dtb[:, :], env["dt_bias"].partition_broadcast(P)).then_inc(params_in, 16)
        eng.dma_start(nega[:, :], env["a_log"].partition_broadcast(P)).then_inc(params_in, 16)
        eng.dma_start(dw_taps[:, :, :], env["w_dw"]).then_inc(params_in, 16)
        eng.dma_start(cf_cols[:, :, :], env["cf_cols"]).then_inc(params_in, 16)

        def load_x(g):
            eng.dma_start(xt[:, :, :], x[tok(g - NG if isinstance(g, int) and g >= NG else g), :]
                          .rearrange("(j p) d -> p j d", p=P)).then_inc(x_in.sem, 16)

        load_x(0)
        for piece, (lo, hi) in enumerate(PIECES):
            eng.dma_start(w_sb[:, :, lo:hi], w_in[:, lo:hi].rearrange("(k p) c -> p k c", p=P)).then_inc(weights_in[piece], 16)

        def body(it):
            if not it.fill:
                eng.wait_ge(bank_full, it.base + 1)
                for n in range(2):
                    for c in (2 * n * P, CF + 2 * n * P):
                        eng.dma_start(env["w_cf"][:, :, c:c + 2 * P], w_in[:, DN_COLS + c:DN_COLS + c + 2 * P]
                                      .rearrange("(k p) c -> p k c", p=P)).then_inc(env["w_cf_in"][n], 16)
            it.full(eng, "h3")
            load_x(it.g + 2)
            if not it.fill:
                for k in range(KD):
                    eng.dma_start(env["w_o"][:, k, :], env["w_out"][k * P:(k + 1) * P, :]).then_inc(env["w_o_in"], 16)
            if it.y_before:
                it.taken(eng, "y1")
                store_y(it.g - 1)

        def store_y(g):
            eng.dma_start(y_dnT[:, tok(g)].rearrange("(h p) t -> p h t", p=P), yT[:, :, :]).then_inc(y_out.sem, 16)

        over_groups(eng, body)
        last.taken(eng, "y1")
        store_y(NG - 1)

    def pe(eng):
        def transposes(it):
            for n in range(4):
                j, half = n // 2, n % 2
                it.open_bank(eng, f"h{n}")
                if half == 0:
                    x_nrm.after(eng, it.g + 1, j + 1)
                for q in range(4):
                    k = half * 4 + q
                    ins = eng.transpose(it.bank(f"h{n}")[:, q * P:(q + 1) * P], xt[:, j, k * P:(k + 1) * P], ident)
                ins.then_inc(bank_full, 1)

        def quarters(it):
            it.taken(eng, "h3")
            it.open_bank(eng, "ba")
            first = not it.chain
            if first:
                eng.wait_ge(weights_in[0], 16)
            dst = it.bank("ba")
            for j in range(2):
                for k in range(KD):
                    ins = eng.matmul(dst[:, j * 8:j * 8 + 8], hT[:, k, j * P:(j + 1) * P],
                                     w_sb[:, k, 4 * DN:DN_COLS], start=(k == 0), stop=(k == KD - 1))
            ins.then_inc(bank_full, 1)
            yield
            for b in range(6):
                it.open_bank(eng, f"c{b}")
                if first and b % 2 == 0:
                    eng.wait_ge(weights_in[1 + b // 2], 16)
                dst = it.bank(f"c{b}")
                for q in range(4):
                    c = 2 * b + q // 2
                    for k in range(4 * (q % 2), 4 * (q % 2) + 4):
                        ins = eng.matmul(dst[:, (q // 2) * G_TOK:(q // 2 + 1) * G_TOK],
                                         w_sb[:, k, c * P:(c + 1) * P], hT[:, k, :],
                                         start=(k == 0), stop=(k == KD - 1))
                    if q == 3:
                        ins.then_inc(bank_full, 1)
                    yield
            for j in range(2):
                it.open_bank(eng, f"z{j}")
                if first and j == 0:
                    eng.wait_ge(weights_in[4], 16)
                dst = it.bank(f"z{j}")
                for q in range(4):
                    for k in (2 * q, 2 * q + 1):
                        ins = eng.matmul(dst[:, :], hT[:, k, j * P:(j + 1) * P], w_sb[:, k, 3 * DN:4 * DN],
                                         start=(k == 0), stop=(k == KD - 1))
                    if q == 3:
                        ins.then_inc(bank_full, 1)
                    yield

        def glu_eighths(it):
            it.taken(eng, "h3")
            for b in range(CF // P):
                it.open_bank(eng, f"g{b}")
                if b % 2 == 0:
                    eng.wait_ge(env["w_cf_in"][b // 2], 32)
                dst = it.bank(f"g{b}")
                for q in range(8):
                    c = b + (q // 4) * (CF // P)
                    for k in (2 * (q % 4), 2 * (q % 4) + 1):
                        ins = eng.matmul(dst[:, (q // 4) * G_TOK:(q // 4 + 1) * G_TOK], env["w_cf"][:, k, c * P:(c + 1) * P],
                                         hT[:, k, :], start=(k == 0), stop=(k == KD - 1))
                    if q == 7:
                        ins.then_inc(bank_full, 1)
                    yield
                if b == 2:
                    yield

        def y_transpose(it, g, j):
            it.open_bank(eng, f"y{j}")
            y_rows.after(eng, g * 2 + j)
            for h in range(H):
                ins = eng.transpose(it.bank(f"y{j}")[:, h * P:(h + 1) * P], Y[j][:, h, :], ident)
            ins.then_inc(bank_full, 1)

        def tile(it, j, fill):
            g, q = it.g, QKV[it.p]
            T = g * 2 + j
            sl = slice(j * P, (j + 1) * P)
            qT = [q[:, h, sl] for h in range(H)]
            kT = [q[:, H + h, sl] for h in range(H)]
            vT = [q[:, 2 * H + h, sl] for h in range(H)]
            squares.after(eng, T)
            gate_g.after(eng, g)
            r_ln.after(eng, T - 1)
            vec_in.after(eng, T - 1)
            for c in range(8):
                eng.matmul(bS[:, c:c + 1], sq[:, c, :], ones[:, 0:1], start=True, stop=True)
            eng.matmul(bS[:, 8:12], tri, gt[it.p][:, j, :], start=True, stop=True)
            eng.matmul(bS[:, 12:16], ones, gt[it.p][:, j, :], start=True, stop=True).then_inc(scal_full.sem, 1)
            o_sum.after(eng, T - 1)
            for h in range(H):
                ins = eng.matmul(B0[:, h, :], gt[it.p][:, j, h:h + 1].to_broadcast([P, P]), tri, start=True, stop=True)
            ins.then_inc(gcrow_full.sem, 1)
            state.after(eng, T - 1)
            for h in range(H):
                eng.matmul(B1[:, h, :], kT[h], kT[h], start=True, stop=True)
            for h in range(H):
                ins = eng.matmul(B2[:, h, :], kT[h], qT[h], start=True, stop=True)
            ins.then_inc(gram_full.sem, 1)
            for h in range(H):
                ins = eng.transpose(B3[:, h, :], kT[h], ident)
            ins.then_inc(tok_full.sem, 1)
            for h in range(H):
                ins = eng.transpose(B4[:, h, :], vT[h], ident)
            ins.then_inc(tok_full.sem, 1)
            if j == 0:
                transposes(it)
            if j == 0 and it.y_before:
                y_transpose(it, g - 1, 1)
            fill()
            fill()
            a_lvl.after(eng, T, 1)
            difs.after(eng, T, 1)
            for h in range(H):
                ins = eng.matmul(B0[:, h, :], Aoff[0][:, h, :], ident, start=True, stop=True)
            ins.then_inc(a0T_full.sem, 1)
            fill()
            for l in range(1, LEVELS):
                a_lvl.after(eng, T, l + 1)
                inv.after(eng, T, 2 * l)
                if l > 1:
                    x_copied.after(eng, T, l - 1)
                for h in range(H):
                    ins = eng.matmul(packed_head(bX, h), Aoff[l][:, h, :], half_cols(M, h, l, 1), start=True, stop=True)
                ins.then_inc(x_full.sem, 1)
                if l == 1:
                    ktok_in.after(eng, T)
                    vb_in.after(eng, T)
                    for h in range(H):
                        ins = eng.matmul(B3[:, h, :], kT[h], S[:, h, :], start=True, stop=True)
                    ins.then_inc(ks_full.sem, 1)
                    for h in range(H):
                        ins = eng.matmul(B4[:, h, :], qT[h], S[:, h, :], start=True, stop=True)
                    ins.then_inc(ks_full.sem, 1)
                    a_mat.after(eng, T)
                    qk_d.after(eng, T)
                fill()
                if j == 1 and l == 3:
                    y_transpose(it, g, 0)
                x_copied.after(eng, T, l)
                for h in range(H):
                    x_cols = half_cols(X[l], h, l, 1) if l < LEVELS - 1 else packed_head(X_last, h)
                    ins = eng.matmul(packed_head(bM, h), T_[:, h, :], x_cols, start=True, stop=True)
                ins.then_inc(d_full.sem, 1)
                if l < LEVELS - 1:
                    for h in range(H):
                        ins = eng.matmul(packed_head(bT, h), X[l][:, h, :], half_cols(T_, h, l, 0), start=True, stop=True)
                    ins.then_inc(d_full.sem, 1)
                fill()
            inv.after(eng, T)
            rhs.after(eng, T)
            for h in range(H):
                ins = eng.matmul(B3[:, h, :], M[:, h, :], R[:, h, :], start=True, stop=True)
            ins.then_inc(vhat_full.sem, 1)
            fill()
            vh_in.after(eng, T)
            for h in range(H):
                ins = eng.matmul(B0[:, h, :], QKd[:, h, :], vh[:, h, :], start=True, stop=True)
            ins.then_inc(o2_full.sem, 1)
            vd_in.after(eng, T)
            for h in range(H):
                ins = eng.matmul(B1[:, h, :], ktok[:, h, :], vd[:, h, :], start=True, stop=True)
            ins.then_inc(ds_full.sem, 1)
            if j == 0:
                fill()

        def body(it):
            quarter = quarters(it) if it.fill else glu_eighths(it)
            fill = lambda: next(quarter, None)
            if it.chain:
                silu_done.after(eng, it.g)
                tile(it, 0, fill)
                tile(it, 1, fill)
            else:
                transposes(it)
            for _ in quarter:
                pass

        eng.wait_ge(env["consts_in"], 16)
        eng.wait_ge(once, ONCE)
        over_groups(eng, body)
        y_transpose(last, NG - 1, 1)

    def act(eng):
        def norm(group):
            eng.wait_ge(x_in.sem, group * 16 + 16 + 1)
            if not isinstance(group, int) or group > 1:
                z_silu.after(eng, group - 2)
            for j in range(2):
                x_sq.after(eng, group, j)
                eng.activation(junk[:, :], xt[:, j, :], ACT.Square, accum_out=xss[:, j:j + 1]).then_inc(x_sq.sem, 1)
            x_sq.after(eng, group)
            eng.activation(xr[:, :], xss[:, :], ACT.Ln, bias=eps[:, 0:1], scale=1.0 / D).then_inc(x_ln.sem, 1)
            x_ln.after(eng, group)
            eng.activation(xr[:, :], xr[:, :], ACT.Exp, scale=-0.5).then_inc(x_rs.sem, 1)

        def take_h(it):
            for n in range(4):
                j, half = n // 2, n % 2
                it.full(eng, f"h{n}")
                eng.activation(hT[:, 4 * half:4 * half + 4, j * P:(j + 1) * P], v4(it.bank(f"h{n}")),
                               ACT.Copy).then_inc(bank_taken, 1)

        def take(it, name):
            if not it.fill:
                return
            it.full(eng, name)
            src, nxt = it.bank(name), 1 - it.p
            if name == "ba":
                eng.activation(ba[:, :, :], src[:, 0:16].rearrange("p (j c) -> p j c", j=2), ACT.Copy).then_inc(bank_taken, 1)
            elif name[0] == "c":
                b = int(name[1])
                if b == 0:
                    hist.after(eng, it.g)
                eng.activation(U[:, 2 * b:2 * b + 2, SHORT - 1:], src[:, :].rearrange("p (c t) -> p c t", c=2),
                               ACT.Copy).then_inc(bank_taken, 1)
            else:
                j = int(name[1])
                if it.chain and j == 0:
                    y_rows.after(eng, it.g * 2 - 1)
                eng.activation(ZS[nxt][:, j, :], src[:, :], ACT.Copy).then_inc(bank_taken, 1)

        def take_glu(it, b):
            it.full(eng, f"g{b}")
            src = it.bank(f"g{b}")
            eng.activation(glu0[:, b, CONF_TAPS - 1:], src[:, 0:G_TOK], ACT.Copy).then_inc(glu_val, 1)
            eng.activation(glu_exp[:, b, :], src[:, G_TOK:], ACT.Exp, scale=-1.0).then_inc(bank_taken, 1)
            it.taken(eng, f"g{b}")
            eng.activation(glu_exp[:, b, :], glu_exp[:, b, :], ACT.Ln, bias=1.0).then_inc(glu_sig, 1)
            eng.wait_ge(glu_sig, 2 * b + 1)
            eng.activation(glu_exp[:, b, :], glu_exp[:, b, :], ACT.Exp, scale=-1.0).then_inc(glu_sig, 1)

        def take_y(it, j):
            it.full(eng, f"y{j}")
            if j == 0:
                y_out.after(eng, it.g - 1)
            eng.activation(yT[:, :, j * P:(j + 1) * P], v4(it.bank(f"y{j}")), ACT.Identity,
                           scale=onorm[:, 0:1]).then_inc(bank_taken, 1)

        def gate_exps(n):
            gate_a.after(eng, n)
            eng.activation(ge[:, 0], ba[:, :, 0:H], ACT.Exp, scale=-1.0).then_inc(gate_e.sem, 1)
            eng.activation(ge[:, 1], ga[:, 1], ACT.Exp, scale=-1.0).then_inc(gate_e.sem, 1)
            gate_e.after(eng, n, 2)
            eng.activation(ge[:, 2], ge[:, 1], ACT.Ln, bias=1.0).then_inc(gate_e.sem, 1)

        def square_tile(g, p, j):
            T = g * 2 + j
            scal_full.after(eng, T - 1)
            eng.activation(sq[:, :, :], QKV[p][:, 0:8, j * P:(j + 1) * P], ACT.Square).then_inc(squares.sem, 1)

        def tile(it, j):
            T = it.g * 2 + j
            scal_full.after(eng, T)
            facs.after(eng, T - 1)
            eng.activation(rn[:, :], bS[:, 0:8], ACT.Ln, bias=eps[:, 0:1]).then_inc(r_ln.sem, 1)
            r_ln.after(eng, T)
            eng.activation(rn[:, :], rn[:, :], ACT.Exp, scale=-0.5).then_inc(r_exp.sem, 1)
            vec_in.after(eng, T)
            eng.activation(evec[:, :], vec[:, :], ACT.Exp).then_inc(dec_e.sem, 1)
            if j == 0:
                take_h(it)
            difs.after(eng, T)
            eng.activation(Dl[:, :, :], Dl[:, :, :], ACT.Exp, scale=-1.0).then_inc(d_exp.sem, 1)
            eng.activation(Du[:, :, :], Du[:, :, :], ACT.Exp).then_inc(d_exp.sem, 1)
            tok_full.after(eng, T, 1)
            eng.activation(ktok[:, :, :], B3, ACT.Copy).then_inc(ktok_in.sem, 1)
            if j == 0:
                if it.y_before:
                    take_y(it, 1)
                take(it, "ba")
                square_tile(it.g, it.p, 1)
                y_rows.after(eng, T - 1)
                eng.activation(ez[:, :, :], ZS[it.p][:, :, :], ACT.Exp, scale=-1.0).then_inc(z_exp.sem, 1)
            for l in range(1, LEVELS):
                x_full.after(eng, T, l)
                if l < LEVELS - 1:
                    eng.activation(half_all(X[l], l, 1), packed(bX, l), ACT.Copy).then_inc(x_copied.sem, 1)
                else:
                    eng.activation(X_last[:, :], bX[:, 0:H * P // 2], ACT.Copy).then_inc(x_copied.sem, 1)
                for at, name in {0: ((1, "c0"), (3, "c1"), (5, "c2")), 1: ((1, "c4"), (3, "c5"), (5, "z0"))}[j]:
                    if at == l:
                        take(it, name)
                if not it.fill and (j, l) in ((0, 4), (1, 3)):
                    take_glu(it, 0 if j == 0 else 2)
                if j == 1 and l == 3:
                    take_y(it, 0)
                if j == 1 and l == 2 and it.fill:
                    gate_exps(it.g + 1)
                if j == 1 and l == 4:
                    norm(it.g + 2)
            if j == 1 and it.fill:
                silu(it)
            vhat_full.after(eng, T)
            eng.activation(vh[:, :, :], B3, ACT.Copy).then_inc(vh_in.sem, 1)
            if j == 1 and it.fill:
                after_silu(it)
            take(it, "c3" if j == 0 else "z1")
            if not it.fill:
                take_glu(it, 1 if j == 0 else 3)
            o_sum.after(eng, T)
            eng.activation(osq[:, :, :], o[:, :, :], ACT.Square).then_inc(o_sq.sem, 1)
            o_red.after(eng, T)
            eng.activation(ors[:, :], oss[:, :], ACT.Ln, bias=eps[:, 0:1], scale=1.0 / P).then_inc(o_ln.sem, 1)
            o_ln.after(eng, T)
            eng.activation(ors[:, :], ors[:, :], ACT.Exp, scale=-0.5).then_inc(o_rs.sem, 1)

        def silu(it):
            eng.preload_act_table_set(SILU)
            conv.after(eng, it.g + 1)
            p = 1 - it.p
            eng.activation(QKV[p][:, :, :], QKV[p][:, :, :], ACT.Silu).then_inc(silu_done.sem, 1)

        def after_silu(it):
            eng.preload_act_table_set(EXP_LN)
            silu_done.after(eng, it.g + 1)
            square_tile(it.g + 1, 1 - it.p, 0)

        def body(it):
            if it.chain:
                tile(it, 0)
                tile(it, 1)
                return
            take_h(it)
            take(it, "ba")
            take(it, "c0")
            gate_exps(0)
            for b in range(1, 6):
                take(it, f"c{b}")
                if b == 2:
                    norm(1)
            take(it, "z0")
            silu(it)
            after_silu(it)
            take(it, "z1")

        eng.preload_act_table_set(EXP_LN)
        eng.wait_ge(env["eps_in"], 1)
        norm(0)
        eng.wait_ge(params_in, 16 * 7)
        eng.activation(nega[:, :], nega[:, :], ACT.Exp).then_inc(once, 1)
        over_groups(eng, body)
        take_y(last, 1)

    def dve(eng):
        def normed(group, tiles=(0, 1)):
            x_rs.after(eng, group)
            for j in tiles:
                eng.scalar_tensor_tensor(out=xt[:, j, :], in0=xt[:, j, :], scalar=xr[:, j:j + 1], in1=nm_bc[:, :],
                                         op0=ALU.mult, op1=ALU.mult).then_inc(x_nrm.sem, 1)

        def convolve(it, b, half):
            if not it.fill:
                return
            n = it.g + 1
            dst = QKV[1 - it.p]
            if half == 0:
                it.taken(eng, f"c{b}")
                if b == 0 and it.chain:
                    ks_full.after(eng, it.g * 2 - 1)
            for tap in (2 * half, 2 * half + 1):
                for c in (2 * b, 2 * b + 1):
                    src = U[:, c, tap:tap + G_TOK]
                    w = convw[:, tap, c:c + 1]
                    if tap == 0:
                        eng.tensor_scalar(dst[:, c, :], src, w, None, ALU.mult).then_inc(conv.sem, 1)
                    else:
                        conv.after(eng, n, b * 8 + 2 * (tap - 1) + c % 2 + 1)
                        eng.scalar_tensor_tensor(out=dst[:, c, :], in0=src, scalar=w, in1=dst[:, c, :],
                                                 op0=ALU.mult, op1=ALU.add).then_inc(conv.sem, 1)
            if b == 5 and half == 1:
                eng.tensor_copy(U[:, :, 0:SHORT - 1], U[:, :, G_TOK:]).then_inc(hist.sem, 1)

        def gates_in(it):
            n = it.g + 1
            it.taken(eng, "ba")
            eng.tensor_tensor(ga[:, 0], ba[:, :, H:2 * H], mid(dtb[:, :], 2), ALU.add).then_inc(gate_a.sem, 1)
            gate_a.after(eng, n, 1)
            eng.scalar_tensor_tensor(out=ga[:, 1], in0=ga[:, 0], scalar=-1.0, in1=ga[:, 0], op0=ALU.mult, op1=ALU.max).then_inc(gate_a.sem, 1)
            eng.tensor_scalar(ga[:, 2], ga[:, 0], 0.0, None, ALU.max).then_inc(gate_a.sem, 1)

        def gates_out(it):
            n = it.g + 1
            p = 1 - it.p
            gate_e.after(eng, n)
            eng.tensor_scalar(ge[:, 0], ge[:, 0], 1.0, None, ALU.add).then_inc(gate_g.sem, 1)
            eng.tensor_tensor(ga[:, 2], ga[:, 2], ge[:, 2], ALU.add).then_inc(gate_g.sem, 1)
            gate_g.after(eng, n, 2)
            eng.reciprocal(beta[p][:, :, :], ge[:, 0]).then_inc(gate_g.sem, 1)
            eng.tensor_tensor(gt[p][:, :, :], ga[:, 2], mid(nega[:, :], 2), ALU.mult).then_inc(gate_g.sem, 1)

        def tile(it, j):
            T = it.g * 2 + j
            egc, egl, dec = evec[:, 0:4], evec[:, 4:8], evec[:, 8:12]
            rb, f, fe, s = fac[:, 0], fac[:, 1], fac[:, 2], fac[:, 3]
            scal_full.after(eng, T)
            dec_e.after(eng, T - 1)
            r_ln.after(eng, T)
            eng.tensor_copy(vec[:, 0:8], bS[:, 8:16]).then_inc(vec_in.sem, 1)
            vec_in.after(eng, T, 1)
            eng.tensor_tensor(vec[:, 8:12], vec[:, 4:8], vec[:, 0:4], ALU.subtract).then_inc(vec_in.sem, 1)
            gcrow_full.after(eng, T)
            eng.tensor_tensor(Du[:, :, :], B0, bcast(vec[:, 0:4], P), ALU.subtract).then_inc(difs.sem, 1)
            difs.after(eng, T, 1)
            eng.tensor_scalar(Dl[:, :, :], Du[:, :, :], 0.0, None, ALU.max).then_inc(difs.sem, 1)
            eng.tensor_scalar(Du[:, :, :], Du[:, :, :], 0.0, None, ALU.min).then_inc(difs.sem, 1)
            r_exp.after(eng, T)
            eng.tensor_tensor(rb, rn[:, 4:8], beta[it.p][:, j, :], ALU.mult).then_inc(facs.sem, 1)
            facs.after(eng, T, 1)
            eng.tensor_tensor(f, rb, rn[:, 4:8], ALU.mult).then_inc(facs.sem, 1)
            facs.after(eng, T, 2)
            dec_e.after(eng, T)
            eng.tensor_tensor(fe, f, egc, ALU.mult).then_inc(facs.sem, 1)
            eng.tensor_scalar(s, rn[:, 0:4], float(P) ** -0.5, None, ALU.mult).then_inc(facs.sem, 1)
            d_exp.after(eng, T, 1)
            gram_full.after(eng, T)
            eng.tensor_tensor(A[:, :, :], B1, Dl[:, :, :], ALU.mult).then_inc(a_mat.sem, 1)
            a_mat.after(eng, T, 1)
            eng.tensor_tensor(A[:, :, :], A[:, :, :], bcast(f, P), ALU.mult).then_inc(a_mat.sem, 1)
            tok_full.after(eng, T)
            eng.tensor_tensor(vb[:, :, :], B4, bcast(rb, P), ALU.mult).then_inc(vb_in.sem, 1)
            du_mask.after(eng, T)
            eng.tensor_tensor(QKd[:, :, :], B2, Du[:, :, :], ALU.mult).then_inc(qk_d.sem, 1)
            a_lvl.after(eng, T, 1)
            eng.tensor_tensor(T_[:, :, :], mid(ident, H), Aoff[0][:, :, :], ALU.subtract).then_inc(inv.sem, 1)
            a0T_full.after(eng, T)
            eng.tensor_tensor(M[:, :, :], mid(ident, H), B0, ALU.subtract).then_inc(inv.sem, 1)
            if j == 1:
                convolve(it, 3, 0)
            for l in range(1, LEVELS):
                if l == 1:
                    ks_full.after(eng, T, 1)
                    facs.after(eng, T)
                    eng.tensor_tensor(R[:, :, :], B3, bcast(fe, P), ALU.mult).then_inc(rhs.sem, 1)
                    ks_full.after(eng, T)
                    eng.tensor_tensor(o[:, :, :], B4, bcast(egc, P), ALU.mult).then_inc(o_q.sem, 1)
                    rhs.after(eng, T, 1)
                    vb_in.after(eng, T)
                    eng.tensor_tensor(R[:, :, :], vb[:, :, :], R[:, :, :], ALU.subtract).then_inc(rhs.sem, 1)
                if not it.fill:
                    if (j, l) in ((0, 5), (1, 1)):
                        glu_part(it, j)
                    conv_ops({0: (0, 0, 0, 0, 9, 9), 1: (0, 9, 8, 9, 6, 3)}[j][l - 1])
                if j == 1 and l >= 5:
                    normed(it.g + 2, (l - 5,))
                d_full.after(eng, T, 2 * l - 1)
                inv.after(eng, T, 2 * l)
                eng.tensor_tensor(half_all(M, l, 1), half_all(M, l, 1), packed(bM, l), ALU.subtract).then_inc(inv.sem, 1)
                if l < LEVELS - 1:
                    d_full.after(eng, T, 2 * l)
                    eng.tensor_tensor(half_all(T_, l, 0), half_all(T_, l, 0), packed(bT, l), ALU.subtract).then_inc(inv.sem, 1)
                if j == 0 and l >= 2:
                    convolve(it, (l - 2) // 2, l % 2)
                if j == 1 and l == 1:
                    convolve(it, 3, 1)
                    if it.fill:
                        gates_in(it)
                if j == 1 and 2 <= l <= 5:
                    convolve(it, 4 + (l - 2) // 2, l % 2)
                if j == 1 and l == 3 and it.fill:
                    gates_out(it)
                if j == 0 and l <= 3:
                    silu_z(it, l)
                if l == 3:
                    st_dec_op(T, egl)
            vh_in.after(eng, T)
            eng.tensor_tensor(vd[:, :, :], vh[:, :, :], bcast(dec, P), ALU.mult).then_inc(vd_in.sem, 1)
            if j == 0:
                convolve(it, 2, 1)
                if not it.fill:
                    conv_ops(9)
            o2_full.after(eng, T)
            o_q.after(eng, T)
            eng.tensor_tensor(o[:, :, :], o[:, :, :], B0, ALU.add).then_inc(o_sum.sem, 1)
            ds_full.after(eng, T)
            st_dec.after(eng, T)
            eng.tensor_tensor(S[:, :, :], S[:, :, :], B1, ALU.add).then_inc(state.sem, 1)
            o_sum.after(eng, T, 1)
            eng.tensor_tensor(o[:, :, :], o[:, :, :], bcast(s, P), ALU.mult).then_inc(o_sum.sem, 1)
            o_sq.after(eng, T)
            eng.tensor_reduce(oss[:, :], osq[:, :, :], AX.X, ALU.add).then_inc(o_red.sem, 1)
            o_rs.after(eng, T)
            if j == 0:
                eng.wait_ge(bank_full, it.base + 1)
            elif it.y_before:
                it.full(eng, "y1")
            eng.tensor_tensor(Y[j][:, :, :], o[:, :, :], bcast(ors[:, :], P), ALU.mult).then_inc(y_rows.sem, 1)
            y_rows.after(eng, T, 1)
            z_silu.after(eng, it.g)
            eng.tensor_tensor(Y[j][:, :, :], Y[j][:, :, :], ZS[it.p][:, j, :].rearrange("p (h n) -> p h n", h=H),
                              ALU.mult).then_inc(y_rows.sem, 1)

        def silu_z(it, step):
            if step == 1:
                z_exp.after(eng, it.g)
                ins = eng.tensor_scalar(ez[:, :, :], ez[:, :, :], 1.0, None, ALU.add)
            else:
                z_silu.after(eng, it.g, step - 1)
                if step == 2:
                    ins = eng.reciprocal(ez[:, :, :], ez[:, :, :])
                else:
                    ins = eng.tensor_tensor(ZS[it.p][:, :, :], ZS[it.p][:, :, :], ez[:, :, :], ALU.mult)
            ins.then_inc(z_silu.sem, 1)

        def glu_part(it, b):
            eng.wait_ge(glu_val, b + 1)
            eng.wait_ge(glu_sig, 2 * b + 2)
            v = glu0[:, b, CONF_TAPS - 1:]
            eng.tensor_tensor(v, v, glu_exp[:, b, :], ALU.mult).then_inc(glu_made, 1)
            if b == 0:
                eng.memset(glu0[:, :, 0:CONF_TAPS - 1], 0.0).then_inc(glu_made, 1)

        conv_done = [0]

        def conv_ops(count):
            for n in range(conv_done[0], min(conv_done[0] + count, 2 * CONF_TAPS)):
                b, tap = divmod(n, CONF_TAPS)
                src, w = glu0[:, b, tap:tap + G_TOK], dw_taps[:, tap, b:b + 1]
                if tap == 0:
                    eng.wait_ge(glu_made, b + 2)
                    ins = eng.tensor_scalar(conv0[:, b, :], src, w, cf_cols[:, 0, b:b + 1], ALU.mult, ALU.add)
                else:
                    eng.wait_ge(conv_early, n)
                    ins = eng.scalar_tensor_tensor(out=conv0[:, b, :], in0=src, scalar=w, in1=conv0[:, b, :],
                                                   op0=ALU.mult, op1=ALU.add)
                ins.then_inc(conv_early, 1)
                conv_done[0] = n + 1

        def st_dec_op(T, egl):
            ks_full.after(eng, T)
            state.after(eng, T - 1)
            eng.tensor_tensor(S[:, :, :], S[:, :, :], bcast(egl, P), ALU.mult).then_inc(st_dec.sem, 1)

        def body(it):
            if it.chain:
                tile(it, 0)
                tile(it, 1)
                if not it.fill:
                    conv_ops(2 * CONF_TAPS)
                    glu_part(it, 2)
                    glu_part(it, 3)
            else:
                gates_in(it)
                for b in range(6):
                    convolve(it, b, 0)
                    convolve(it, b, 1)
                    if b == 0:
                        gates_out(it)
                normed(1)

        eng.memset(U[:, :, 0:SHORT - 1], 0.0).then_inc(once, 1)
        eng.memset(S[:, :, :], 0.0).then_inc(once, 1)
        for l in range(1, LEVELS - 1):
            eng.memset(X[l][:, :, :], 0.0).then_inc(once, 1)
        eng.wait_ge(params_in, 16 * 7)
        eng.wait_ge(once, ONCE)
        eng.tensor_scalar(nega[:, :], nega[:, :], -1.0, None, ALU.mult).then_inc(once, 1)
        eng.wait_ge(once, ONCE + 1)
        normed(0)
        over_groups(eng, body)

    def pool(eng):
        def tile(it, j):
            T = it.g * 2 + j
            d_exp.after(eng, T)
            eng.tensor_tensor(Du[:, :, :], Du[:, :, :], mid(tri, H), ALU.mult).then_inc(du_mask.sem, 1)
            a_mat.after(eng, T)
            vhat_full.after(eng, T - 1)
            for l in range(LEVELS):
                eng.tensor_tensor(Aoff[l][:, :, :], A[:, :, :], mid(const(C_LVL + l), H), ALU.mult).then_inc(a_lvl.sem, 1)

        def body(it):
            if it.chain:
                tile(it, 0)
                tile(it, 1)

        over_groups(eng, body)

    def started(name, program):
        def run(eng):
            for s in ahead[name]:
                eng.sem_inc(s.sem if isinstance(s, Signal) else s, 1)
            program(eng)
        return run

    programs = dict(sync=sp, tensor=pe, scalar=act, vector=dve, gpsimd=pool)
    return own, {name: started(name, program) for name, program in programs.items()}


def conformer_pass(nc, ctx, env):
    x, w_in, w_out = env["x"], env["w_in"], env["w_out"]
    consts, banks, eps = env["consts"], env["banks"], env["eps"]
    own = ctx.enter_context(ExitStack())

    def sb(name, shape, dt=F32):
        return own.enter_context(nc.sbuf_tensor(name, shape, dt))

    ident = consts[:, C_ID * P:(C_ID + 1) * P]
    ones = consts[:, C_ONES * P:(C_ONES + 1) * P]
    N_PARAMS = 3
    HIST = CONF_TAPS - 1
    CB = CF // P
    HALF = D // 2

    w_cf, w_o = env["w_cf"], env["w_o"]
    nm_bc, xt = env["norm_mix_rows"], env["x_group"]
    w_r = sb("w_router", [P, KD, N_LOGIT])
    b_r = sb("b_router_rows", [P, N_LOGIT])
    nf_bc = sb("norm_ffn_rows", [P, D])
    taps, cols = env["dw_taps"], env["cf_columns"]
    mean_w = sb("mean_weights", [P, P])
    junk = sb("square_junk2", [P, D])
    xss = sb("x2_sumsq", [P, 2])
    xr = sb("x2_rstd", [P, 2])
    hT = env["hT"]
    sg = sb("glu_sigmoid", [P, CB, G_TOK])
    G = [env["glu0"], sb("glu1", [P, CB, HIST + G_TOK])]
    C = [env["conv0"], sb("conv_out1", [P, CB, G_TOK])]
    csq = sb("conv_squares", [P, CB, G_TOK])
    vrs = sb("ln_rstd", [P, G_TOK])
    ycf = sb("y_cf_columns", [P, CB, G_TOK])
    ydn = sb("y_dn_columns", [P, CB, G_TOK])
    res = sb("residual", [P, 2, D])
    x2 = [sb(f"x_mixed{i}", [P, 2, D]) for i in range(2)]
    x2ss = sb("x_mixed_sumsq", [P, 2])
    x2rs = sb("x_mixed_rstd", [P, 2])
    h2 = sb("h_ffn", [P, 2, D])
    h2T = sb("h_ffnT", [P, KD, G_TOK])
    logits = env["logits"]

    v4 = lambda b: b[:, :].rearrange("p (h n) -> p h n", h=4)
    ring, outb, bStat, bLog = banks[0:4], banks[4:6], banks[6], banks[7]
    mean_v, var_v = bStat[:, 0:G_TOK], bStat[:, G_TOK:2 * G_TOK]

    sem = env["sem"]
    params_in, w_o_in = sem("p2_params_in"), env["w_o_in"]
    mean_w_in = sem("p2_mean_weights")
    x_in, ydn_in, res_in = Signal(sem("p2_x_in"), 16, 1 - 32), Signal(sem("p2_ydn_in"), 16), Signal(sem("p2_res_in"), 16)
    x2_out, h2_out = Signal(sem("p2_x2_out"), 16), Signal(sem("p2_h2_out"), 16)
    h_full, glu_full = Signal(sem("p2_h_full"), 4, 1 - 4), Signal(sem("p2_glu_full"), 4, 1 - 4)
    mean_full, var_full = Signal(sem("p2_mean_full")), Signal(sem("p2_var_full"))
    out_full = Signal(sem("p2_out_full"), 4)
    h2_full, log_full = Signal(sem("p2_h2_full"), 4), Signal(sem("p2_logits_full"))
    x_sq, x_ln, x_rs = Signal(sem("p2_x_sq"), 2, 1 - 4), Signal(sem("p2_x_ln"), 1, 1 - 2), Signal(sem("p2_x_rstd"), 1, 1 - 2)
    h_taken, h2_taken = Signal(sem("p2_h_taken"), 4, 1 - 4), Signal(sem("p2_h2_taken"), 4)
    c_sq, v_ln, v_rs = Signal(sem("p2_c_sq")), Signal(sem("p2_v_ln")), Signal(sem("p2_v_rstd"))
    silu_c, sigm = Signal(sem("p2_silu"), 4), Signal(sem("p2_sigmoid"), 4, 1 - 4)
    x2_sq, x2_ln, x2_rs = Signal(sem("p2_x2_sq"), 2), Signal(sem("p2_x2_ln")), Signal(sem("p2_x2_rstd"))
    x_nrm, h2_nrm = Signal(sem("p2_x_normed"), 2, 1 - 4), Signal(sem("p2_h2_normed"), 2)
    centred, c_nrm = Signal(sem("p2_centred")), Signal(sem("p2_c_normed"))
    glu, conv = Signal(sem("p2_glu"), 4, 1 - 4), Signal(sem("p2_conv"), CONF_TAPS * 4, 1 - CONF_TAPS * 2)
    x2_sum, logit = Signal(sem("p2_x2_sum"), 4), Signal(sem("p2_logit"))
    hist = Signal(sem("p2_history"))
    ahead = dict(
        sync=[x_in, ydn_in, res_in, x2_out, h2_out],
        tensor=[h_full, glu_full, mean_full, var_full, out_full, h2_full, log_full],
        scalar=[x_sq, x_ln, x_rs, h_taken, h2_taken, c_sq, v_ln, v_rs, silu_c, sigm, x2_sq, x2_ln, x2_rs],
        vector=[x_nrm, h2_nrm, centred, c_nrm, glu, conv, x2_sum, logit, hist],
        gpsimd=[])
    env["x2_out"], env["h2_out"], env["logit"] = x2_out, h2_out, logit

    class Step:

        def __init__(self, s, parity, steady=False):
            self.s, self.p = s, parity
            def has(n):
                return steady or 0 <= s + n < NG
            self.norm, self.proj, self.conv, self.out, self.logits = has(2), has(1), has(0), has(-1), has(-2)
            self.steady = steady

    def over_steps(eng, body):
        for s in (0, 1):
            body(Step(s, s % 2))
        with eng.Fori(0, (NG - 4) // 2) as i:
            body(Step(i * 2 + 2, 0, True))
            body(Step(i * 2 + 3, 1, True))
        for s in range(NG - 2, NG + 2):
            body(Step(s, s % 2))

    def tok(g, j=0, n=G_TOK):
        return bass.ds(g * G_TOK + j * P, n)

    def by_tile(dram, g):
        return dram[tok(g), :].rearrange("(j p) d -> p j d", p=P)

    def sp(eng):
        def load_x(g):
            eng.dma_start(xt[:, :, :], by_tile(x, g)).then_inc(x_in.sem, 16)

        for dst, src in ((nf_bc, env["norm_ffn"].partition_broadcast(P)), (b_r, env["b_router"].partition_broadcast(P))):
            eng.dma_start(dst[:, :], src).then_inc(params_in, 16)
        eng.dma_start(w_r[:, :, :], env["w_router"].rearrange("(k p) n -> p k n", p=P)).then_inc(params_in, 16)
        def body(it):
            s = it.s
            if it.norm:
                h_full.after(eng, s + 1)
                load_x(s + 2)
            if it.out:
                if it.steady or s >= 2:
                    x2_sum.after(eng, s - 2)
                eng.dma_start(ydn[:, :, :], env["y_dnT"][:, tok(s - 1)].rearrange("(h p) t -> p h t", p=P)).then_inc(ydn_in.sem, 16)
                eng.dma_start(res[:, :, :], by_tile(x, s - 1)).then_inc(res_in.sem, 16)
            if it.logits:
                h2_nrm.after(eng, s - 2)
                eng.dma_start(by_tile(env["h_rows"], s - 2), h2[:, :, :]).then_inc(h2_out.sem, 16)
            if it.out:
                x2_sum.after(eng, s - 1)
                eng.dma_start(by_tile(env["x_rows"], s - 1), x2[1 - it.p][:, :, :]).then_inc(x2_out.sem, 16)

        over_steps(eng, body)

    def pe(eng):
        def transposes(g, src, full, waits, ready):
            for n in range(4):
                j, half = n // 2, n % 2
                for w in waits:
                    w(n)
                if half == 0 and ready:
                    ready.after(eng, g, j + 1)
                for q in range(4):
                    k = half * 4 + q
                    ins = eng.transpose(ring[n][:, q * P:(q + 1) * P], src[:, j, k * P:(k + 1) * P], ident)
                ins.then_inc(full.sem, 1)

        def glu_unit(it, b):
            for part in range(2):
                c = b + part * CB
                for k in range(KD):
                    ins = eng.matmul(ring[b][:, part * G_TOK:(part + 1) * G_TOK], w_cf[:, k, c * P:(c + 1) * P],
                                     hT[:, k, :], start=(k == 0), stop=(k == KD - 1))
            ins.then_inc(glu_full.sem, 1)

        def body(it):
            s = it.s
            if it.out:
                conv.after(eng, s - 1)
                if it.steady or s >= 2:
                    centred.after(eng, s - 2)
                for b in range(CB):
                    ins = eng.matmul(mean_v, mean_w[:, :], C[1 - it.p][:, b, :], start=(b == 0), stop=(b == CB - 1))
                ins.then_inc(mean_full.sem, 1)
            if it.proj:
                h_taken.after(eng, s + 1)
                glu_unit(it, 0)
            if it.out:
                c_sq.after(eng, s - 1)
                if it.steady or s >= 2:
                    v_ln.after(eng, s - 2)
                for b in range(CB):
                    ins = eng.matmul(var_v, mean_w[:, :], csq[:, b, :], start=(b == 0), stop=(b == CB - 1))
                ins.then_inc(var_full.sem, 1)
            if it.proj:
                for b in range(1, 4):
                    glu_unit(it, b)

            def out_tile(j):
                for half in range(2):
                    if j == 1:
                        x2_sum.after(eng, s - 1, half + 1)
                    elif it.steady or s >= 2:
                        x2_sum.after(eng, s - 2, 3 + half)
                    for k in range(KD):
                        y = ydn if k < CB else ycf
                        ins = eng.matmul(outb[half][:, :], y[:, k % CB, j * P:(j + 1) * P],
                                         w_o[:, k, half * HALF:(half + 1) * HALF], start=(k == 0), stop=(k == KD - 1))
                    ins.then_inc(out_full.sem, 1)

            if it.out:
                if not it.steady and s == 1:
                    eng.wait_ge(w_o_in, 16 * KD)
                    eng.wait_ge(params_in, 16 * N_PARAMS)
                ydn_in.after(eng, s - 1)
                silu_c.after(eng, s - 1)
                out_tile(0)
            if it.logits:
                free = (lambda n: glu.after(eng, s + 1, n + 1)) if it.proj else (lambda n: h2_taken.after(eng, s - 3, n + 1))
                transposes(s - 2, h2, h2_full, [free], h2_nrm)
            if it.out:
                out_tile(1)
            if it.norm:
                if it.logits:
                    free = lambda n: h2_taken.after(eng, s - 2, n + 1)
                else:
                    free = lambda n: glu.after(eng, s + 1, n + 1)
                transposes(s + 2, xt, h_full, [free], x_nrm)
            if it.logits:
                h2_taken.after(eng, s - 2)
                if it.steady or s >= 3:
                    logit.after(eng, s - 3)
                for j in range(2):
                    for k in range(KD):
                        ins = eng.matmul(bLog[:, j * N_LOGIT:(j + 1) * N_LOGIT], h2T[:, k, j * P:(j + 1) * P],
                                         w_r[:, k, :], start=(k == 0), stop=(k == KD - 1))
                ins.then_inc(log_full.sem, 1)

        eng.wait_ge(mean_w_in, 1)
        transposes(1, xt, h_full, [], None)
        over_steps(eng, body)

    def act(eng):
        def x_norm(g):
            x_in.after(eng, g)
            for j in range(2):
                x_sq.after(eng, g, j)
                eng.activation(junk[:, :], xt[:, j, :], ACT.Square, accum_out=xss[:, j:j + 1]).then_inc(x_sq.sem, 1)
            x_sq.after(eng, g)
            eng.activation(xr[:, :], xss[:, :], ACT.Ln, bias=eps[:, 0:1], scale=1.0 / D).then_inc(x_ln.sem, 1)
            x_ln.after(eng, g)
            eng.activation(xr[:, :], xr[:, :], ACT.Exp, scale=-0.5).then_inc(x_rs.sem, 1)

        def take(g, full, dst, sig):
            for n in range(4):
                j, half = n // 2, n % 2
                full.after(eng, g, n + 1)
                eng.activation(dst[:, 4 * half:4 * half + 4, j * P:(j + 1) * P], v4(ring[n]), ACT.Copy).then_inc(sig.sem, 1)

        def square_x2(it, j):
            g = it.s - 1
            x2_sum.after(eng, g, 2 * j + 2)
            x2_sq.after(eng, g, j)
            if it.logits and j == 0:
                x2_rs.after(eng, g - 1)
            eng.activation(junk[:, :], x2[1 - it.p][:, j, :], ACT.Square, accum_out=x2ss[:, j:j + 1]).then_inc(x2_sq.sem, 1)

        def body(it):
            s = it.s
            if it.logits:
                x2_sq.after(eng, s - 2)
                eng.activation(x2rs[:, :], x2ss[:, :], ACT.Ln, bias=eps[:, 0:1], scale=1.0 / D).then_inc(x2_ln.sem, 1)
                x2_ln.after(eng, s - 2)
                eng.activation(x2rs[:, :], x2rs[:, :], ACT.Exp, scale=-0.5).then_inc(x2_rs.sem, 1)
            if it.out:
                centred.after(eng, s - 1)
                eng.activation(csq[:, :, :], C[1 - it.p][:, :, :], ACT.Square).then_inc(c_sq.sem, 1)
            if it.norm:
                x_norm(s + 2)
            if it.out:
                var_full.after(eng, s - 1)
                if it.steady or s >= 2:
                    c_nrm.after(eng, s - 2)
                eng.activation(vrs[:, :], var_v, ACT.Ln, bias=eps[:, 0:1]).then_inc(v_ln.sem, 1)
                v_ln.after(eng, s - 1)
                eng.activation(vrs[:, :], vrs[:, :], ACT.Exp, scale=-0.5).then_inc(v_rs.sem, 1)
                eng.preload_act_table_set(SILU)
                c_nrm.after(eng, s - 1)
                if it.steady or s >= 2:
                    out_full.after(eng, s - 2)
                for b in range(CB):
                    eng.activation(ycf[:, b, :], C[1 - it.p][:, b, :], ACT.Silu, scale=cols[:, 1, b:b + 1],
                                   bias=cols[:, 2, b:b + 1]).then_inc(silu_c.sem, 1)
            if it.proj:
                eng.preload_act_table_set(SIGMOID)
                for b in range(CB):
                    glu_full.after(eng, s + 1, b + 1)
                    if it.steady or s >= 1:
                        glu.after(eng, s, b + 1)
                    eng.activation(sg[:, b, :], ring[b][:, G_TOK:], ACT.Sigmoid).then_inc(sigm.sem, 1)
            eng.preload_act_table_set(EXP_LN)
            if it.logits:
                if it.steady or s >= 3:
                    log_full.after(eng, s - 3)
                take(s - 2, h2_full, h2T, h2_taken)
            if it.out:
                square_x2(it, 0)
            if it.norm:
                take(s + 2, h_full, hT, h_taken)
            if it.out:
                square_x2(it, 1)

        take(1, h_full, hT, h_taken)
        eng.preload_act_table_set(EXP_LN)
        over_steps(eng, body)

    def dve(eng):
        def normed(g):
            x_rs.after(eng, g)
            for j in range(2):
                eng.scalar_tensor_tensor(out=xt[:, j, :], in0=xt[:, j, :], scalar=xr[:, j:j + 1], in1=nm_bc[:, :],
                                         op0=ALU.mult, op1=ALU.mult).then_inc(x_nrm.sem, 1)

        def glu_unit(it, b):
            if not it.proj:
                return
            g = it.s + 1
            sigm.after(eng, g, b + 1)
            if b == 0:
                if it.steady or it.s >= 1:
                    conv.after(eng, it.s - 1)
                hist.after(eng, it.s)
            eng.tensor_tensor(G[1 - it.p][:, b, HIST:], ring[b][:, 0:G_TOK], sg[:, b, :], ALU.mult).then_inc(glu.sem, 1)

        def convolve(it, t0, n):
            if not it.conv:
                return
            src, dst = G[it.p], C[it.p]
            if t0 == 0:
                glu.after(eng, it.s)
                if it.steady or it.s >= 1:
                    hist.after(eng, it.s - 1)
                if it.steady or it.s >= 2:
                    silu_c.after(eng, it.s - 2)
            first = not it.steady and it.s == 0
            blocks = range(CB // 2, CB) if first else range(CB)
            for tap in range(t0, t0 + n):
                for b in blocks:
                    w = taps[:, tap, b:b + 1]
                    if tap == 0:
                        ins = eng.tensor_scalar(dst[:, b, :], src[:, b, tap:tap + G_TOK], w, cols[:, 0, b:b + 1],
                                                ALU.mult, ALU.add)
                    else:
                        if first:
                            eng.wait_ge(conv.sem, 2 * (tap - 1) + b - CB // 2 + 1 + 1)
                        else:
                            conv.after(eng, it.s, CB * (tap - 1) + b + 1)
                        ins = eng.scalar_tensor_tensor(out=dst[:, b, :], in0=src[:, b, tap:tap + G_TOK], scalar=w,
                                                       in1=dst[:, b, :], op0=ALU.mult, op1=ALU.add)
                    ins.then_inc(conv.sem, 1)

        def add_residual(it, j, half):
            if not it.out:
                return
            g = it.s - 1
            if j == 0 and half == 0:
                res_in.after(eng, g)
                if it.steady or it.s >= 3:
                    x2_out.after(eng, g - 2)
            out_full.after(eng, g, 2 * j + half + 1)
            cs = slice(half * HALF, (half + 1) * HALF)
            eng.tensor_tensor(x2[1 - it.p][:, j, cs], outb[half][:, :], res[:, j, cs], ALU.add).then_inc(x2_sum.sem, 1)

        def body(it):
            s = it.s
            if it.logits:
                x2_rs.after(eng, s - 2)
                if it.steady or s >= 3:
                    h2_out.after(eng, s - 3)
                    h2_full.after(eng, s - 3)
                for j in range(2):
                    eng.scalar_tensor_tensor(out=h2[:, j, :], in0=x2[it.p][:, j, :], scalar=x2rs[:, j:j + 1],
                                             in1=nf_bc[:, :], op0=ALU.mult, op1=ALU.mult).then_inc(h2_nrm.sem, 1)
            if it.out:
                mean_full.after(eng, s - 1)
                c = C[1 - it.p]
                eng.tensor_tensor(c[:, :, :], c[:, :, :], mid(mean_v, CB), ALU.subtract).then_inc(centred.sem, 1)
            if it.conv and it.proj:
                glu.after(eng, s)
                if it.steady or s >= 1:
                    conv.after(eng, s - 1)
                eng.tensor_copy(G[1 - it.p][:, :, 0:HIST], G[it.p][:, :, G_TOK:]).then_inc(hist.sem, 1)
            ends = (4, 9, 17, 25, 30, 31) if not it.steady and s == 0 else (4, 8, 11, 13, 15, 19, 23, 28, 31)

            def part(n):
                if n < len(ends):
                    t0 = ends[n - 1] if n else 0
                    convolve(it, t0, ends[n] - t0)

            part(0)
            if it.out:
                v_rs.after(eng, s - 1)
                c = C[1 - it.p]
                centred.after(eng, s - 1)
                eng.tensor_tensor(c[:, :, :], c[:, :, :], mid(vrs[:, :], CB), ALU.mult).then_inc(c_nrm.sem, 1)
            part(1)
            glu_unit(it, 0)
            part(2)
            glu_unit(it, 1)
            part(3)
            glu_unit(it, 2)
            if it.norm:
                normed(s + 2)
            part(4)
            glu_unit(it, 3)
            part(5)
            add_residual(it, 0, 0)
            part(6)
            add_residual(it, 0, 1)
            part(7)
            add_residual(it, 1, 0)
            part(8)
            add_residual(it, 1, 1)
            if it.logits:
                log_full.after(eng, s - 2)
                eng.tensor_tensor(logits[:, bass.ds((s - 2) * 2, 2), :],
                                  bLog[:, 0:2 * N_LOGIT].rearrange("p (j n) -> p j n", j=2), mid(b_r[:, :], 2),
                                  ALU.add).then_inc(logit.sem, 1)

        eng.tensor_scalar(mean_w[:, :], ones, 1.0 / CF, None, ALU.mult).then_inc(mean_w_in, 1)
        eng.wait_ge(params_in, 16 * N_PARAMS)
        over_steps(eng, body)

    def started(name, program):
        def run(eng):
            for s in ahead[name]:
                eng.sem_inc(s.sem, 1)
            program(eng)
        return run

    programs = dict(sync=sp, tensor=pe, scalar=act, vector=dve)
    return own, {name: started(name, program) for name, program in programs.items()}


N_BLOCK = SEQ * 2 // P + N_EXP
SLOTS = N_EXP * SEQ
AHEAD = 3
FAR = -1e30
ENTRY = 2


def router_pass(nc, ctx, env):
    consts, banks, logits = env["consts"], env["banks"], env["logits"]
    own = ctx.enter_context(ExitStack())
    NGr, NE = N_GROUPS, EXP_PER_GROUP

    def sb(name, shape, dt=F32):
        return own.enter_context(nc.sbuf_tensor(name, shape, dt))

    strict = consts[:, C_STRICT * P:(C_STRICT + 1) * P]
    ones = consts[:, C_ONES * P:(C_ONES + 1) * P]
    gl = logits[:, :, 0:NGr]
    el = logits[:, :, NGr:].rearrange("p t (g e) -> p t g e", g=NGr)
    down = sb("count_down", [P, NE])
    gmax, gsum, pg = sb("r_gmax", [P, NT]), sb("r_gsum", [P, NT]), sb("r_pg", [P, NT])
    gd, gval, gsel = sb("r_gd", [P, NT, NGr]), sb("r_gval", [P, NT, NGr]), sb("r_gsel", [P, NT, NGr])
    esel4, e8 = sb("r_esel4", [P, NT, NGr, NE]), sb("r_e8", [P, NT, NE])
    m = [sb(f"r_max{k}", [P, NT]) for k in range(2)]
    val, vmax = sb("r_val", [P, NT, NE]), sb("r_vmax", [P, NT])
    one = [sb(f"r_onehot{k}", [P, NT, NE]) for k in range(2)]
    e8b = sb("r_e8b", [P, NT, NE])
    ed, wden = sb("r_exp_diff", [P, NT]), sb("r_wden", [P, NT])
    wt = [sb(f"r_weight{k}", [P, NT]) for k in range(2)]
    OH = [sb(f"r_choice{k}", [P, NT, NGr, NE]) for k in range(2)]
    M = sb("r_chosen", [P, NT, N_EXP])
    cum = sb("r_before", [P, NT + 1, N_EXP])
    region = sb("r_region", [P, N_EXP])
    R = sb("r_rank", [P, NT, N_EXP])
    prod = sb("r_prod", [P, NT, N_EXP])
    slotf = sb("r_slotf", [P, 2, NT])
    slot = sb("r_slot", [P, NT, 2], U32)
    entry = sb("r_entry", [P, NT, 2, ENTRY], I32)
    fill = sb("r_fill", [P, SLOTS // P + AHEAD, ENTRY], I32)
    zero_rows = sb("r_zero_rows", [P, D])
    cnt = sb("r_count", [P, N_EXP])
    cnt_i = sb("r_count_i", [P, N_EXP], I32)
    nbf = sb("r_blocks_f", [P, N_EXP])
    bs = [sb(f"r_base{k}", [P, N_EXP]) for k in range(2)]
    base = sb("r_base", [P, N_EXP])
    step = sb("r_step", [P, N_EXP])
    blk = sb("r_block_no", [P, N_BLOCK + AHEAD])
    reach = sb("r_reach", [P, N_BLOCK + AHEAD, N_EXP])
    first = sb("r_first_slot", [P, N_BLOCK + AHEAD])
    meta = env["meta"]

    sem = env["sem"]
    fill_made, fill_in = sem("r_fill_made"), sem("r_fill_in")
    entries_in = sem("r_entries_in")
    steps = sem("r_steps")
    exps = sem("r_exps")
    ranks = sem("r_ranks")
    iotas = sem("r_iotas")
    entry_ready = sem("r_entry_ready")
    env["meta_in"] = sem("r_meta_in")
    at = {}

    def dve(eng):
        n = [0]

        def op(name, ins):
            ins.then_inc(steps, 1)
            n[0] += 1
            at[name] = n[0]

        def need(*names):
            eng.wait_ge(steps, max(at[x] for x in names))

        eng.wait_ge(iotas, 4)
        env["logit"].after(eng, NG - 1)
        op("gmax", eng.tensor_reduce(gmax[:, :], gl, AX.X, ALU.max))
        need("gmax")
        op("gd", eng.tensor_tensor(gd[:, :, :], gl, bcast(gmax[:, :], NGr), ALU.subtract))
        op("geq", eng.tensor_tensor(gval[:, :, :], gl, bcast(gmax[:, :], NGr), ALU.is_equal))
        need("geq")
        op("gval", eng.tensor_tensor(gval[:, :, :], gval[:, :, :], mid(down[:, NE - NGr:], NT), ALU.mult))
        need("gval")
        op("gtop", eng.tensor_reduce(vmax[:, :], gval[:, :, :], AX.X, ALU.max))
        need("gtop")
        op("gsel", eng.tensor_tensor(gsel[:, :, :], gval[:, :, :], bcast(vmax[:, :], NGr), ALU.is_equal))
        eng.wait_ge(exps, 1)
        op("gsum", eng.tensor_reduce(gsum[:, :], gd[:, :, :], AX.X, ALU.add))
        need("gsum")
        op("pg", eng.reciprocal(pg[:, :], gsum[:, :]))
        op("esel4", eng.tensor_tensor(esel4[:, :, :, :], el, bcast(gsel[:, :, :], NE), ALU.mult))
        need("esel4")
        op("e8", eng.tensor_reduce(e8[:, :, :], esel4[:, :, :, :].rearrange("p t g e -> p t e g"), AX.X, ALU.add))
        for k in range(2):
            src = e8 if k == 0 else e8b
            need("e8" if k == 0 else "e8b")
            op(f"m{k}", eng.tensor_reduce(m[k][:, :], src[:, :, :], AX.X, ALU.max))
            need(f"m{k}")
            op("val", eng.tensor_tensor(val[:, :, :], src[:, :, :], bcast(m[k][:, :], NE), ALU.is_equal))
            need("val")
            op("val", eng.tensor_tensor(val[:, :, :], val[:, :, :], mid(down[:, :], NT), ALU.mult))
            need("val")
            op("vmax", eng.tensor_reduce(vmax[:, :], val[:, :, :], AX.X, ALU.max))
            need("vmax")
            op(f"one{k}", eng.tensor_tensor(one[k][:, :, :], val[:, :, :], bcast(vmax[:, :], NE), ALU.is_equal))
            need(f"one{k}")
            if k == 0:
                op("e8b", eng.scalar_tensor_tensor(out=e8b[:, :, :], in0=one[0][:, :, :], scalar=FAR, in1=e8[:, :, :],
                                                   op0=ALU.mult, op1=ALU.add))
            for g in range(NGr):
                op(f"OH{k}", eng.tensor_tensor(OH[k][:, :, g, :], one[k][:, :, :],
                                               gsel[:, :, g:g + 1].to_broadcast([P, NT, NE]), ALU.mult))
        op("ed", eng.tensor_tensor(ed[:, :], m[1][:, :], m[0][:, :], ALU.subtract))
        need("OH1")
        ch = [OH[k][:, :, :, :].rearrange("p t g e -> p t (g e)") for k in range(2)]
        op("M", eng.tensor_tensor(M[:, :, :], ch[0], ch[1], ALU.add))
        op("cum0", eng.memset(cum[:, 0, :], 0.0))
        need("cum0")
        for t in range(NT):
            op(f"cum{t + 1}", eng.tensor_tensor(cum[:, t + 1, :], cum[:, t, :], M[:, t, :], ALU.add))
            need(f"cum{t + 1}")
        eng.wait_ge(exps, 2)
        op("wden", eng.tensor_scalar(wden[:, :], ed[:, :], 1.0, None, ALU.add))
        need("wden")
        op("wden", eng.reciprocal(wden[:, :], wden[:, :]))
        need("wden")
        op("wt0", eng.tensor_tensor(wt[0][:, :], pg[:, :], wden[:, :], ALU.mult))
        need("wt0")
        op("wt1", eng.tensor_tensor(wt[1][:, :], wt[0][:, :], ed[:, :], ALU.mult))
        eng.wait_ge(ranks, 1)
        op("R", eng.tensor_tensor(R[:, :, :], banks[0][:, :].rearrange("p (t e) -> p t e", t=NT),
                                  mid(region[:, :], NT), ALU.add))
        for k in range(2):
            need("R")
            op("prod", eng.tensor_tensor(prod[:, :, :], ch[k], R[:, :, :], ALU.mult))
            need("prod")
            op("slotf", eng.tensor_reduce(slotf[:, k, :], prod[:, :, :], AX.X, ALU.add))
            need("slotf")
            op("slot", eng.tensor_copy(slot[:, :, k], slotf[:, k, :]))
            need("slot", "wt1")
            op("entry", eng.tensor_copy(entry[:, :, k, 1].bitcast(F32), wt[k][:, :]))
            need("entry")
            eng.sem_inc(entry_ready, 1)
        eng.wait_ge(ranks, 2)
        op("cnt", eng.tensor_scalar(cnt[:, :], banks[1][:, 0:N_EXP], 1.0, float(P - 1), ALU.max, ALU.add))
        need("cnt")
        op("cnt_i", eng.tensor_copy(cnt_i[:, :], cnt[:, :]))
        need("cnt_i")
        op("nblk", eng.tensor_scalar(cnt_i[:, :], cnt_i[:, :], 7, None, ALU.arith_shift_right))
        need("nblk")
        op("nbf", eng.tensor_copy(nbf[:, :], cnt_i[:, :]))
        src, name = nbf, "nbf"
        for i in range(5):
            s, dst = 1 << i, bs[i % 2]
            need(name)
            op("a", eng.tensor_copy(dst[:, 0:s], src[:, 0:s]))
            op(f"bs{i}", eng.tensor_tensor(dst[:, s:], src[:, s:], src[:, 0:N_EXP - s], ALU.add))
            src, name = dst, f"bs{i}"
        need(name)
        op("base", eng.tensor_tensor(base[:, :], src[:, :], nbf[:, :], ALU.subtract))
        op("meta", eng.tensor_copy(meta[:, N_EXP:2 * N_EXP], src[:, :]))
        need("base")
        op("meta", eng.tensor_copy(meta[:, 0:N_EXP], base[:, :]))
        need("base")
        op("step0", eng.memset(step[:, 0:1], 0.0))
        op("step", eng.tensor_scalar(step[:, 1:], nbf[:, 0:N_EXP - 1], -float(P), float(SEQ), ALU.mult, ALU.add))
        op("reach", eng.tensor_tensor(reach[:, :, :], bcast(blk[:, :], N_EXP), mid(base[:, :], N_BLOCK + AHEAD), ALU.is_ge))
        need("reach")
        op("reach", eng.tensor_tensor(reach[:, :, :], reach[:, :, :], mid(step[:, :], N_BLOCK + AHEAD), ALU.mult))
        need("reach")
        op("first", eng.tensor_reduce(first[:, :], reach[:, :, :], AX.X, ALU.add))
        need("first")
        op("first", eng.scalar_tensor_tensor(out=first[:, :], in0=blk[:, :], scalar=float(P), in1=first[:, :],
                                             op0=ALU.mult, op1=ALU.add))
        need("first")
        eng.tensor_copy(meta[:, 2 * N_EXP:2 * N_EXP + N_BLOCK + AHEAD], first[:, :]).then_inc(env["meta_in"], 1)

    def act(eng):
        eng.preload_act_table_set(EXP_LN)
        eng.wait_ge(steps, at["gd"])
        eng.activation(gd[:, :, :], gd[:, :, :], ACT.Exp).then_inc(exps, 1)
        eng.wait_ge(steps, at["ed"])
        eng.activation(ed[:, :], ed[:, :], ACT.Exp).then_inc(exps, 1)

    def pe(eng):
        flat = lambda a: a.rearrange("p t e -> p (t e)")
        eng.wait_ge(steps, at[f"cum{NT}"])
        eng.matmul(banks[0][:, :], strict, flat(M[:, :, :]), start=True, stop=False)
        eng.matmul(banks[0][:, :], ones, flat(cum[:, 0:NT, :]), start=False, stop=True).then_inc(ranks, 1)
        eng.matmul(banks[1][:, 0:N_EXP], ones, cum[:, NT, :], start=True, stop=True).then_inc(ranks, 1)

    def pool(eng):
        eng.iota(down[:, :], [[-1, NE]], base=NE, channel_multiplier=0, allow_small_or_imprecise_dtypes=True).then_inc(iotas, 1)
        eng.iota(region[:, :], [[SEQ, N_EXP]], base=0, channel_multiplier=0, allow_small_or_imprecise_dtypes=True).then_inc(iotas, 1)
        eng.iota(blk[:, :], [[1, N_BLOCK + AHEAD]], base=0, channel_multiplier=0, allow_small_or_imprecise_dtypes=True).then_inc(iotas, 1)
        eng.iota(entry[:, :, :, 0], [[P, NT], [0, 2]], base=0, channel_multiplier=1).then_inc(iotas, 1)
        eng.iota(fill[:, :, 1], [[0, SLOTS // P + AHEAD]], base=0, channel_multiplier=0).then_inc(fill_made, 1)
        eng.memset(zero_rows[:, :], 0.0).then_inc(fill_made, 1)
        eng.iota(fill[:, :, 0], [[1, SLOTS // P + AHEAD]], base=0, channel_multiplier=SLOTS // P + AHEAD).then_inc(fill_made, 1)
        eng.wait_ge(fill_in, 16 * 4)
        for k in range(2):
            eng.wait_ge(entry_ready, k + 1)
            for t in range(NT):
                eng.indirect_dma_start(out=env["table"][:, :], out_offset=bass.IndirectOffsetOnAxis(ap=slot[:, t, k:k + 1], axis=0),
                                       in_=entry[:, t, k, :], in_offset=None).then_inc(entries_in, 16)
        eng.wait_ge(entries_in, 16 * 2 * NT)

    def sp(eng):
        eng.wait_ge(env["fill_masked"], 1)
        eng.dma_start(env["table"].rearrange("(p j) c -> p j c", p=P), fill[:, :, :]).then_inc(fill_in, 16)
        for rows in ("h_rows", "x_rows", "out"):
            eng.dma_start(env[rows][SEQ:, :], zero_rows[:, :]).then_inc(fill_in, 16)

    def mask_fill(eng):
        eng.wait_ge(fill_made, 3)
        eng.tensor_scalar(fill[:, :, 0], fill[:, :, 0], P - 1, SEQ, ALU.bitwise_and, ALU.bitwise_or).then_inc(env["fill_masked"], 1)

    env["fill_masked"] = sem("r_fill_masked")

    def dve_all(eng):
        mask_fill(eng)
        dve(eng)

    return own, dict(sync=sp, tensor=pe, scalar=act, vector=dve_all, gpsimd=pool)


def expert_pass(nc, ctx, env):
    consts, banks, meta = env["consts"], env["banks"], env["meta"]
    own = ctx.enter_context(ExitStack())
    ident = consts[:, C_ID * P:(C_ID + 1) * P]
    DE = 512
    KE = DE // P
    HALF = D // 2

    def sb(name, shape, dt=F32):
        return own.enter_context(nc.sbuf_tensor(name, shape, dt))

    W = env["expert_w"]
    wg = [w[:, 0, :].rearrange("p (k n) -> p k n", k=KD) for w in W]
    wu = [w[:, 1, :].rearrange("p (k n) -> p k n", k=KD) for w in W]
    wd = [w[:, 2, :].rearrange("p (k n) -> p k n", k=KE) for w in W]
    e_far = sb("entries_far", [P, ENTRY], I32)
    e_next = sb("entries_next", [P, ENTRY], I32)
    e_mid = sb("entries_mid", [P, ENTRY], I32)
    e_cur = sb("entries_now", [P, ENTRY], I32)
    xg = sb("gathered_rows", [P, D])
    xT = sb("gathered_T", [P, KD, P])
    hg = sb("silu_gate", [P, DE])
    ha = sb("hidden", [P, DE])
    haT = sb("hidden_T", [P, KE, P])
    acc = sb("residual_rows", [P, D])
    y = sb("sum_rows", [P, D])
    out_rows = sb("normed_sums", [P, D])
    nfin = sb("norm_final_rows", [P, D])
    junk = sb("square_junk3", [P, D])
    y_ss = sb("sum_sumsq", [P, 1])

    bG, bU, bX, bA, bY = banks[0], banks[1], banks[2:4], [banks[4], banks[7]], banks[5:7]
    v4 = lambda b: b[:, :].rearrange("p (h n) -> p h n", h=4)
    sem = env["sem"]
    w_in = [sem(f"m_weight_halves{k}_in") for k in range(2)]
    ent_in, rows_in = Signal(sem("m_entries_in"), 16, 0), Signal(sem("m_rows_in"), 16, 0)
    acc_in, stored = Signal(sem("m_residual_in"), 16, 0), Signal(sem("m_stored"), 32, 16)
    nfin_in = sem("m_norm_final_in")
    y_sq, y_ln, y_rs = Signal(sem("m_y_squared")), Signal(sem("m_y_ln")), Signal(sem("m_y_rstd"))
    y_nrm = Signal(sem("m_y_normed"))
    xT_full, gu_full = Signal(sem("m_xT_full"), 2), Signal(sem("m_gate_up_full"), 2)
    hT_full, y_full = Signal(sem("m_hidden_T_full"), 2), Signal(sem("m_y_full"), 2)
    xT_a, xT_v = Signal(sem("m_xT_by_act")), Signal(sem("m_xT_by_dve"))
    silu, hid = Signal(sem("m_silu")), Signal(sem("m_hidden"))
    hT_a, hT_v = Signal(sem("m_hidden_T_by_act")), Signal(sem("m_hidden_T_by_dve"))
    y_lo, y_hi = Signal(sem("m_y_first_half")), Signal(sem("m_y_second_half"))
    steps_begun = sem("m_pool_steps_begun")
    e_kept, e_moved, e_set = Signal(sem("m_entries_kept")), Signal(sem("m_entries_moved")), Signal(sem("m_entries_set"))
    ahead = dict(sync=[], tensor=[xT_full, gu_full, hT_full, y_full], scalar=[xT_a, silu, hT_a, y_sq, y_ln, y_rs],
                 vector=[xT_v, hid, hT_v, y_lo, y_hi, y_nrm, e_kept, e_moved, e_set], gpsimd=[])
    HI = N_BLOCK

    def n_blocks(eng):
        return eng.value_load(meta[0:1, 2 * N_EXP - 1:2 * N_EXP], min_val=N_EXP, max_val=HI)

    def load_expert(eng, e, half):
        run = KD * DE // 2
        for i, src in enumerate((env["w_gate"], env["w_up"], env["w_down"])):
            part = src[bass.ds(e, 1)].rearrange("a (p k) n -> p (a k n)", p=P)
            for c in range(2):
                if not isinstance(e, int) or e > 0 or i > 0:
                    eng.wait_ge(w_in[c], e * 48 + i * 16)
                eng.dma_start(W[half][:, i, c * run:(c + 1) * run], part[:, c * run:(c + 1) * run]).then_inc(w_in[c], 16)

    def sp(eng):
        eng.dma_start(nfin[:, :], env["norm_final"].partition_broadcast(P)).then_inc(nfin_in, 16)
        with eng.Fori(0, N_EXP // 2 - 1) as pair:
            for half in range(2):
                done = eng.value_load(meta[0:1, bass.ds(pair * 2 + (N_EXP + half), 1)], min_val=1, max_val=HI)
                y_full.after(eng, done, 0)
                load_expert(eng, pair * 2 + 2 + half, half)

    def pe(eng):
        def x_transposes(i):
            rows_in.after(eng, i)
            for half in range(2):
                (xT_a if half == 0 else xT_v).after(eng, i - 1)
                for q in range(4):
                    k = 4 * half + q
                    ins = eng.transpose(bX[half][:, q * P:(q + 1) * P], xg[:, k::KD], ident)
                ins.then_inc(xT_full.sem, 1)

        def block(i, pair, half):
            for c in range(2):
                eng.wait_ge(w_in[c], pair * 96 + half * 48 + 48)
            xT_a.after(eng, i)
            xT_v.after(eng, i)
            silu.after(eng, i - 1)
            for k in range(KD):
                ins = eng.matmul(bG[:, :], xT[:, k, :], wg[half][:, k, :], start=(k == 0), stop=(k == KD - 1))
            ins.then_inc(gu_full.sem, 1)
            hid.after(eng, i - 1)
            for k in range(KD):
                ins = eng.matmul(bU[:, :], xT[:, k, :], wu[half][:, k, :], start=(k == 0), stop=(k == KD - 1))
            ins.then_inc(gu_full.sem, 1)
            x_transposes(i + 1)
            hid.after(eng, i)
            for part, taken in enumerate((hT_v, hT_a)):
                taken.after(eng, i - 1)
                for q in range(KE // 2):
                    ins = eng.transpose(bA[part][:, q * P:(q + 1) * P], ha[:, part * (KE // 2) + q::KE], ident)
                ins.then_inc(hT_full.sem, 1)
            hT_v.after(eng, i)
            for n in range(2):
                (y_lo if n == 0 else y_hi).after(eng, i - 1)
                for q in range(KE):
                    if n == 0 and q == KE // 2:
                        hT_a.after(eng, i)
                    ins = eng.matmul(bY[n][:, :], haT[:, q, :], wd[half][:, q, n * HALF:(n + 1) * HALF],
                                     start=(q == 0), stop=(q == KE - 1))
                ins.then_inc(y_full.sem, 1)

        x_transposes(0)
        with eng.Fori(0, N_EXP // 2) as pair:
            for half in range(2):
                e = pair * 2 + half
                start = eng.value_load(meta[0:1, bass.ds(e, 1)], min_val=0, max_val=HI)
                end = eng.value_load(meta[0:1, bass.ds(e + N_EXP, 1)], min_val=1, max_val=HI)
                with eng.Fori(start, end) as i:
                    block(i, pair, half)

    def act(eng):
        def take_x(i):
            xT_full.after(eng, i, 1)
            gu_full.after(eng, i - 1)
            eng.activation(xT[:, 0:4, :], v4(bX[0]), ACT.Copy).then_inc(xT_a.sem, 1)

        eng.preload_act_table_set(SILU)
        take_x(0)
        with eng.Fori(0, n_blocks(eng)) as i:
            gu_full.after(eng, i, 1)
            hid.after(eng, i - 1)
            eng.activation(hg[:, :], bG[:, :], ACT.Silu).then_inc(silu.sem, 1)
            take_x(i + 1)
            hT_full.after(eng, i)
            y_full.after(eng, i - 1)
            eng.activation(haT[:, 2:4, :], bA[1][:, 0:2 * P].rearrange("p (h n) -> p h n", h=2), ACT.Copy).then_inc(hT_a.sem, 1)
            eng.preload_act_table_set(EXP_LN)
            y_lo.after(eng, i)
            y_hi.after(eng, i)
            y_sq.after(eng, i - 1)
            y_nrm.after(eng, i - 1)
            eng.activation(junk[:, :], y[:, :], ACT.Square, accum_out=y_ss[:, :]).then_inc(y_sq.sem, 1)
            y_sq.after(eng, i)
            eng.activation(y_ss[:, :], y_ss[:, :], ACT.Ln, bias=env["eps"][:, 0:1], scale=1.0 / D).then_inc(y_ln.sem, 1)
            y_ln.after(eng, i)
            eng.activation(y_ss[:, :], y_ss[:, :], ACT.Exp, scale=-0.5).then_inc(y_rs.sem, 1)
            eng.preload_act_table_set(SILU)

    def dve(eng):
        def take_x(i):
            xT_full.after(eng, i)
            gu_full.after(eng, i - 1)
            eng.tensor_copy(xT[:, 4:8, :], v4(bX[1])).then_inc(xT_v.sem, 1)

        def move(i):
            ent_in.after(eng, i)
            eng.tensor_copy(e_next[:, :], e_far[:, :]).then_inc(e_moved.sem, 1)

        eng.wait_ge(nfin_in, 16)
        def keep(i):
            e_set.after(eng, i - 1)
            e_moved.after(eng, i)
            eng.tensor_copy(e_mid[:, :], e_next[:, :]).then_inc(e_kept.sem, 1)
            e_kept.after(eng, i)
            move(i + 1)

        move(0)
        take_x(0)
        keep(0)
        with eng.Fori(0, n_blocks(eng)) as i:
            stored.after(eng, i - 1)
            e_kept.after(eng, i)
            eng.tensor_copy(e_cur[:, :], e_mid[:, :]).then_inc(e_set.sem, 1)
            silu.after(eng, i)
            hT_full.after(eng, i - 1)
            gu_full.after(eng, i)
            eng.tensor_tensor(ha[:, :], hg[:, :], bU[:, :], ALU.mult).then_inc(hid.sem, 1)
            hT_full.after(eng, i, 1)
            y_full.after(eng, i - 1)
            eng.tensor_copy(haT[:, 0:2, :], bA[0][:, 0:2 * P].rearrange("p (h n) -> p h n", h=2)).then_inc(hT_v.sem, 1)
            take_x(i + 1)
            keep(i + 1)
            acc_in.after(eng, i)
            e_set.after(eng, i)
            for n, done in enumerate((y_lo, y_hi)):
                y_full.after(eng, i, n + 1)
                cs = slice(n * HALF, (n + 1) * HALF)
                eng.scalar_tensor_tensor(out=y[:, cs], in0=bY[n][:, :], scalar=e_cur[:, 1:2].bitcast(F32), in1=acc[:, cs],
                                         op0=ALU.mult, op1=ALU.add).then_inc(done.sem, 1)
            y_rs.after(eng, i)
            eng.scalar_tensor_tensor(out=out_rows[:, :], in0=y[:, :], scalar=y_ss[:, 0:1], in1=nfin[:, :],
                                     op0=ALU.mult, op1=ALU.mult).then_inc(y_nrm.sem, 1)

    def pool(eng):
        def settle():
            eng.sem_inc(steps_begun, 1)

        def rows_of(e):
            return bass.IndirectOffsetOnAxis(ap=e[:, 0:1].bitcast(U32), axis=0)

        def entries(slot):
            eng.dma_start(e_far[:, :], env["table"][bass.ds(slot, P), :]).then_inc(ent_in.sem, 16)

        def gather(i):
            e_moved.after(eng, i)
            settle()
            eng.indirect_dma_start(out=xg[:, :], out_offset=None, in_=env["h_rows"][:, :],
                                   in_offset=rows_of(e_next)).then_inc(rows_in.sem, 16)

        def slot_of(i):
            return eng.value_load(meta[0:1, bass.ds(i + 2 * N_EXP, 1)], min_val=0, max_val=SLOTS + (AHEAD - 1) * P)

        entries(0)
        eng.dma_start(e_cur[:, :], env["table"][SLOTS:SLOTS + P, :]).then_inc(stored.sem, 16)
        gather(0)
        entries(slot_of(1))
        xT_full.after(eng, 0)
        gather(1)
        entries(slot_of(2))
        with eng.Fori(0, n_blocks(eng)) as i:
            e_set.after(eng, i)
            settle()
            eng.indirect_dma_start(out=acc[:, :], out_offset=None, in_=env["x_rows"][:, :],
                                   in_offset=rows_of(e_cur)).then_inc(acc_in.sem, 16)
            xT_full.after(eng, i + 1)
            gather(i + 2)
            entries(slot_of(i + 3))
            y_lo.after(eng, i)
            y_hi.after(eng, i)
            settle()
            eng.indirect_dma_start(out=env["x_rows"][:, :], out_offset=rows_of(e_cur), in_=y[:, :], in_offset=None).then_inc(stored.sem, 16)
            y_nrm.after(eng, i)
            settle()
            eng.indirect_dma_start(out=env["out"][:, :], out_offset=rows_of(e_cur), in_=out_rows[:, :], in_offset=None).then_inc(stored.sem, 16)
        stored.after(eng, n_blocks(eng) - 1)
        settle()

    def started(name, program):
        def run(eng):
            for s in ahead[name]:
                eng.sem_inc(s.sem, 1)
            program(eng)
        return run

    def first_experts(eng):
        load_expert(eng, 0, 0)
        load_expert(eng, 1, 1)

    env["first_experts"] = first_experts
    programs = dict(sync=sp, tensor=pe, scalar=act, vector=dve, gpsimd=pool)
    return own, {name: started(name, program) for name, program in programs.items()}


def build(nc, t):
    with ExitStack() as ctx:
        count = [0]

        def sem(name):
            count[0] += 1
            return ctx.enter_context(nc.semaphore(name))

        env = dict(t)
        env["sem"] = sem
        env["consts"] = ctx.enter_context(nc.sbuf_tensor("consts", [P, N_CONST * P], F32))
        env["eps"] = ctx.enter_context(nc.sbuf_tensor("eps", [P, 1], F32))
        env["banks"] = [ctx.enter_context(nc.psum_tensor(f"bank{i}", [P, 512], F32)) for i in range(8)]
        env["consts_in"] = sem("consts_in")
        env["eps_in"] = sem("eps_in")
        env["logits"] = ctx.enter_context(nc.sbuf_tensor("logits", [P, NT, N_LOGIT], F32))
        env["meta"] = ctx.enter_context(nc.sbuf_tensor("block_table", [P, 2 * N_EXP + N_BLOCK + AHEAD], I32))
        over = [sem(f"pass{n}_over") for n in range(1, 4)]
        block = ctx.enter_context(nc.Block())
        passes = []
        shared = ctx.enter_context(ExitStack())
        env["weights"] = shared.enter_context(nc.sbuf_tensor("mixer_weights", [P, KD * DN_COLS], F32))
        half = KD * 2 * CF
        env["w_cf"] = env["weights"][:, 0:half].rearrange("p (k c) -> p k c", k=KD)
        env["w_o"] = env["weights"][:, half:half + KD * D].rearrange("p (k c) -> p k c", k=KD)
        env["norm_mix_rows"] = shared.enter_context(nc.sbuf_tensor("norm_mix_rows", [P, D], F32))
        env["x_group"] = shared.enter_context(nc.sbuf_tensor("x_group", [P, 2, D], F32))
        env["hT"] = shared.enter_context(nc.sbuf_tensor("hT", [P, KD, G_TOK], F32))
        env["conv0"] = shared.enter_context(nc.sbuf_tensor("conv_out0", [P, CF // P, G_TOK], F32))
        env["dw_taps"] = shared.enter_context(nc.sbuf_tensor("dw_taps", [P, CONF_TAPS, CF // P], F32))
        env["cf_columns"] = shared.enter_context(nc.sbuf_tensor("cf_columns", [P, 3, CF // P], F32))
        env["qkv0"] = shared.enter_context(nc.sbuf_tensor("qkv0", [P, 12, G_TOK], F32))
        flat = env["qkv0"][:, :, :].rearrange("p c t -> p (c t)")
        width = CF // P * (CONF_TAPS - 1 + G_TOK)
        env["glu0"] = flat[:, 0:width].rearrange("p (b t) -> p b t", b=CF // P)
        env["glu_exp"] = flat[:, width:width + CF // P * G_TOK].rearrange("p (b t) -> p b t", b=CF // P)
        env["w_cf_in"], env["w_o_in"] = [sem(f"p2_wcf_in{n}") for n in range(2)], sem("p2_wout_in")
        own, programs = deltanet_pass(nc, ctx, env)
        passes.append(programs)
        own.close()
        own, programs = conformer_pass(nc, ctx, env)
        passes.append(programs)
        own.close()
        shared.close()
        weights = ctx.enter_context(ExitStack())
        env["expert_w"] = [weights.enter_context(nc.sbuf_tensor(f"expert_w{k}", [P, 3, KD * 512], F32)) for k in range(2)]
        own, programs = router_pass(nc, ctx, env)
        passes.append(programs)
        own.close()
        own, programs = expert_pass(nc, ctx, env)
        passes.append(programs)
        own.close()

        def meet(eng, n):
            eng.drain()
            eng.sem_inc(over[n - 1], 1)
            eng.wait_ge(over[n - 1], 5)

        @block.vector
        def _(eng):
            eng.wait_ge(env["consts_in"], 16)
            passes[0]["vector"](eng)
            meet(eng, 1)
            passes[1]["vector"](eng)
            meet(eng, 2)
            passes[2]["vector"](eng)
            meet(eng, 3)
            eng.wait_ge(env["meta_in"], 1)
            passes[3]["vector"](eng)

        @block.sync
        def _(eng):
            eng.dma_start(env["consts"][:, :], t["shape_consts"]).then_inc(env["consts_in"], 16)
            passes[0]["sync"](eng)
            env["p1_done"].after(eng, NG - 1)
            meet(eng, 1)
            passes[1]["sync"](eng)
            env["x2_out"].after(eng, NG - 1)
            env["h2_out"].after(eng, NG - 1)
            meet(eng, 2)
            passes[2]["sync"](eng)
            env["first_experts"](eng)
            meet(eng, 3)
            eng.wait_ge(env["meta_in"], 1)
            passes[3]["sync"](eng)

        @block.gpsimd
        def _(eng):
            eng.memset(env["eps"][:, :], EPS).then_inc(env["eps_in"], 1)
            eng.wait_ge(env["consts_in"], 16)
            passes[0]["gpsimd"](eng)
            meet(eng, 1)
            meet(eng, 2)
            passes[2]["gpsimd"](eng)
            meet(eng, 3)
            eng.wait_ge(env["meta_in"], 1)
            passes[3]["gpsimd"](eng)

        @block.scalar
        def _(eng):
            passes[0]["scalar"](eng)
            meet(eng, 1)
            passes[1]["scalar"](eng)
            meet(eng, 2)
            passes[2]["scalar"](eng)
            meet(eng, 3)
            eng.wait_ge(env["meta_in"], 1)
            passes[3]["scalar"](eng)

        @block.tensor
        def _(eng):
            passes[0]["tensor"](eng)
            meet(eng, 1)
            passes[1]["tensor"](eng)
            meet(eng, 2)
            passes[2]["tensor"](eng)
            meet(eng, 3)
            eng.wait_ge(env["meta_in"], 1)
            passes[3]["tensor"](eng)


def kernel(**inputs):
    import numpy as _np
    import concourse.bacc as _bacc
    from concourse import mybir as _mybir
    from concourse.bass_utils import run_bass_kernel_spmd as _run

    nc = _bacc.Bacc("TRN2", target_bir_lowering=False, num_devices=1)
    n = _np.arange(P)
    row, col = n[:, None], n[None, :]
    parts = [row == col, row <= col, row < col, row >= 0 * col]
    for l in range(LEVELS):
        parts.append((row > col) & ((row ^ col) >> l == 1))
    shape_consts = _np.concatenate([m.astype(_np.float32) for m in parts], axis=1)
    arrays = {"shape_consts": shape_consts}
    for name, a in inputs.items():
        a = _np.asarray(a)
        arrays[name] = _np.ascontiguousarray(a.reshape(a.shape[1:]) if a.ndim > 1 and a.shape[0] == 1 else a)
    arrays["conv_qkv"] = _np.ascontiguousarray(arrays["conv_qkv"].reshape(4, 12, 128).transpose(2, 0, 1))
    arrays["w_dw"] = _np.ascontiguousarray(arrays["w_dw"].reshape(CONF_TAPS, 4, 128).transpose(2, 0, 1))
    arrays["cf_cols"] = _np.ascontiguousarray(
        _np.stack([arrays.pop(n).reshape(4, 128) for n in ("b_dw", "ln_g", "ln_b")]).transpose(2, 0, 1))
    arrays["w_router"] = _np.concatenate([arrays.pop("w_rg"), arrays.pop("w_re")], axis=1)
    arrays["b_router"] = _np.concatenate([arrays.pop("b_rg"), arrays.pop("b_re")])
    t = {}
    for name, a in arrays.items():
        t[name] = nc.dram_tensor(f"in_{name}", a.shape, _mybir.dt.from_np(a.dtype), kind="ExternalInput").ap()
    t["conv_qkvT"] = t["conv_qkv"]
    t["y_dnT"] = nc.dram_tensor("y_dnT", (DN, SEQ), F32).ap()
    out = nc.dram_tensor("out", (SEQ + P, D), F32, kind="ExternalOutput").ap()
    t["h_rows"] = nc.dram_tensor("h_rows", (SEQ + P, D), F32).ap()
    t["x_rows"] = nc.dram_tensor("x_rows", (SEQ + P, D), F32).ap()
    t["table"] = nc.dram_tensor("slot_table", (SLOTS + AHEAD * P, ENTRY), I32).ap()
    t["out"] = out
    build(nc, t)
    r = _run(nc, [{f"in_{k}": v for k, v in arrays.items()}], core_ids=[0])
    return r.results[0]["out"][:SEQ].reshape(1, SEQ, D)
```
